# Optimizing a Trainium2 kernel written in Bass

```python
import math
import jax
import jax.numpy as jnp
from jax import lax
import numpy as np

D_MODEL = 1024
BATCH = 1
SEQ = 256
DEPTH = 2

HEAD_DIM = 64
D_FF = 2816
NORM_EPS = 1e-6
NUM_BUCKETS = 32
MAX_DISTANCE = 1024
BAND_BLOCK = 128
NSA_HEADS = 8
NSA_KV = 2
NSA_GROUP = NSA_HEADS // NSA_KV
CMP_LEN = 32
CMP_STRIDE = 16
CMP_HIDDEN = 128
SEL_LEN = 64
SEL_TOPK = 16
SEL_QCHUNK = 64
NSA_WINDOW = 512
SWA_HEADS = 8
SWA_KV = 2
SWA_GROUP = SWA_HEADS // SWA_KV
SWA_WINDOW = 128
MLA_HEADS = 8
MLA_Q_RANK = 384
MLA_KV_RANK = 256
MLA_NOPE = 64
MLA_ROPE = 32
MLA_V = 64
MLA_QBLOCK = 128
ROPE_BASE = 10000.0
N_BRANCH = 3
BRANCH_WIDTH = NSA_HEADS * HEAD_DIM
N_BIAS_HEADS = NSA_HEADS + SWA_HEADS
NEG_INF = -1e30
SEL_FORCE = 1e9
IN_SIZES = (
    NSA_HEADS * HEAD_DIM,
    NSA_KV * HEAD_DIM, NSA_KV * HEAD_DIM,
    NSA_KV * HEAD_DIM, NSA_KV * HEAD_DIM,
    NSA_KV * HEAD_DIM, NSA_KV * HEAD_DIM,
    3 * NSA_HEADS,
    SWA_HEADS * HEAD_DIM,
    SWA_KV * HEAD_DIM, SWA_KV * HEAD_DIM,
    MLA_Q_RANK,
    MLA_KV_RANK,
    MLA_ROPE,
    N_BRANCH * D_MODEL,
)
IN_WIDTH = sum(IN_SIZES)

kernel_name = "hybrid_gated_nsa_swa_mla_macaron"

def rmsnorm(x, g):
    xf = x.astype(jnp.float32)
    inv = lax.rsqrt(jnp.mean(xf * xf, axis=-1, keepdims=True) + NORM_EPS)
    return (xf * inv).astype(x.dtype) * g

def split_cols(z):
    outs = []
    off = 0
    for n in IN_SIZES:
        outs.append(z[..., off:off + n])
        off += n
    return outs

def t5_bucket(dist):
    max_exact = NUM_BUCKETS // 2
    d = jnp.maximum(dist, 0)
    df = jnp.maximum(d, 1).astype(jnp.float32)
    large = max_exact + (jnp.log(df / max_exact) / math.log(MAX_DISTANCE / max_exact)
                         * (NUM_BUCKETS - max_exact)).astype(jnp.int32)
    large = jnp.minimum(large, NUM_BUCKETS - 1)
    return jnp.where(d < max_exact, d, large)

def rel_bias(dist, table):
    return table[t5_bucket(dist)].astype(jnp.float32)

def rope(x, pos):
    half = x.shape[-1] // 2
    inv_freq = ROPE_BASE ** (-jnp.arange(half, dtype=jnp.float32) / half)
    ang = pos.astype(jnp.float32)[:, None] * inv_freq[None, :]
    cos = jnp.cos(ang)[None, :, None, :].astype(x.dtype)
    sin = jnp.sin(ang)[None, :, None, :].astype(x.dtype)
    x1, x2 = x[..., :half], x[..., half:]
    return jnp.concatenate([x1 * cos - x2 * sin, x1 * sin + x2 * cos], axis=-1)

def macaron_ffn(x, g_pre, w_gu, w_down, g_post):
    h = rmsnorm(x, g_pre)
    gu = h @ w_gu
    y = (jax.nn.silu(gu[..., :D_FF]) * gu[..., D_FF:]) @ w_down
    return x + 0.5 * rmsnorm(y, g_post)

def banded_attention(q, k, v, window, table, sinks=None):
    B, S, Hkv, G, d = q.shape
    blk = BAND_BLOCK
    nb = S // blk
    n_prev = window // blk
    span = (n_prev + 1) * blk
    pad = ((0, 0), (n_prev * blk, 0), (0, 0), (0, 0))
    kp = jnp.pad(k, pad)
    vp = jnp.pad(v, pad)
    qi = jnp.arange(blk)[:, None]
    kj = jnp.arange(span)[None, :]
    dist = qi + n_prev * blk - kj
    bias = rel_bias(dist, table).transpose(2, 0, 1).reshape(Hkv, G, blk, span)
    in_band = (dist >= 0) & (dist < window)
    scale = d ** -0.5

    def one_block(n):
        qb = lax.dynamic_slice_in_dim(q, n * blk, blk, axis=1)
        kb = lax.dynamic_slice_in_dim(kp, n * blk, span, axis=1)
        vb = lax.dynamic_slice_in_dim(vp, n * blk, span, axis=1)
        s = jnp.einsum('bqhgd,bkhd->bhgqk', qb, kb).astype(jnp.float32) * scale + bias
        valid = in_band & ((n - n_prev) * blk + kj >= 0)
        s = jnp.where(valid, s, NEG_INF)
        if sinks is None:
            p = jax.nn.softmax(s, axis=-1)
        else:
            sk = sinks.astype(jnp.float32).reshape(Hkv, G, 1, 1)
            m = jnp.maximum(jnp.max(s, axis=-1, keepdims=True), sk)
            e = jnp.exp(s - m)
            p = e / (jnp.sum(e, axis=-1, keepdims=True) + jnp.exp(sk - m))
        return jnp.einsum('bhgqk,bkhd->bqhgd', p.astype(v.dtype), vb)

    o = lax.map(one_block, jnp.arange(nb))
    return o.transpose(1, 0, 2, 3, 4, 5).reshape(B, S, Hkv, G, d)

def nsa_compress(kv, pe, w1, w2):
    B, S, Hkv, d = kv.shape
    nc = (S - CMP_LEN) // CMP_STRIDE + 1
    idx = jnp.arange(nc)[:, None] * CMP_STRIDE + jnp.arange(CMP_LEN)[None, :]
    blocks = kv[:, idx] + pe[:, None, :]
    flat = blocks.transpose(0, 1, 3, 2, 4).reshape(B, nc, Hkv, CMP_LEN * d)
    return jax.nn.gelu(flat @ w1) @ w2

def nsa_attention(q, k_c, v_c, k_s, v_s, k_w, v_w, gate, pos, table,
                  pe_k, w1_k, w2_k, pe_v, w1_v, w2_v):
    B, S, Hkv, G, d = q.shape
    scale = d ** -0.5
    kc = nsa_compress(k_c, pe_k, w1_k, w2_k)
    vc = nsa_compress(v_c, pe_v, w1_v, w2_v)
    nc = kc.shape[1]
    cmp_end = jnp.arange(nc) * CMP_STRIDE + CMP_LEN - 1
    dist_c = pos[:, None] - cmp_end[None, :]
    valid_c = dist_c >= 0
    bias_c = rel_bias(dist_c, table).transpose(2, 0, 1).reshape(Hkv, G, S, nc)
    s = jnp.einsum('bthgd,bchd->bhgtc', q, kc).astype(jnp.float32) * scale + bias_c
    s = jnp.where(valid_c, s, NEG_INF)
    e = jnp.where(valid_c, jnp.exp(s - jnp.max(s, axis=-1, keepdims=True)), 0.0)
    den = jnp.sum(e, axis=-1, keepdims=True)
    p_c = e / jnp.where(den > 0, den, 1.0)
    o_cmp = jnp.einsum('bhgtc,bchd->bthgd', p_c.astype(vc.dtype), vc)

    n_sel = S // SEL_LEN
    top_k = min(SEL_TOPK, n_sel)
    ci = jnp.arange(nc)[:, None] * CMP_STRIDE
    sj = jnp.arange(n_sel)[None, :] * SEL_LEN
    overlap = jnp.maximum(jnp.minimum(ci + CMP_LEN, sj + SEL_LEN) - jnp.maximum(ci, sj), 0)
    overlap = overlap.astype(jnp.float32) / CMP_LEN
    imp = jnp.einsum('bhgtc,cj->bhtj', p_c, overlap)
    cur = pos // SEL_LEN
    jj = jnp.arange(n_sel)[None, :]
    forced = (jj == 0) | (jj == cur[:, None]) | (jj == cur[:, None] - 1)
    causal_blk = jj <= cur[:, None]
    score = jnp.where(forced, SEL_FORCE, jnp.where(causal_blk, imp, -SEL_FORCE))
    _, sel_idx = lax.top_k(score, top_k)

    ks_blk = k_s.reshape(B, n_sel, SEL_LEN, Hkv, d).transpose(0, 3, 1, 2, 4)
    vs_blk = v_s.reshape(B, n_sel, SEL_LEN, Hkv, d).transpose(0, 3, 1, 2, 4)
    tb_h = table.reshape(NUM_BUCKETS, Hkv, G).transpose(1, 0, 2)
    bi = jnp.arange(B)[:, None, None, None]
    hi = jnp.arange(Hkv)[None, :, None, None]
    C = SEL_QCHUNK

    def one_chunk(c):
        qc = lax.dynamic_slice_in_dim(q, c * C, C, axis=1)
        ic = lax.dynamic_slice_in_dim(sel_idx, c * C, C, axis=2)
        pc = lax.dynamic_slice_in_dim(pos, c * C, C, axis=0)
        kg = ks_blk[bi, hi, ic]
        vg = vs_blk[bi, hi, ic]
        s = jnp.einsum('bchgd,bhcnpd->bhgcnp', qc, kg).astype(jnp.float32) * scale
        dist = pc[:, None, None] - (ic[..., None] * SEL_LEN + jnp.arange(SEL_LEN))
        bias = tb_h[hi[..., None], t5_bucket(dist)].astype(jnp.float32)
        s = s + jnp.moveaxis(bias, -1, 2)
        s = jnp.where((dist >= 0)[:, :, None], s, NEG_INF)
        p = jax.nn.softmax(s.reshape(B, Hkv, G, C, -1), axis=-1).reshape(s.shape)
        return jnp.einsum('bhgcnp,bhcnpd->bchgd', p.astype(vg.dtype), vg)

    o_sel = lax.map(one_chunk, jnp.arange(S // C))
    o_sel = o_sel.transpose(1, 0, 2, 3, 4, 5).reshape(B, S, Hkv, G, d)

    o_win = banded_attention(q, k_w, v_w, NSA_WINDOW, table)

    g = jax.nn.sigmoid(gate.astype(jnp.float32)).reshape(B, S, Hkv, G, 3).astype(q.dtype)
    o = g[..., 0:1] * o_cmp + g[..., 1:2] * o_sel + g[..., 2:3] * o_win
    return o.reshape(B, S, Hkv * G * d)

def mla_attention(q_c, kv_c, k_r, pos, q_norm, w_qb, kv_norm, w_kvb):
    B, S, _ = q_c.shape
    H = MLA_HEADS
    q = (rmsnorm(q_c, q_norm) @ w_qb).reshape(B, S, H, MLA_NOPE + MLA_ROPE)
    q_nope = q[..., :MLA_NOPE]
    q_rope = rope(q[..., MLA_NOPE:], pos)
    kv = (rmsnorm(kv_c, kv_norm) @ w_kvb).reshape(B, S, H, MLA_NOPE + MLA_V)
    k_nope, v = kv[..., :MLA_NOPE], kv[..., MLA_NOPE:]
    k_rope = rope(k_r[:, :, None, :], pos)[:, :, 0]
    scale = (MLA_NOPE + MLA_ROPE) ** -0.5
    QB = MLA_QBLOCK

    def one_block(n):
        qn = lax.dynamic_slice_in_dim(q_nope, n * QB, QB, axis=1)
        qr = lax.dynamic_slice_in_dim(q_rope, n * QB, QB, axis=1)
        pq = lax.dynamic_slice_in_dim(pos, n * QB, QB, axis=0)
        s = (jnp.einsum('bqhd,bkhd->bhqk', qn, k_nope)
             + jnp.einsum('bqhd,bkd->bhqk', qr, k_rope)).astype(jnp.float32) * scale
        s = jnp.where(pq[:, None] >= pos[None, :], s, NEG_INF)
        p = jax.nn.softmax(s, axis=-1)
        return jnp.einsum('bhqk,bkhd->bqhd', p.astype(v.dtype), v)

    o = lax.map(one_block, jnp.arange(S // QB))
    return o.transpose(1, 0, 2, 3, 4).reshape(B, S, H * MLA_V)

def token_mixing(h, pos, table, w_in, nsa_pe_k, nsa_w1_k, nsa_w2_k, nsa_pe_v, nsa_w1_v, nsa_w2_v,
                 swa_sinks, mla_q_norm, mla_w_qb, mla_kv_norm, mla_w_kvb, w_branch, w_out):
    B, S, _ = h.shape
    (nq, nkc, nvc, nks, nvs, nkw, nvw, ngate, sq, sk, sv,
     mq, mkv, mkr, mgate) = split_cols(h @ w_in)
    kvs_a = (B, S, NSA_KV, HEAD_DIM)
    o_a = nsa_attention(nq.reshape(B, S, NSA_KV, NSA_GROUP, HEAD_DIM),
                        nkc.reshape(kvs_a), nvc.reshape(kvs_a), nks.reshape(kvs_a),
                        nvs.reshape(kvs_a), nkw.reshape(kvs_a), nvw.reshape(kvs_a),
                        ngate, pos, table[:, :NSA_HEADS],
                        nsa_pe_k, nsa_w1_k, nsa_w2_k, nsa_pe_v, nsa_w1_v, nsa_w2_v)
    kvs_b = (B, S, SWA_KV, HEAD_DIM)
    o_b = banded_attention(sq.reshape(B, S, SWA_KV, SWA_GROUP, HEAD_DIM),
                           sk.reshape(kvs_b), sv.reshape(kvs_b), SWA_WINDOW,
                           table[:, NSA_HEADS:], swa_sinks).reshape(B, S, BRANCH_WIDTH)
    o_c = mla_attention(mq, mkv, mkr, pos, mla_q_norm, mla_w_qb, mla_kv_norm, mla_w_kvb)
    branches = jnp.stack([o_a, o_b, o_c], axis=2)
    y = jnp.einsum('bsnc,ncd->bsnd', branches, w_branch)
    gates = jax.nn.sigmoid(mgate.astype(jnp.float32)).reshape(B, S, N_BRANCH, D_MODEL).astype(y.dtype)
    return jnp.sum(gates * y, axis=2) @ w_out

def setup_inputs(seed: int = 0) -> dict:
    key = jax.random.key(seed)
    ks = jax.random.split(key, 26)
    f32 = jnp.float32
    L = DEPTH

    def dense(k, shape, fan_in):
        return jax.random.normal(k, shape, f32) * fan_in ** -0.5

    def gain(k, shape):
        return 1.0 + 0.05 * jax.random.normal(k, shape, f32)

    return {
        "x": jax.random.normal(ks[0], (BATCH, SEQ, D_MODEL), f32),
        "rel_bias_table": 0.2 * jax.random.normal(ks[1], (NUM_BUCKETS, N_BIAS_HEADS), f32),
        "ffn1_norm_pre": gain(ks[2], (L, D_MODEL)),
        "ffn1_w_gu": dense(ks[3], (L, D_MODEL, 2 * D_FF), D_MODEL),
        "ffn1_w_down": dense(ks[4], (L, D_FF, D_MODEL), D_FF),
        "ffn1_norm_post": gain(ks[5], (L, D_MODEL)),
        "mix_norm_pre": gain(ks[6], (L, D_MODEL)),
        "w_in": dense(ks[7], (L, D_MODEL, IN_WIDTH), D_MODEL),
        "nsa_pe_k": 0.1 * jax.random.normal(ks[8], (L, CMP_LEN, HEAD_DIM), f32),
        "nsa_w1_k": dense(ks[9], (L, CMP_LEN * HEAD_DIM, CMP_HIDDEN), CMP_LEN * HEAD_DIM),
        "nsa_w2_k": dense(ks[10], (L, CMP_HIDDEN, HEAD_DIM), CMP_HIDDEN),
        "nsa_pe_v": 0.1 * jax.random.normal(ks[11], (L, CMP_LEN, HEAD_DIM), f32),
        "nsa_w1_v": dense(ks[12], (L, CMP_LEN * HEAD_DIM, CMP_HIDDEN), CMP_LEN * HEAD_DIM),
        "nsa_w2_v": dense(ks[13], (L, CMP_HIDDEN, HEAD_DIM), CMP_HIDDEN),
        "swa_sinks": jax.random.normal(ks[14], (L, SWA_HEADS), f32),
        "mla_q_norm": gain(ks[15], (L, MLA_Q_RANK)),
        "mla_w_qb": dense(ks[16], (L, MLA_Q_RANK, MLA_HEADS * (MLA_NOPE + MLA_ROPE)), MLA_Q_RANK),
        "mla_kv_norm": gain(ks[17], (L, MLA_KV_RANK)),
        "mla_w_kvb": dense(ks[18], (L, MLA_KV_RANK, MLA_HEADS * (MLA_NOPE + MLA_V)), MLA_KV_RANK),
        "w_branch": dense(ks[19], (L, N_BRANCH, BRANCH_WIDTH, D_MODEL), BRANCH_WIDTH),
        "w_out": dense(ks[20], (L, D_MODEL, D_MODEL), D_MODEL),
        "mix_norm_post": gain(ks[21], (L, D_MODEL)),
        "ffn2_norm_pre": gain(ks[22], (L, D_MODEL)),
        "ffn2_w_gu": dense(ks[23], (L, D_MODEL, 2 * D_FF), D_MODEL),
        "ffn2_w_down": dense(ks[24], (L, D_FF, D_MODEL), D_FF),
        "ffn2_norm_post": gain(ks[25], (L, D_MODEL)),
    }

def reference(x, rel_bias_table, ffn1_norm_pre, ffn1_w_gu, ffn1_w_down, ffn1_norm_post,
              mix_norm_pre, w_in, nsa_pe_k, nsa_w1_k, nsa_w2_k, nsa_pe_v, nsa_w1_v, nsa_w2_v,
              swa_sinks, mla_q_norm, mla_w_qb, mla_kv_norm, mla_w_kvb, w_branch, w_out,
              mix_norm_post, ffn2_norm_pre, ffn2_w_gu, ffn2_w_down, ffn2_norm_post):
    pos = jnp.arange(x.shape[1], dtype=jnp.int32)
    for l in range(DEPTH):
        x = macaron_ffn(x, ffn1_norm_pre[l], ffn1_w_gu[l], ffn1_w_down[l], ffn1_norm_post[l])
        h = rmsnorm(x, mix_norm_pre[l])
        m = token_mixing(h, pos, rel_bias_table, w_in[l],
                         nsa_pe_k[l], nsa_w1_k[l], nsa_w2_k[l], nsa_pe_v[l], nsa_w1_v[l], nsa_w2_v[l],
                         swa_sinks[l], mla_q_norm[l], mla_w_qb[l], mla_kv_norm[l], mla_w_kvb[l],
                         w_branch[l], w_out[l])
        x = x + rmsnorm(m, mix_norm_post[l])
        x = macaron_ffn(x, ffn2_norm_pre[l], ffn2_w_gu[l], ffn2_w_down[l], ffn2_norm_post[l])
    return x


_drawn_inputs = setup_inputs


def setup_inputs(seed=0):
    import zlib

    import numpy as np

    out = dict(_drawn_inputs(seed))
    spreads = {}
    factors = {'nsa_pe_k': 5.565, 'mla_q_norm': 3.17}
    for name, (base, spread) in spreads.items():
        noise = np.random.default_rng([zlib.crc32(name.encode()), seed]).standard_normal(out[name].shape)
        drawn = base * np.exp(spread * noise) if base else spread * noise
        out[name] = jnp.asarray(drawn.astype(out[name].dtype))
    for name, factor in factors.items():
        out[name] = (out[name] * factor).astype(out[name].dtype)
    return out
```

```python
from contextlib import ExitStack

import numpy as np

import concourse.bass as bass
from concourse import mybir

ALU = mybir.AluOpType
ACT = mybir.ActivationFunctionType
F32 = mybir.dt.float32
F32R = mybir.dt.float32r

P = 128
S = 256
D = 1024
L = 2
NH = S // P
KD = D // P
FF = 2816
FW = 256
FJ = FF // FW
EPS = 1e-6
HD = 64
G = 4
HEADS = 8
NCMP = 15
CMP_LEN, CMP_STRIDE, CMP_HID = 32, 16, 128
QR, KVR, ROPE = 384, 256, 32
QK = HD + ROPE
NB = 32
TW = 384
NEG = -1e30
BAR = -1e29
SC = HD ** -0.5
SC_MLA = QK ** -0.5

C_NQ, C_KC, C_KS, C_KW, C_GATE, C_SQ, C_SK = 0, 512, 768, 1024, 1280, 1304, 1816
C_MQ, C_MKR, C_MG = 2072, 2712, 2744
LAT = QR + KVR
TM = LAT + ROPE + 24

RING = 3
CH = 2048
FC = 3 * FJ
MIX0 = FC
M_KC, M_TM, M_NQ, M_KS, M_QB, M_KVB, M_KW, M_SQ, M_SK, M_GATES, M_BR, M_OUT = (
    0, 1, 5, 7, 8, 11, 13, 14, 16, 17, 29, 35)
MC = 39
FFN2_0 = FC + MC
NC = FC + MC + FC
assert NC % RING == 0
GATE_ORDER = [8, 9, 0, 1, 2, 3, 4, 5, 6, 7, 10, 11]
BRANCHES = [(2, 0), (2, 1), (0, 0), (0, 1), (1, 0), (1, 1)]

DMAS = {**{MIX0 + M_TM + i: 2 for i in range(4)}, **{MIX0 + m: 4 for m in (M_NQ, M_NQ + 1, M_SQ, M_SQ + 1)}}
ARRIVED = [16 * sum(DMAS.get(k, 1) for k in range(n % RING, n + 1, RING)) for n in range(NC)]
ARRIVED_LAYER = [ARRIVED[NC - RING + i] for i in range(RING)]

DENSE = [M_KC, M_NQ, M_NQ + 1, M_KS, M_KW, M_SQ, M_SQ + 1, M_SK] + [M_GATES + i for i in range(12)]
DIDX = {m: i for i, m in enumerate(DENSE)}
ND = len(DENSE)

UNITS = [("mla", g, q) for g in range(2) for q in range(2)]
UNITS += [(k, g, q) for g in range(2) for q in range(2) for k in ("cmp", "sel", "win")]
UNITS += [("swa", g, q) for g in range(2) for q in range(2)]
NU = len(UNITS)
OGROUP = [u for u, (k, _, _) in enumerate(UNITS) if k in ("mla", "win", "swa")]
NOG = len(OGROUP)
STEPS = {0: M_SQ + 1, 1: M_SK, 14: M_BR, 16: M_BR + 1, 18: M_BR + 2, 20: M_BR + 3}
STEPS.update({2 + i: M_GATES + i for i in range(12)})
NSTEP = NU + 2


def width(n):
    m = n - MIX0
    if M_TM <= m < M_TM + 4:
        return 2 * TM
    if M_QB <= m < M_QB + QR // P:
        return HEADS * QK
    if M_KVB <= m < M_KVB + KVR // P:
        return HEADS * 2 * HD
    return CH


def group_of(u):
    return next(i for i, last in enumerate(OGROUP) if last >= u)


def keys_of(u):
    kind, _, q = UNITS[u]
    if kind == "cmp":
        return (NCMP if q else 7), 1, 16, SC
    return (S if q else P), (2 if q else 1), (S if q else P), (SC_MLA if kind == "mla" else SC)


def decoder_kernel(nc, A, out):
    ctx = ExitStack()
    with ctx:
        def sb(name, shape, dt=F32):
            return ctx.enter_context(nc.sbuf_tensor(name, shape, dt))

        def sem(name):
            return ctx.enter_context(nc.semaphore(name))

        x = sb("x", [P, NH, D])
        work = sb("work", [P, NH, D])
        hT_hi = sb("hT_hi", [P, KD, S], F32R)
        hT_lo = sb("hT_lo", [P, KD, S], F32R)
        stage = [sb(f"stage{i}", [P, CH]) for i in range(RING)]
        w_hi = [sb(f"w_hi{i}", [P, CH], F32R) for i in range(RING)]
        w_lo = [sb(f"w_lo{i}", [P, CH], F32R) for i in range(RING)]
        bias = sb("bias", [P, 2 * HEADS, S])
        Z = sb("Z", [P, 8192])
        oT_hi = sb("oT_hi", [P, 12, S], F32R)
        oT_lo = sb("oT_lo", [P, 12, S], F32R)
        gpre = sb("gpre", [P, D])
        gpost = sb("gpost", [P, D])
        qsT = sb("qsT", [P, 8, S])
        kT = sb("kT", [P, 3, S])
        vtok = sb("vtok", [P, 3, NH, P])
        ident = sb("ident", [P, P])
        causal = sb("causal", [P, S])
        cs = sb("cs", [P, 2, NH, 16])
        gl = sb("gl", [P, LAT])
        w2 = sb("w2", [P, 2, HD])
        pe_rows = sb("pe_rows", [CMP_LEN, 2, 2, HD])
        peT = sb("peT", [P, 2, CMP_LEN])
        sk8 = sb("sk8", [P, HEADS])
        tm = sb("tm", [P, NH, ROPE + 24])
        krot = sb("krot", [P, NH, ROPE])
        kcmp = sb("kcmp", [P, 16])
        vcmp = sb("vcmp", [16, 2, HD])
        hid = sb("hid", [P, 2, 32])
        table8 = sb("table8", [NB + 1, 2 * HEADS])
        ssq = sb("ssq", [P, 8])
        ms = sb("ms", [P, 8])
        rstd = sb("rstd", [P, 8])
        mhalf = sb("mhalf", [P, 2])
        mx = sb("mx", [P, NU, G])
        nb = sb("nb", [P, NU, G])
        den = sb("den", [P, NU, G])
        fac = sb("fac", [P, NU, G])
        dsk = sb("dsk", [P, 4, G])
        esk = sb("esk", [P, 4, G])

        silu = qsT[:, 0:2, :]
        act = qsT[:, 2:4, :]
        act_hi, act_lo = oT_hi[:, 0:2, :], oT_lo[:, 0:2, :]
        workf = work[:].rearrange("p a b -> p (a b)")
        latn = workf[:, 0:2 * LAT].rearrange("p (h c) -> p h c", h=NH)
        blk = [workf[:, 1280:1760].rearrange("p (l c) -> p l c", c=NCMP),
               qsT[:, 6:8, :].rearrange("p a b -> p (a b)")[:, 0:480].rearrange("p (l c) -> p l c", c=NCMP)]
        kv_raw = qsT[:, 4:6, :]
        ktok = workf[:, 0:NH * HEADS * QK].rearrange("p (h n c) -> p h n c", h=NH, c=QK)
        w1 = Z[:].rearrange("p (v l n) -> p v l n", v=2, l=CMP_LEN)
        mqT = Z[0:QK, 0:2048].rearrange("p (n t) -> p n t", n=HEADS)
        mkT = Z[0:QK, 2048:4096].rearrange("p (n t) -> p n t", n=HEADS)
        rtmp = Z[:, 4096:5120].rearrange("p (i h n c) -> p i h n c", i=4, h=NH, n=HEADS)
        vmla = Z[:, 5120:6144].rearrange("p (h n c) -> p h n c", h=NH, c=HD)
        qtok = Z[:, 6144:7680].rearrange("p (h n c) -> p h n c", h=NH, c=QK)
        gates = Z[:, 0:6144].rearrange("p (i t) -> p i t", t=S)
        rev = Z[:, 0:6144].rearrange("p (i u) -> p i u", u=TW)
        onehot = qsT[:].rearrange("p a b -> p (a b)")[0:NB + 1, 0:2 * TW].rearrange("p (a u) -> p a u", a=2)
        lat_hi, lat_lo = oT_hi[:, 0:5, :], oT_lo[:, 0:5, :]
        mg_hi, mg_lo = hT_hi, hT_lo

        def pt_sb(u):
            return Z[:, 6144 + 1024 * (u % 2):7168 + 1024 * (u % 2)].rearrange("p (k i t) -> p k i t", k=2, i=G)

        def prob(u):
            n, _, _, _ = keys_of(u)
            return work[:, u % 2, :].rearrange("p (i j) -> p i j", i=G)[:, :, 0:n]

        ps = ctx.enter_context(nc.psum_tensor("ps", [P, 8, 512], F32))

        def bank(i):
            return ps[:, i, :]

        def ybanks(h):
            return ps[:, 2 * h:2 * h + 2, :].rearrange("p a b -> p (a b)")

        def s_ps(u):
            n, _, step, _ = keys_of(u)
            return ps[:, 0:2, :].rearrange("p a b -> p (a b)")[:, 0:G * step].rearrange(
                "p (i j) -> p i j", i=G)[:, :, 0:n]

        def o_ps(u):
            return bank(4 + group_of(u) % 2)[:, 0:S].rearrange("p (a t) -> p a t", a=2)

        const_in = sem("const_in")
        table_in = sem("table_in")
        table_ok = sem("table_ok")
        rev_done = sem("rev_done")
        rev_sb = sem("rev_sb")
        rev_out = sem("rev_out")
        bias_in = sem("bias_in")
        w_landed = [sem(f"w_landed{i}") for i in range(RING)]
        w_split_hi = sem("w_split_hi")
        w_split = sem("w_split")
        w_used = sem("w_used")
        gpre_in = sem("gpre_in")
        gpost_in = sem("gpost_in")
        mix_in = sem("mix_in")
        x_sq = sem("x_sq")
        x_r = sem("x_r")
        xn_ok = sem("xn_ok")
        tr_done = sem("tr_done")
        hT_hi_ok = sem("hT_hi_ok")
        hT_ok = sem("hT_ok")
        y_done = sem("y_done")
        y_sq = sem("y_sq")
        y_r = sem("y_r")
        x_up = sem("x_up")
        silu_ok = sem("silu_ok")
        mul_ok = sem("mul_ok")
        act_hi_ok = sem("act_hi_ok")
        act_ok = sem("act_ok")
        d_evac = sem("d_evac")
        pe_tr = sem("pe_tr")
        pe_ev = sem("pe_ev")
        blk_ok = sem("blk_ok")
        hid_done = sem("hid_done")
        gelu_ok = sem("gelu_ok")
        cmp_done = sem("cmp_done")
        cmp_ev = sem("cmp_ev")
        lat_sq = sem("lat_sq")
        lat_r = sem("lat_r")
        lat_n = sem("lat_n")
        lat_tr = sem("lat_tr")
        lat_hi_ok = sem("lat_hi_ok")
        lat_ok = sem("lat_ok")
        ng_exp = sem("ng_exp")
        q_cp = sem("q_cp")
        q_ok = sem("q_ok")
        q_tr = sem("q_tr")
        q_ev = sem("q_ev")
        kv_cp = sem("kv_cp")
        k_ok = sem("k_ok")
        k_tr = sem("k_tr")
        k_ev = sem("k_ev")
        sc_done = sem("sc_done")
        sm_bias = sem("sm_bias")
        sm_exp = sem("sm_exp")
        sm_norm = sem("sm_norm")
        pt_done = sem("pt_done")
        pt_ev = sem("pt_ev")
        pv_done = sem("pv_done")
        o_hi_ok = sem("o_hi_ok")
        o_ok = sem("o_ok")
        b_half = sem("b_half")
        b_ev = sem("b_ev")
        mg_sum = sem("mg_sum")
        mg_hi_ok = sem("mg_hi_ok")
        mg_ok = sem("mg_ok")
        out_sem = sem("out_sem")
        passed = sem("passed")

        rev_dram = nc.dram_tensor("rev_rows", (2 * HEADS, P, TW), F32, kind="Internal").ap()

        block = ctx.enter_context(nc.Block())

        def used(l, n, dj=None):
            v = l * NC + (n + 1 + RING)
            return v if dj is None else v + dj * RING

        split = used

        def free(l, n, dj=None):
            v = l * NC + (n + 1)
            return v if dj is None else v + dj * RING

        def landed(l, n, dj=None):
            v = l * ARRIVED_LAYER[n % RING] + ARRIVED[n]
            return v if dj is None else v + dj * 16

        def nth(l, per_layer, k, dj=None):
            v = l * per_layer + (k + 1)
            return v if dj is None else v + dj

        def chunk_g(c0, j):
            return c0 + (3 * j - 1 if j else 0)

        def chunk_u(c0, j):
            return c0 + (3 * j if j else 1)

        def chunk_d(c0, j):
            return c0 + (3 * j + 4 if j < FJ - 1 else FC - 1)

        def wait_apart(eng, semaphore, value):
            eng.wait_ge(semaphore, value)
            eng.sem_inc(passed, 1)

        FFN_LOOP = (2, FJ - 1)

        @block.sync
        def _(sp):
            sp.dma_start(onehot, A["c_onehot"]).then_inc(table_in, 16)
            sp.dma_start(table8[0:NB, :], A["rel_bias_table"]).then_inc(table_in, 16)
            sp.dma_start(x[:], A["x"].rearrange("b (h p) d -> p (b h) d", p=P)).then_inc(const_in, 16)
            sp.dma_start(ident[:], A["c_ident"]).then_inc(const_in, 16)
            sp.dma_start(causal[:], A["c_causal"]).then_inc(const_in, 16)
            sp.dma_start(cs[:], A["c_rope"]).then_inc(const_in, 16)

            def chunk(l, n, pieces, dj=None):
                target = sp.snap(free(l, n, dj))
                slot = stage[n % RING]
                for i, (dst, src) in enumerate(pieces(slot)):
                    if i == 0:
                        wait_apart(sp, w_split, target)
                    sp.dma_start(dst, src).then_inc(w_landed[n % RING], 16)

            def columns(w, l, at, width=FW, k0=0, kn=KD, off=0, pitch=None):
                pitch = pitch or width

                def of(slot):
                    dst = slot[:, 0:kn * pitch].rearrange("p (k c) -> p k c", k=kn)[:, :, off:off + width]
                    src = A[w][l, k0 * P:(k0 + kn) * P, bass.ds(at, width)].rearrange("(k p) c -> p k c", p=P)
                    return dst, src
                return of

            def one(*args, **kw):
                return lambda slot: [columns(*args, **kw)(slot)]

            def ffn(l, c0, gu, down):
                def gate(j, jr, dj):
                    chunk(l, chunk_g(c0, j), lambda s: [columns(gu, l, jr * FW)(s)], dj)

                def up(j, jr, dj):
                    chunk(l, chunk_u(c0, j), lambda s: [columns(gu, l, jr * FW + FF)(s)], dj)

                def rows(j, jr, dj):
                    def of(slot):
                        dst = slot[:].rearrange("p (k c) -> p k c", k=2)
                        src = A[down][l, bass.ds(jr * FW, FW), :].rearrange("(k p) c -> p k c", p=P)
                        return [(dst, src)]
                    chunk(l, chunk_d(c0, j), of, dj)

                gate(0, 0, None)
                up(0, 0, None)
                gate(1, 1, None)
                up(1, 1, None)
                rows(0, 0, None)
                lo, hi = FFN_LOOP
                with sp.Fori(0, hi - lo) as dj:
                    gate(lo, dj + lo, dj)
                    up(lo, dj + lo, dj)
                    rows(lo - 1, dj + (lo - 1), dj)
                gate(FJ - 1, FJ - 1, None)
                up(FJ - 1, FJ - 1, None)
                rows(FJ - 2, FJ - 2, None)
                rows(FJ - 1, FJ - 1, None)

            with sp.Fori(0, L) as l:
                ffn(l, 0, "ffn1_w_gu", "ffn1_w_down")

                def m(k, *sources):
                    chunk(l, MIX0 + k, lambda s: [f(s) for f in sources])

                def pairs(at, t):
                    return [columns("w_in", l, at + (2 * t + i // 2 + G * (i % 2)) * HD, HD, off=i * HD, pitch=FW)
                            for i in range(4)]

                m(M_KC, columns("w_in", l, C_KC))
                for i in range(4):
                    m(M_TM + i, columns("w_in", l, C_MQ, LAT + ROPE, 2 * i, 2, 0, TM),
                      columns("w_in", l, C_GATE, 24, 2 * i, 2, LAT + ROPE, TM))
                m(M_NQ, *pairs(C_NQ, 0))
                m(M_NQ + 1, *pairs(C_NQ, 1))
                m(M_KS, columns("w_in", l, C_KS))
                for i in range(QR // P):
                    m(M_QB + i, columns("mla_w_qb", l, 0, HEADS * QK, i, 1))
                for i in range(KVR // P):
                    m(M_KVB + i, columns("mla_w_kvb", l, 0, HEADS * 2 * HD, i, 1))
                m(M_KW, columns("w_in", l, C_KW))
                m(M_SQ, *pairs(C_SQ, 0))
                m(M_SQ + 1, *pairs(C_SQ, 1))
                m(M_SK, columns("w_in", l, C_SK))
                for i, c in enumerate(GATE_ORDER):
                    m(M_GATES + i, columns("w_in", l, C_MG + c * FW))
                for i, (n, half) in enumerate(BRANCHES):
                    def branch(slot, n=n, half=half):
                        src = A["w_branch"][l, n, :, half * 512:half * 512 + 512]
                        return (slot[:].rearrange("p (k c) -> p k c", k=4), src.rearrange("(k p) c -> p k c", p=P))
                    m(M_BR + i, branch)
                for i in range(4):
                    m(M_OUT + i, columns("w_out", l, 0, D, 2 * i, 2))
                ffn(l, FFN2_0, "ffn2_w_gu", "ffn2_w_down")

            sp.wait_ge(x_up, NH + L * 3 * NH)
            sp.dma_start(out.rearrange("b (h p) d -> p (b h) d", p=P), x[:]).then_inc(out_sem, 16)
            sp.wait_ge(out_sem, 16)

        @block.gpsimd
        def _(pool):
            pool.memset(mhalf[:], -0.5)

            def inv_rms(at, n, over, four):
                k = 4.0 if four else 1.0
                nc.gpsimd.tensor_scalar(ms[:, at:at + n], ssq[:, at:at + n], k / over, k * EPS, ALU.mult, ALU.add)
                pool.drain()
                return nc.gpsimd.tensor_tensor(rstd[:, at:at + n], ms[:, at:at + n], mhalf[:, 0:n], ALU.pow)

            def gains(l, sub):
                return [("ffn1_norm_pre", "ffn1_norm_post"), ("mix_norm_pre", "mix_norm_post"),
                        ("ffn2_norm_pre", "ffn2_norm_post")][sub]

            def norm_in(l, sub):
                for h in range(NH):
                    wait_apart(pool, x_sq, nth(l, 6, 2 * sub + h))
                    inv_rms(h, 1, D, False).then_inc(x_r, 1)
                if sub < 2:
                    wait_apart(pool, xn_ok, nth(l, 6, 2 * sub + 1))
                    pool.dma_start(gpre[:], A[gains(l, sub + 1)[0]][l, :].partition_broadcast(P)).then_inc(gpre_in, 16)

            def norm_out(l, sub):
                for h in range(NH):
                    wait_apart(pool, y_sq, nth(l, 6, 2 * sub + h))
                    inv_rms(2 + h, 1, D, sub != 1).then_inc(y_r, 1)
                if sub < 2:
                    wait_apart(pool, x_up, nth(l, 6, 2 * sub + 1 + NH))
                    pool.dma_start(gpost[:], A[gains(l, sub + 1)[1]][l, :].partition_broadcast(P)).then_inc(gpost_in, 16)

            pool.drain()
            with pool.Fori(0, L) as l:
                pool.dma_start(gpre[:], A["ffn1_norm_pre"][l, :].partition_broadcast(P)).then_inc(gpre_in, 16)
                wait_apart(pool, x_up, l * 6 + NH)
                pool.dma_start(gpost[:], A["ffn1_norm_post"][l, :].partition_broadcast(P)).then_inc(gpost_in, 16)
                norm_in(l, 0)
                pool.wait_ge(rev_out, 16)
                toeplitz = bass.AP(rev_dram.tensor, P - 1, [[TW - 1, P], [TW * P, 2 * HEADS], [1, S]])
                pool.dma_start(bias[:], toeplitz).then_inc(mix_in, 16)
                for v, name in enumerate(("nsa_w1_k", "nsa_w1_v")):
                    for g in range(2):
                        pool.dma_start(w1[HD * g:HD * g + HD, v], A[name][l].rearrange("(l d) n -> d l n", d=HD)
                                       ).then_inc(mix_in, 16)
                for v, name in enumerate(("nsa_w2_k", "nsa_w2_v")):
                    pool.dma_start(w2[:, v, :], A[name][l]).then_inc(mix_in, 16)
                for v, name in enumerate(("nsa_pe_k", "nsa_pe_v")):
                    for g in range(2):
                        pool.dma_start(pe_rows[:, v, g, :], A[name][l]).then_inc(mix_in, 16)
                pool.dma_start(sk8[:], A["swa_sinks"][l, :].partition_broadcast(P)).then_inc(mix_in, 16)
                pool.dma_start(gl[:, 0:QR], A["mla_q_norm"][l, :].partition_broadcast(P)).then_inc(mix_in, 16)
                pool.dma_start(gl[:, QR:LAT], A["mla_kv_norm"][l, :].partition_broadcast(P)).then_inc(mix_in, 16)
                norm_out(l, 0)
                norm_in(l, 1)
                wait_apart(pool, lat_sq, l + 1)
                inv_rms(4, 2, QR, False)
                inv_rms(6, 2, KVR, False).then_inc(lat_r, 1)
                norm_out(l, 1)
                norm_in(l, 2)
                norm_out(l, 2)

        MIX_LOADS = 14 * 16
        MIX_LAST = MIX_LOADS - 1

        @block.scalar
        def _(act_):
            copy = ACT.Copy

            def hi(l, n, dj=None):
                if n >= NC:
                    return
                act_.wait_ge(w_landed[n % RING], landed(l, n, dj))
                act_.wait_ge(w_used, free(l, n, dj))
                nc.scalar.activation(w_hi[n % RING][:, 0:width(n)], stage[n % RING][:, 0:width(n)], copy
                                     ).then_inc(w_split_hi, 1)

            def norm_in(l, sub):
                for h in range(NH):
                    act_.wait_ge(x_up, l * 6 + (2 * sub + h + 1))
                    nc.scalar.activation(work[:, h, :], x[:, h, :], ACT.Square, accum_out=ssq[:, h:h + 1]
                                         ).then_inc(x_sq, 1)
                for h in range(NH):
                    act_.wait_ge(tr_done, nth(l, 6, 2 * sub + h))
                    for b in range(2):
                        nc.scalar.activation(hT_hi[:, 4 * b:4 * b + 4, h * P:h * P + P],
                                             bank(4 + 2 * h + b).rearrange("p (k t) -> p k t", k=4), copy
                                             ).then_inc(hT_hi_ok, 1)

            def norm_out(l, sub, last):
                for h in range(NH):
                    if h == 0:
                        act_.wait_ge(y_done, nth(l, 3, sub))
                    else:
                        act_.wait_ge(w_used, used(l, last))
                    nc.scalar.activation(work[:, h, :], ybanks(h), ACT.Square, accum_out=ssq[:, 2 + h:3 + h]
                                         ).then_inc(y_sq, 1)

            def ffn(l, f, c0):
                def step(j, dj=None):
                    n = chunk_g(c0, j)
                    hi(l, n + RING, dj)
                    act_.wait_ge(w_used, used(l, n, dj))
                    if j:
                        act_.wait_ge(mul_ok, nth(l, 2 * FJ, f * FJ + j - 1, dj))
                    nc.scalar.activation(silu, bank(4).rearrange("p (a t) -> p a t", a=2), ACT.Silu).then_inc(silu_ok, 1)
                    hi(l, chunk_u(c0, j) + RING, dj)
                    act_.wait_ge(mul_ok, nth(l, 2 * FJ, f * FJ + j, dj))
                    if j:
                        act_.wait_ge(w_used, used(l, chunk_d(c0, j - 1), dj))
                    nc.scalar.activation(act_hi, act, copy).then_inc(act_hi_ok, 1)
                    if j:
                        hi(l, chunk_d(c0, j - 1) + RING, dj)

                step(0)
                step(1)
                with act_.Fori(0, FFN_LOOP[1] - FFN_LOOP[0]) as dj:
                    step(FFN_LOOP[0], dj)
                step(FJ - 1)
                hi(l, chunk_d(c0, FJ - 1) + RING)

            def project_out(l, m_):
                i = DIDX[m_]
                n = MIX0 + m_
                src = bank(6 + i % 2)
                pair = src.rearrange("p (a t) -> p a t", a=2)
                act_.wait_ge(w_used, used(l, n))
                if m_ == M_KC:
                    ins = nc.scalar.activation(kv_raw, pair, copy)
                elif m_ in (M_NQ, M_NQ + 1):
                    t = 2 * (m_ - M_NQ)
                    ins = nc.scalar.activation(qsT[:, t:t + 2, :], pair, copy)
                elif m_ in (M_SQ, M_SQ + 1):
                    t = 4 + 2 * (m_ - M_SQ)
                    ins = nc.scalar.activation(qsT[:, t:t + 2, :], pair, copy)
                elif m_ in (M_KS, M_KW, M_SK):
                    k = (M_KS, M_KW, M_SK).index(m_)
                    nc.scalar.activation(kT[:, k, :], src[:, 0:S], copy)
                    ins = nc.scalar.activation(vtok[:, k], src[:, S:2 * S].rearrange("p (a t) -> p a t", a=2), copy)
                else:
                    c = GATE_ORDER[m_ - M_GATES]
                    ins = nc.scalar.activation(gates[:, 2 * c:2 * c + 2, :], pair, ACT.Exp, scale=-1.0)
                ins.then_inc(d_evac, 1)
                hi(l, n + RING)

            for h in range(2 * HEADS):
                act_.wait_ge(rev_done, h + 1)
                nc.scalar.activation(rev[:, h, :], bank(h % 8)[:, 0:TW], copy).then_inc(rev_sb, 1)
            act_.wait_ge(rev_sb, 2 * HEADS)
            act_.dma_start(rev_dram.rearrange("h p u -> p h u"), rev).then_inc(rev_out, 16)

            with act_.Fori(0, L) as l:
                for n in range(RING):
                    hi(l, n)
                norm_in(l, 0)
                ffn(l, 0, 0)
                norm_out(l, 0, FC - 1)
                norm_in(l, 1)

                project_out(l, M_KC)
                act_.wait_ge(pe_tr, l + 1)
                nc.scalar.activation(peT[:], bank(4)[:, 0:2 * CMP_LEN].rearrange("p (v l) -> p v l", v=2), copy
                                     ).then_inc(pe_ev, 1)
                for i in range(4):
                    hi(l, MIX0 + M_TM + i + RING)
                act_.wait_ge(w_used, used(l, MIX0 + M_TM + 3))
                for part, (col, w) in enumerate(((0, QR), (0, KVR))):
                    for h in range(NH):
                        k = 4 + 2 * part + h
                        ins = nc.scalar.activation(latn[:, h, QR * part:QR * part + w],
                                                   bank(2 * h + part)[:, col:col + w], ACT.Square,
                                                   accum_out=ssq[:, k:k + 1])
                ins.then_inc(lat_sq, 1)
                project_out(l, M_NQ)
                project_out(l, M_NQ + 1)
                act_.wait_ge(hid_done, l + 1)
                for g in range(2):
                    ins = nc.scalar.activation(hid[:, g, 0:32].rearrange("p (v c) -> p v c", v=2)[:, :, 0:NCMP],
                                               bank(4 + g)[:, 0:32].rearrange("p (v c) -> p v c", v=2)[:, :, 0:NCMP],
                                               ACT.Gelu_apprx_tanh)
                ins.then_inc(gelu_ok, 1)
                act_.wait_ge(lat_tr, l + 1)
                for b in range(3):
                    n = 2 if b < 2 else 1
                    ins = nc.scalar.activation(lat_hi[:, 2 * b:2 * b + n, :],
                                               bank(b)[:, 0:n * S].rearrange("p (a t) -> p a t", a=n), copy)
                    ins.then_inc(lat_hi_ok, 1)
                act_.wait_ge(lat_n, l + 1)
                nc.scalar.activation(tm[:, :, ROPE:], tm[:, :, ROPE:], ACT.Exp, scale=-1.0).then_inc(ng_exp, 1)
                project_out(l, M_KS)
                act_.wait_ge(cmp_done, l + 1)
                nc.scalar.activation(kcmp[:, 0:NCMP], bank(4)[:, 0:NCMP], copy)
                nc.scalar.activation(vcmp[0:NCMP], bank(5)[0:NCMP, 0:P].rearrange("p (g d) -> p g d", g=2), copy
                                     ).then_inc(cmp_ev, 1)
                for i in range(3):
                    hi(l, MIX0 + M_QB + i + RING)
                act_.wait_ge(w_used, used(l, MIX0 + M_QB + 2))
                for h in range(NH):
                    for p in range(2):
                        ins = nc.scalar.activation(qtok[:, h, 4 * p:4 * p + 4, :],
                                                   bank(2 * h + p)[:, 0:4 * QK].rearrange("p (n c) -> p n c", n=4), copy)
                ins.then_inc(q_cp, 1)
                for i in range(2):
                    hi(l, MIX0 + M_KVB + i + RING)
                act_.wait_ge(w_used, used(l, MIX0 + M_KVB + 1))
                for h in range(NH):
                    for p in range(2):
                        src = bank(4 + 2 * h + p).rearrange("p (n c) -> p n c", n=4)
                        nc.scalar.activation(ktok[:, h, 4 * p:4 * p + 4, 0:HD], src[:, :, 0:HD], copy)
                        ins = nc.scalar.activation(vmla[:, h, 4 * p:4 * p + 4, :], src[:, :, HD:], copy)
                ins.then_inc(kv_cp, 1)
                project_out(l, M_KW)
                act_.wait_ge(q_tr, l + 1)
                for b in range(4):
                    ins = nc.scalar.activation(mqT[:, 2 * b:2 * b + 2, :],
                                               bank(b)[0:QK, :].rearrange("p (n t) -> p n t", n=2), copy)
                ins.then_inc(q_ev, 1)
                project_out(l, M_SQ)
                act_.wait_ge(k_tr, l + 1)
                for b in range(4):
                    ins = nc.scalar.activation(mkT[:, 2 * b:2 * b + 2, :],
                                               bank(b)[0:QK, :].rearrange("p (n t) -> p n t", n=2), copy)
                ins.then_inc(k_ev, 1)

                for s in range(NSTEP):
                    if s < NU:
                        kind, g, q = UNITS[s]
                        scale = keys_of(s)[3]
                        act_.wait_ge(sm_bias, nth(l, NU, s))
                        for i in range(G):
                            ins = nc.scalar.activation(prob(s)[:, i, :], prob(s)[:, i, :], ACT.Exp,
                                                       bias=nb[:, s, i:i + 1], scale=scale,
                                                       accum_out=den[:, s, i:i + 1])
                        if kind == "swa":
                            k = s - (NU - 4)
                            ins = nc.scalar.activation(esk[:, k, :], dsk[:, k, :], ACT.Exp, scale=SC)
                        ins.then_inc(sm_exp, 1)
                    if 0 <= s - 1 < NU:
                        u = s - 1
                        n, tiles, _, _ = keys_of(u)
                        rows = min(n, P)
                        act_.wait_ge(pt_done, nth(l, NU, u))
                        if u >= 2:
                            act_.wait_ge(pv_done, nth(l, NU, u - 2))
                        nc.scalar.activation(pt_sb(u)[0:rows, 0:tiles],
                                             ps[0:rows, 2:2 + tiles, :].rearrange("p k (i t) -> p k i t", i=G), copy
                                             ).then_inc(pt_ev, 1)
                    if s in STEPS:
                        if STEPS[s] in DIDX:
                            project_out(l, STEPS[s])
                        else:
                            hi(l, MIX0 + STEPS[s] + RING)
                    u = s - 2
                    if u in OGROUP:
                        kind, g, q = UNITS[u]
                        t = {"win": 0, "swa": 4, "mla": 8}[kind] + 2 * g
                        act_.wait_ge(pv_done, nth(l, NU, u))
                        nc.scalar.activation(oT_hi[:, t:t + 2, q * P:q * P + P], o_ps(u), copy).then_inc(o_hi_ok, 1)

                for i in (4, 5):
                    hi(l, MIX0 + M_BR + i + RING)
                for half in range(2):
                    act_.wait_ge(mg_sum, nth(l, 4, 2 * half + 1))
                    nc.scalar.activation(mg_hi[:, 4 * half:4 * half + 4, :], gates[:, 16 + 4 * half:20 + 4 * half, :],
                                         copy).then_inc(mg_hi_ok, 1)
                for i in range(4):
                    hi(l, MIX0 + M_OUT + i + RING)
                norm_out(l, 1, FFN2_0 - 1)
                norm_in(l, 2)
                ffn(l, 1, FFN2_0)
                norm_out(l, 2, NC - 1)

        @block.vector
        def _(dve):
            def lo(l, n, dj=None):
                if n >= NC:
                    return
                dve.wait_ge(w_split_hi, nth(l, NC, n) if dj is None else nth(l, NC, n, dj * RING))
                w = slice(0, width(n))
                nc.vector.tensor_tensor(w_lo[n % RING][:, w], stage[n % RING][:, w],
                                        w_hi[n % RING][:, w].bitcast(F32), ALU.subtract).then_inc(w_split, 1)

            def norm_in(l, sub):
                dve.wait_ge(gpre_in, l * 48 + 16 * (sub + 1))
                for h in range(NH):
                    dve.wait_ge(x_r, nth(l, 6, 2 * sub + h))
                    nc.vector.scalar_tensor_tensor(work[:, h, :], x[:, h, :], rstd[:, h:h + 1], gpre[:],
                                                   ALU.mult, ALU.mult).then_inc(xn_ok, 1)
                for h in range(NH):
                    for b in range(2):
                        dve.wait_ge(hT_hi_ok, nth(l, 12, 4 * sub + 2 * h + b))
                        t = (slice(None), slice(4 * b, 4 * b + 4), slice(h * P, h * P + P))
                        nc.vector.tensor_tensor(hT_lo[t], bank(4 + 2 * h + b).rearrange("p (k t) -> p k t", k=4),
                                                hT_hi[t].bitcast(F32), ALU.subtract).then_inc(hT_ok, 1)

            def norm_out(l, sub):
                dve.wait_ge(gpost_in, l * 48 + 16 * (sub + 1))
                for h in range(NH):
                    dve.wait_ge(y_r, nth(l, 6, 2 * sub + h))
                    nc.vector.scalar_tensor_tensor(work[:, h, :], ybanks(h), rstd[:, 2 + h:3 + h], gpost[:],
                                                   ALU.mult, ALU.mult)
                    dve.drain()
                    nc.vector.tensor_tensor(x[:, h, :], x[:, h, :], work[:, h, :], ALU.add).then_inc(x_up, 1)

            def ffn(l, f, c0):
                def step(j, dj=None):
                    lo(l, chunk_g(c0, j) + RING, dj)
                    dve.wait_ge(silu_ok, nth(l, 2 * FJ, f * FJ + j, dj))
                    dve.wait_ge(w_used, used(l, chunk_u(c0, j), dj))
                    if j:
                        dve.wait_ge(act_ok, nth(l, 2 * FJ, f * FJ + j - 1, dj))
                    nc.vector.tensor_tensor(act, bank(5).rearrange("p (a t) -> p a t", a=2), silu, ALU.mult
                                            ).then_inc(mul_ok, 1)
                    lo(l, chunk_u(c0, j) + RING, dj)
                    dve.wait_ge(act_hi_ok, nth(l, 2 * FJ, f * FJ + j, dj))
                    nc.vector.tensor_tensor(act_lo, act, act_hi.bitcast(F32), ALU.subtract).then_inc(act_ok, 1)
                    if j:
                        lo(l, chunk_d(c0, j - 1) + RING, dj)

                step(0)
                step(1)
                with dve.Fori(0, FFN_LOOP[1] - FFN_LOOP[0]) as dj:
                    step(FFN_LOOP[0], dj)
                step(FJ - 1)
                lo(l, chunk_d(c0, FJ - 1) + RING)

            def rope(src, dst, heads):
                x1, x2 = src[:, :, :, 0:16], src[:, :, :, 16:32]
                cos, sin = (cs[:, i].unsqueeze(2).to_broadcast([P, NH, heads, 16]) for i in range(2))
                t = [rtmp[:, i, :, 0:heads, :] for i in range(4)]
                nc.vector.tensor_tensor(t[0], x1, cos, ALU.mult)
                nc.vector.tensor_tensor(t[1], x2, sin, ALU.mult)
                nc.vector.tensor_tensor(t[2], x1, sin, ALU.mult)
                nc.vector.tensor_tensor(t[3], x2, cos, ALU.mult)
                dve.drain()
                nc.vector.tensor_tensor(dst[:, :, :, 0:16], t[0], t[1], ALU.subtract)
                return nc.vector.tensor_tensor(dst[:, :, :, 16:32], t[2], t[3], ALU.add)

            def biased(l, u):
                kind, g, q = UNITS[u]
                n, _, _, scale = keys_of(u)
                off = 0 if q else P
                if u >= 2:
                    dve.wait_ge(pt_done, nth(l, NU, u - 2))
                wait_apart(dve, sc_done, nth(l, NU, u))
                for i in range(G):
                    if kind == "mla":
                        b = causal[:, off:off + n]
                    elif kind == "cmp":
                        first = CMP_LEN - 1 + off
                        b = bias[:, G * g + i, first:first + CMP_STRIDE * (n - 1) + 1:CMP_STRIDE]
                    else:
                        b = bias[:, (HEADS if kind == "swa" else 0) + G * g + i, off:off + n]
                    nc.vector.tensor_tensor_reduce(prob(u)[:, i, :], s_ps(u)[:, i, :], b, 1.0, -3.0e38,
                                                   ALU.add, ALU.max, mx[:, u, i:i + 1])
                dve.drain()
                if kind == "cmp":
                    ins = nc.vector.tensor_scalar(nb[:, u, :], mx[:, u, :], BAR, -scale, ALU.max, ALU.mult)
                elif kind == "swa":
                    k = u - (NU - 4)
                    sink = sk8[:, G * g:G * g + G]
                    nc.vector.tensor_tensor(mx[:, u, :], mx[:, u, :], sink, ALU.max)
                    dve.drain()
                    nc.vector.tensor_tensor(dsk[:, k, :], sink, mx[:, u, :], ALU.subtract)
                    ins = nc.vector.tensor_scalar(nb[:, u, :], mx[:, u, :], -scale, None, ALU.mult)
                else:
                    ins = nc.vector.tensor_scalar(nb[:, u, :], mx[:, u, :], -scale, None, ALU.mult)
                ins.then_inc(sm_bias, 1)

            def normalised(l, u):
                kind, g, q = UNITS[u]
                n = keys_of(u)[0]
                dve.wait_ge(sm_exp, nth(l, NU, u))
                if kind == "cmp":
                    nc.vector.tensor_scalar(den[:, u, :], den[:, u, :], 1e-30, None, ALU.max)
                    dve.drain()
                elif kind == "swa":
                    nc.vector.tensor_tensor(den[:, u, :], den[:, u, :], esk[:, u - (NU - 4), :], ALU.add)
                    dve.drain()
                nc.vector.reciprocal(fac[:, u, :], den[:, u, :])
                dve.drain()
                if kind in ("cmp", "sel", "win"):
                    first = ROPE + 3 * G * g + ("cmp", "sel", "win").index(kind)
                    nc.vector.tensor_tensor(fac[:, u, :], fac[:, u, :], tm[:, q, first:first + 3 * (G - 1) + 1:3],
                                            ALU.mult)
                    dve.drain()
                nc.vector.tensor_tensor(prob(u), prob(u), fac[:, u, :].unsqueeze(2).to_broadcast([P, G, n]),
                                        ALU.mult).then_inc(sm_norm, 1)

            def gate_final(l, m_):
                c = GATE_ORDER[m_ - M_GATES]
                t = gates[:, 2 * c:2 * c + 2, :]
                dve.wait_ge(d_evac, nth(l, ND, DIDX[m_]))
                nc.vector.tensor_scalar(t, t, 1.0, None, ALU.add)
                dve.drain()
                nc.vector.reciprocal(t, t)

            def merged(l, b):
                n, half = BRANCHES[b]
                for p in range(2):
                    t = 4 * half + 2 * p
                    src = bank(6 + p).rearrange("p (a t) -> p a t", a=2)
                    gate, total = gates[:, 8 * n + t:8 * n + t + 2, :], gates[:, 16 + t:18 + t, :]
                    dve.drain()
                    if p == 0:
                        dve.wait_ge(b_half, nth(l, 6, b))
                    else:
                        dve.wait_ge(w_used, used(l, MIX0 + M_BR + b))
                    nc.vector.tensor_tensor(gate, src, gate, ALU.mult).then_inc(b_ev, 1)
                    if b >= 2:
                        dve.drain()
                        ins = nc.vector.tensor_tensor(total, total, gate, ALU.add)
                        if b >= 4:
                            ins.then_inc(mg_sum, 1)
                lo(l, MIX0 + M_BR + b + RING)

            nc.vector.memset(table8[NB:NB + 1, :], 8 * NEG)
            dve.wait_ge(table_in, 32)
            nc.vector.tensor_scalar(table8[0:NB, :], table8[0:NB, :], 8.0, None, ALU.mult).then_inc(table_ok, 1)
            dve.sem_inc(w_split, RING)
            dve.wait_ge(const_in, 64)
            dve.sem_inc(x_up, NH)

            with dve.Fori(0, L) as l:
                for n in range(RING):
                    lo(l, n)
                norm_in(l, 0)
                ffn(l, 0, 0)
                norm_out(l, 0)
                norm_in(l, 1)

                lo(l, MIX0 + M_KC + RING)
                dve.wait_ge(mix_in, l * MIX_LOADS + MIX_LOADS)
                nc.vector.tensor_scalar(sk8[:], sk8[:], 1.0 / SC, None, ALU.mult)
                dve.wait_ge(pe_ev, l + 1)
                dve.wait_ge(d_evac, nth(l, ND, 0))
                for v in range(2):
                    for part in range(2):
                        at = CMP_STRIDE * part
                        tok = kv_raw[:, v, at:at + CMP_STRIDE * NCMP].rearrange("p (c l) -> p l c", l=CMP_STRIDE)
                        pos = peT[:, v, at:at + CMP_STRIDE].unsqueeze(2).to_broadcast([P, CMP_STRIDE, NCMP])
                        ins = nc.vector.tensor_tensor(blk[v][:, at:at + CMP_STRIDE, :], tok, pos, ALU.add)
                ins.then_inc(blk_ok, 1)
                for i in range(4):
                    lo(l, MIX0 + M_TM + i + RING)
                dve.wait_ge(lat_r, l + 1)
                for part, w in enumerate((QR, KVR)):
                    for h in range(NH):
                        c = slice(QR * part, QR * part + w)
                        k = 4 + 2 * part + h
                        nc.vector.scalar_tensor_tensor(latn[:, h, c], bank(2 * h + part)[:, 0:w], rstd[:, k:k + 1],
                                                       gl[:, c], ALU.mult, ALU.mult)
                for h in range(NH):
                    ins = nc.vector.tensor_copy(tm[:, h, :], bank(2 * h + 1)[:, KVR:KVR + ROPE + 24])
                ins.then_inc(lat_n, 1)
                lo(l, MIX0 + M_NQ + RING)
                lo(l, MIX0 + M_NQ + 1 + RING)
                for b in range(3):
                    n = 2 if b < 2 else 1
                    dve.wait_ge(lat_hi_ok, nth(l, 3, b))
                    ins = nc.vector.tensor_tensor(lat_lo[:, 2 * b:2 * b + n, :],
                                                  bank(b)[:, 0:n * S].rearrange("p (a t) -> p a t", a=n),
                                                  lat_hi[:, 2 * b:2 * b + n, :].bitcast(F32), ALU.subtract)
                ins.then_inc(lat_ok, 1)
                dve.wait_ge(ng_exp, l + 1)
                nc.vector.tensor_scalar(tm[:, :, ROPE:], tm[:, :, ROPE:], 1.0, None, ALU.add)
                dve.drain()
                nc.vector.reciprocal(tm[:, :, ROPE:], tm[:, :, ROPE:])
                lo(l, MIX0 + M_KS + RING)
                for i in range(3):
                    lo(l, MIX0 + M_QB + i + RING)
                dve.wait_ge(hid_done, l + 1)
                rope(tm[:, :, 0:ROPE].unsqueeze(2), krot[:].unsqueeze(2), 1)
                dve.drain()
                dve.wait_ge(q_cp, l + 1)
                rope(qtok[:, :, :, HD:], qtok[:, :, :, HD:], HEADS).then_inc(q_ok, 1)
                for i in range(2):
                    lo(l, MIX0 + M_KVB + i + RING)
                dve.wait_ge(kv_cp, l + 1)
                for h in range(NH):
                    ins = nc.vector.tensor_copy(ktok[:, h, :, HD:], krot[:, h:h + 1, :].to_broadcast([P, HEADS, ROPE]))
                ins.then_inc(k_ok, 1)
                lo(l, MIX0 + M_KW + RING)
                lo(l, MIX0 + M_SQ + RING)

                for s in range(NSTEP):
                    if s < NU:
                        biased(l, s)
                        normalised(l, s)
                    u = s - 2
                    if s in STEPS:
                        m_ = STEPS[s]
                        if m_ in DIDX:
                            lo(l, MIX0 + m_ + RING)
                            if m_ >= M_GATES:
                                gate_final(l, m_)
                        else:
                            merged(l, m_ - M_BR)
                    if u in OGROUP:
                        kind, g, q = UNITS[u]
                        t = {"win": 0, "swa": 4, "mla": 8}[kind] + 2 * g
                        dst = (slice(None), slice(t, t + 2), slice(q * P, q * P + P))
                        dve.wait_ge(o_hi_ok, nth(l, NOG, OGROUP.index(u)))
                        nc.vector.tensor_tensor(oT_lo[dst], o_ps(u), oT_hi[dst].bitcast(F32), ALU.subtract
                                                ).then_inc(o_ok, 1)
                for b in (4, 5):
                    merged(l, b)
                for half in range(2):
                    dve.wait_ge(mg_hi_ok, nth(l, 2, half))
                    t = slice(4 * half, 4 * half + 4)
                    nc.vector.tensor_tensor(mg_lo[:, t, :], gates[:, 16 + 4 * half:20 + 4 * half, :],
                                            mg_hi[:, t, :].bitcast(F32), ALU.subtract).then_inc(mg_ok, 1)
                for i in range(4):
                    lo(l, MIX0 + M_OUT + i + RING)
                norm_out(l, 1)
                norm_in(l, 2)
                ffn(l, 1, FFN2_0)
                norm_out(l, 2)

        @block.tensor
        def _(pe):
            def mm3(dst, a, b, start, stop):
                (a_hi, a_lo), (b_hi, b_lo) = a, b
                nc.tensor.matmul(dst, a_hi, b_hi, start=start, stop=False)
                nc.tensor.matmul(dst, a_hi, b_lo, start=False, stop=False)
                return nc.tensor.matmul(dst, a_lo, b_hi, start=False, stop=stop)

            def both(hi_, lo_, *at):
                return hi_[at], lo_[at]

            def ring(n, lo_, hi_):
                at = (slice(None), slice(lo_, hi_))
                return both(w_hi[n % RING], w_lo[n % RING], *at)

            def tokens(h):
                return slice(h * P, h * P + P)

            ALL = slice(None)

            def turn(dst, src):
                rows = src.shape[0]
                return nc.tensor.transpose(dst, src, ident[0:rows, 0:rows])

            def norm_in(l, sub):
                for h in range(NH):
                    pe.wait_ge(xn_ok, nth(l, 6, 2 * sub + h))
                    for k in range(KD):
                        ins = turn(bank(4 + 2 * h + k // 4)[:, (k % 4) * P:(k % 4) * P + P],
                                   work[:, h, k * P:k * P + P])
                    ins.then_inc(tr_done, 1)
                pe.wait_ge(hT_ok, nth(l, 12, 4 * sub + 3))

            def two_tiles(n, dst):
                for c in range(2):
                    for k in range(KD):
                        a = ring(n, k * FW + c * P, k * FW + c * P + P)
                        ins = mm3(dst[:, c * S:c * S + S], a, both(hT_hi, hT_lo, ALL, k, ALL), k == 0, k == KD - 1)
                return ins

            def rows_out(l, n, sub, lhs, first, last, dj=None):
                for h in range(NH):
                    for kt in range(2):
                        for c in range(2):
                            ins = mm3(bank(2 * h + c), lhs(kt, h), ring(n, kt * D + c * 512, kt * D + c * 512 + 512),
                                      first and kt == 0, last and kt == 1)
                    if last and h == 0:
                        ins.then_inc(y_done, 1)
                ins.then_inc(w_used, 1)

            def ffn(l, f, c0):
                def down(j, dj=None):
                    n = chunk_d(c0, j)
                    pe.wait_ge(w_split, split(l, n, dj))
                    pe.wait_ge(act_ok, nth(l, 2 * FJ, f * FJ + j, dj))
                    rows_out(l, n, 2 * f, lambda kt, h: both(act_hi, act_lo, ALL, kt, tokens(h)),
                             j == 0, j == FJ - 1)

                def step(j, dj=None):
                    n = chunk_g(c0, j)
                    pe.wait_ge(w_split, split(l, n, dj))
                    if j:
                        pe.wait_ge(silu_ok, nth(l, 2 * FJ, f * FJ + j - 1, dj))
                    two_tiles(n, bank(4)).then_inc(w_used, 1)
                    n = chunk_u(c0, j)
                    pe.wait_ge(w_split, split(l, n, dj))
                    if j:
                        pe.wait_ge(mul_ok, nth(l, 2 * FJ, f * FJ + j - 1, dj))
                    two_tiles(n, bank(5)).then_inc(w_used, 1)
                    if j:
                        down(j - 1, dj)

                step(0)
                step(1)
                with pe.Fori(0, FFN_LOOP[1] - FFN_LOOP[0]) as dj:
                    step(FFN_LOOP[0], dj)
                step(FJ - 1)
                down(FJ - 1)

            def project(l, m_):
                n, i = MIX0 + m_, DIDX[m_]
                dst = bank(6 + i % 2)
                pe.wait_ge(w_split, split(l, n))
                if i >= 2:
                    pe.wait_ge(d_evac, nth(l, ND, i - 2))
                if m_ in (M_KS, M_KW, M_SK):
                    for k in range(KD):
                        mm3(dst[:, 0:S], ring(n, k * FW, k * FW + P), both(hT_hi, hT_lo, ALL, k, ALL),
                            k == 0, k == KD - 1)
                    for h in range(NH):
                        for k in range(KD):
                            ins = mm3(dst[:, S + h * P:S + h * P + P], both(hT_hi, hT_lo, ALL, k, tokens(h)),
                                      ring(n, k * FW + P, k * FW + 2 * P), k == 0, k == KD - 1)
                else:
                    ins = two_tiles(n, dst)
                ins.then_inc(w_used, 1)

            def scores(l, u):
                kind, g, q = UNITS[u]
                n, _, _, _ = keys_of(u)
                if u == 0:
                    pe.wait_ge(k_ev, l + 1)
                else:
                    pe.wait_ge(sm_bias, nth(l, NU, u - 1))
                if kind == "cmp":
                    pe.wait_ge(cmp_ev, l + 1)
                if kind == "sel":
                    pe.wait_ge(d_evac, nth(l, ND, DIDX[M_KS]))
                if kind == "win":
                    pe.wait_ge(d_evac, nth(l, ND, DIDX[M_KW]))
                if kind == "swa":
                    pe.wait_ge(d_evac, nth(l, ND, DIDX[M_SK]))
                rows = slice(HD * g, HD * g + HD)
                for i in range(G):
                    if kind == "mla":
                        a, b = mqT[:, G * g + i, tokens(q)], mkT[:, G * g + i, 0:n]
                    else:
                        a = qsT[rows, (4 if kind == "swa" else 0) + i, tokens(q)]
                        b = (kcmp[rows, 0:n] if kind == "cmp"
                             else kT[rows, ("sel", "win", "swa").index(kind), 0:n])
                    ins = nc.tensor.matmul(s_ps(u)[:, i, :], a, b, start=True, stop=True)
                ins.then_inc(sc_done, 1)

            def turn_p(l, u):
                n, tiles, _, _ = keys_of(u)
                rows = min(n, P)
                pe.wait_ge(sm_norm, nth(l, NU, u))
                if u >= 1:
                    pe.wait_ge(pt_ev, nth(l, NU, u - 1))
                for kt in range(tiles):
                    for i in range(G):
                        ins = turn(bank(2 + kt)[0:rows, i * P:i * P + P], prob(u)[:, i, kt * P:kt * P + rows])
                ins.then_inc(pt_done, 1)

            def values(l, u):
                kind, g, q = UNITS[u]
                n, tiles, _, _ = keys_of(u)
                rows = min(n, P)
                og = group_of(u)
                first = kind in ("cmp", "mla", "swa")
                last = kind in ("win", "mla", "swa")
                pe.wait_ge(pt_ev, nth(l, NU, u))
                if first and og >= 2:
                    pe.wait_ge(o_ok, nth(l, NOG, og - 2))
                for odd in range(2):
                    part = slice(HD * odd, HD * odd + HD)
                    if kind == "mla":
                        for pair in range(2):
                            i = 2 * pair + odd
                            for kt in range(tiles):
                                ins = nc.tensor.matmul(o_ps(u)[part, pair, :], vmla[:, kt, G * g + i, :],
                                                       pt_sb(u)[:, kt, i, :], start=kt == 0, stop=kt == tiles - 1)
                        continue
                    for kt in range(tiles):
                        v = (vcmp[0:rows, g, :] if kind == "cmp" else
                             vtok[:, ("sel", "win", "swa").index(kind), kt, HD * g:HD * g + HD])
                        ins = nc.tensor.matmul(o_ps(u)[part], v, pt_sb(u)[0:rows, kt, odd:G:2, :],
                                               start=first and kt == 0, stop=last and kt == tiles - 1)
                ins.then_inc(pv_done, 1)

            def branch(l, b):
                n, (br, half) = MIX0 + M_BR + b, BRANCHES[b]
                base = 4 * br
                pe.wait_ge(w_split, split(l, n))
                if b in (0, 2, 4):
                    done = max(i for i, u in enumerate(OGROUP) if UNITS[u][0] == ("win", "swa", "mla")[br])
                    pe.wait_ge(o_ok, nth(l, NOG, done))
                for p in range(2):
                    if b == 0:
                        pe.wait_ge(d_evac, nth(l, ND, ND - 2 + p))
                    else:
                        pe.wait_ge(b_ev, nth(l, 12, 2 * (b - 1) + p))
                    for c in range(2):
                        for k in range(4):
                            at = k * 512 + (2 * p + c) * P
                            ins = mm3(bank(6 + p)[:, c * S:c * S + S], ring(n, at, at + P),
                                      both(oT_hi, oT_lo, ALL, base + k, ALL), k == 0, k == 3)
                    ins.then_inc(b_half if p == 0 else w_used, 1)

            pe.sem_inc(w_used, RING)
            pe.wait_ge(table_ok, 1)
            for h in range(2 * HEADS):
                if h >= 8:
                    pe.wait_ge(rev_sb, h - 7)
                nc.tensor.matmul(bank(h % 8)[:, 0:TW], table8[:, h:h + 1].to_broadcast([NB + 1, P]),
                                 onehot[:, h // HEADS, :], start=True, stop=True).then_inc(rev_done, 1)
            pe.wait_ge(rev_sb, 2 * HEADS)
            pe.wait_ge(const_in, 64)

            with pe.Fori(0, L) as l:
                norm_in(l, 0)
                ffn(l, 0, 0)
                norm_in(l, 1)
                project(l, M_KC)
                wait_apart(pe, mix_in, l * MIX_LOADS + MIX_LOADS)
                for v in range(2):
                    ins = turn(bank(4)[:, v * CMP_LEN:v * CMP_LEN + CMP_LEN],
                               pe_rows[:, v].rearrange("p g d -> p (g d)"))
                ins.then_inc(pe_tr, 1)
                for i in range(4):
                    n = MIX0 + M_TM + i
                    pe.wait_ge(w_split, split(l, n))
                    for h in range(NH):
                        for kt in range(2):
                            k = 2 * i + kt
                            a = both(hT_hi, hT_lo, ALL, k, tokens(h))
                            for dst, lo_, hi_ in ((bank(2 * h), 0, QR), (bank(2 * h + 1), QR, TM)):
                                ins = mm3(dst[:, 0:hi_ - lo_], a, ring(n, kt * TM + lo_, kt * TM + hi_),
                                          k == 0, k == KD - 1)
                    ins.then_inc(w_used, 1)
                project(l, M_NQ)
                project(l, M_NQ + 1)
                pe.wait_ge(blk_ok, l + 1)
                for g in range(2):
                    rows = slice(HD * g, HD * g + HD)
                    for v in range(2):
                        for i in range(CMP_LEN):
                            ins = nc.tensor.matmul(bank(4 + g)[:, 16 * v:16 * v + NCMP], w1[rows, v, i, :],
                                                   blk[v][rows, i, :], start=i == 0, stop=i == CMP_LEN - 1)
                ins.then_inc(hid_done, 1)
                pe.wait_ge(lat_n, l + 1)
                for t in range(LAT // P):
                    for h in range(NH):
                        ins = turn(bank(t // 2)[:, (t % 2) * S + h * P:(t % 2) * S + h * P + P],
                                   latn[:, h, t * P:t * P + P])
                ins.then_inc(lat_tr, 1)
                project(l, M_KS)
                pe.wait_ge(gelu_ok, l + 1)
                for g in range(2):
                    nc.tensor.matmul(bank(4)[HD * g:HD * g + HD, 0:NCMP], w2[:, 0, :], hid[:, g, 0:NCMP],
                                     start=True, stop=True)
                for g in range(2):
                    ins = nc.tensor.matmul(bank(5)[0:NCMP, HD * g:HD * g + HD], hid[:, g, 16:16 + NCMP], w2[:, 1, :],
                                           start=True, stop=True)
                ins.then_inc(cmp_done, 1)
                pe.wait_ge(lat_ok, l + 1)
                for i in range(QR // P):
                    n = MIX0 + M_QB + i
                    pe.wait_ge(w_split, split(l, n))
                    for h in range(NH):
                        for p in range(2):
                            ins = mm3(bank(2 * h + p)[:, 0:4 * QK], both(lat_hi, lat_lo, ALL, i, tokens(h)),
                                      ring(n, p * 4 * QK, (p + 1) * 4 * QK), i == 0, i == QR // P - 1)
                    ins.then_inc(w_used, 1)
                pe.wait_ge(cmp_ev, l + 1)
                pe.wait_ge(d_evac, nth(l, ND, DIDX[M_KS]))
                for i in range(KVR // P):
                    n = MIX0 + M_KVB + i
                    pe.wait_ge(w_split, split(l, n))
                    for h in range(NH):
                        for p in range(2):
                            ins = mm3(bank(4 + 2 * h + p), both(lat_hi, lat_lo, ALL, QR // P + i, tokens(h)),
                                      ring(n, p * 512, (p + 1) * 512), i == 0, i == KVR // P - 1)
                    ins.then_inc(w_used, 1)
                pe.wait_ge(kv_cp, l + 1)
                project(l, M_KW)
                pe.wait_ge(q_ok, l + 1)
                for n in range(HEADS):
                    for h in range(NH):
                        ins = turn(bank(n // 2)[0:QK, (n % 2) * S + h * P:(n % 2) * S + h * P + P], qtok[:, h, n, :])
                ins.then_inc(q_tr, 1)
                project(l, M_SQ)
                pe.wait_ge(k_ok, l + 1)
                pe.wait_ge(q_ev, l + 1)
                for n in range(HEADS):
                    for h in range(NH):
                        ins = turn(bank(n // 2)[0:QK, (n % 2) * S + h * P:(n % 2) * S + h * P + P], ktok[:, h, n, :])
                ins.then_inc(k_tr, 1)

                for s in range(NSTEP):
                    if s < NU:
                        scores(l, s)
                    if s in STEPS:
                        if STEPS[s] in DIDX:
                            project(l, STEPS[s])
                        else:
                            branch(l, STEPS[s] - M_BR)
                    if 0 <= s - 1 < NU:
                        turn_p(l, s - 1)
                    if s >= 2:
                        values(l, s - 2)
                branch(l, 4)
                branch(l, 5)
                for i in range(4):
                    n = MIX0 + M_OUT + i
                    pe.wait_ge(w_split, split(l, n))
                    pe.wait_ge(mg_ok, nth(l, 2, i // 2))
                    rows_out(l, n, 1, lambda kt, h, i=i: both(mg_hi, mg_lo, ALL, 2 * i + kt, tokens(h)),
                             i == 0, i == 3)
                norm_in(l, 2)
                ffn(l, 1, FFN2_0)


_INS = ["x", "rel_bias_table", "ffn1_norm_pre", "ffn1_w_gu", "ffn1_w_down", "ffn1_norm_post",
        "mix_norm_pre", "w_in", "nsa_pe_k", "nsa_w1_k", "nsa_w2_k", "nsa_pe_v", "nsa_w1_v", "nsa_w2_v",
        "swa_sinks", "mla_q_norm", "mla_w_qb", "mla_kv_norm", "mla_w_kvb", "w_branch", "w_out",
        "mix_norm_post", "ffn2_norm_pre", "ffn2_w_gu", "ffn2_w_down", "ffn2_norm_post"]


def shape_constants():
    dist = np.arange(S, dtype=np.int32)
    ratio = np.log(np.maximum(dist, 1).astype(np.float32) / np.float32(16)) / np.float32(np.log(64.0))
    far = np.minimum(16 + (ratio * np.float32(16)).astype(np.int32), NB - 1)
    bucket = np.where(dist < 16, dist, far)
    onehot = np.zeros((NB + 1, 2, TW), np.float32)
    for u in range(TW):
        d = S - 1 - u
        for kind, window in enumerate((S, P)):
            onehot[bucket[d] if 0 <= d < window else NB, kind, u] = 1.0
    p, j = np.arange(P)[:, None], np.arange(S)[None, :]
    causal = np.where(P + p - j >= 0, 0.0, NEG).astype(np.float32)
    inv = (10000.0 ** (-np.arange(16, dtype=np.float32) / 16)).astype(np.float32)
    ang = np.arange(S, dtype=np.float32)[:, None] * inv[None, :]
    rope = np.stack([np.cos(ang), np.sin(ang)]).astype(np.float32).reshape(2, NH, P, 16).transpose(2, 0, 1, 3)
    return {"c_onehot": onehot, "c_causal": causal, "c_rope": rope, "c_ident": np.eye(P, dtype=np.float32)}


def kernel(**inputs):
    import concourse.bacc as _bacc
    from concourse import mybir as _mybir
    from concourse.bass_utils import run_bass_kernel_spmd as _run

    nc = _bacc.Bacc("TRN2", target_bir_lowering=False, num_devices=1)
    arrays, aps = {}, {}
    for name, a in list((n, inputs[n]) for n in _INS) + list(shape_constants().items()):
        a = np.ascontiguousarray(a)
        arrays[f"in_{name}_dram"] = a
        aps[name] = nc.dram_tensor(f"in_{name}_dram", a.shape, _mybir.dt.from_np(a.dtype), kind="ExternalInput").ap()
    out = nc.dram_tensor("out_0_dram", (1, S, D), _mybir.dt.float32, kind="ExternalOutput").ap()
    decoder_kernel(nc, aps, out)
    r = _run(nc, [arrays], core_ids=[0])
    return r.results[0]["out_0_dram"]
```

```python
from contextlib import ExitStack

import numpy as np

import concourse.bass as bass
from concourse import mybir

ALU = mybir.AluOpType
ACT = mybir.ActivationFunctionType
F32 = mybir.dt.float32
F32R = mybir.dt.float32r

P = 128
S = 256
D = 1024
L = 2
NH = S // P
KD = D // P
FF = 2816
FW = 256
FJ = FF // FW
EPS = 1e-6
HD = 64
G = 4
HEADS = 8
NCMP = 15
CMP_LEN, CMP_STRIDE, CMP_HID = 32, 16, 128
QR, KVR, ROPE = 384, 256, 32
QK = HD + ROPE
NB = 32
TW = 384
NEG = -1e30
BAR = -1e29
SC = HD ** -0.5
SC_MLA = QK ** -0.5

C_NQ, C_KC, C_KS, C_KW, C_GATE, C_SQ, C_SK, C_SV = 0, 512, 768, 1024, 1280, 1304, 1816, 1944
C_MG = 2744
LAT = QR + KVR
TM1 = P + QR
TM2 = KVR + ROPE + 24
TM = TM1 + TM2

RING = 3
CH = 2048
FC = 3 * FJ
MIX0 = FC
M_TM, M_KC, M_NQ, M_QB, M_KK, M_KVB, M_VV, M_SQ, M_SK, M_GATES, M_BR, M_OUT = (
    0, 4, 5, 7, 10, 11, 13, 14, 16, 17, 29, 35)
MC = 39
FFN2_0 = FC + MC
NC = FC + MC + FC
assert NC % RING == 0
GATE_ORDER = [8, 9, 0, 1, 2, 3, 4, 5, 6, 7, 10, 11]
BRANCHES = [(2, 0), (2, 1), (0, 0), (0, 1), (1, 0), (1, 1)]

DMAS = {**{MIX0 + m: 2 for m in (*range(M_TM, M_TM + 4), M_KK, M_VV)}, **{MIX0 + m: 4 for m in (M_NQ, M_NQ + 1, M_SQ, M_SQ + 1)}}
ARRIVED = [16 * sum(DMAS.get(k, 1) for k in range(n % RING, n + 1, RING)) for n in range(NC)]
ARRIVED_LAYER = [ARRIVED[NC - RING + i] for i in range(RING)]

DENSE = [M_KC, M_NQ, M_NQ + 1, M_KK, M_VV, M_SQ, M_SQ + 1, M_SK] + [M_GATES + i for i in range(12)]
DIDX = {m: i for i, m in enumerate(DENSE)}
ND = len(DENSE)

UNITS = [("mla", g, q) for g in range(2) for q in range(2)]
UNITS += [(k, g, q) for g in range(2) for q in range(2) for k in ("cmp", "sel", "win")]
UNITS += [("swa", g, q) for g in range(2) for q in range(2)]
NU = len(UNITS)
OGROUP = [u for u, (k, _, _) in enumerate(UNITS) if k in ("mla", "win", "swa")]
NOG = len(OGROUP)
STEPS = {0: M_SK, 14: M_BR, 16: M_BR + 1, 18: M_BR + 2, 22: M_BR + 3}
STEPS.update({1 + i: M_GATES + i for i in range(12)})
NSTEP = NU + 3


def width(n):
    m = n - MIX0
    if M_TM <= m < M_TM + 4:
        return 2 * TM
    if M_QB <= m < M_QB + QR // P:
        return HEADS * QK
    if M_KVB <= m < M_KVB + KVR // P:
        return HEADS * 2 * HD
    if m == M_SK:
        return KD * P
    return CH


def group_of(u):
    return next(i for i, last in enumerate(OGROUP) if last >= u)


def keys_of(u):
    kind, _, q = UNITS[u]
    if kind == "cmp":
        return (NCMP if q else 7), 1, 16, SC
    return (S if q else P), (2 if q else 1), (S if q else P), (SC_MLA if kind == "mla" else SC)


def decoder_kernel(nc, A, out):
    ctx = ExitStack()
    with ctx:
        def sb(name, shape, dt=F32):
            return ctx.enter_context(nc.sbuf_tensor(name, shape, dt))

        def sem(name):
            return ctx.enter_context(nc.semaphore(name))

        x = sb("x", [P, NH, D])
        work = sb("work", [P, NH, D])
        hT_hi = sb("hT_hi", [P, KD, S], F32R)
        hT_lo = sb("hT_lo", [P, KD, S], F32R)
        stage = [sb(f"stage{i}", [P, CH]) for i in range(RING)]
        w_hi = [sb(f"w_hi{i}", [P, CH], F32R) for i in range(RING)]
        w_lo = [sb(f"w_lo{i}", [P, CH], F32R) for i in range(RING)]
        bias = sb("bias", [P, 2 * HEADS, S])
        Z = sb("Z", [P, 8192])
        oT_hi = sb("oT_hi", [P, 12, S], F32R)
        oT_lo = sb("oT_lo", [P, 12, S], F32R)
        gpre = sb("gpre", [P, D])
        gpost = sb("gpost", [P, D])
        qsT = sb("qsT", [P, 8, S])
        kT = sb("kT", [P, 3, S])
        vtok = sb("vtok", [P, 3, NH, P])
        ident = sb("ident", [P, P])
        causal = sb("causal", [P, S])
        cs = sb("cs", [P, 2, NH, 16])
        gl = sb("gl", [P, LAT])
        w2 = sb("w2", [P, 2, HD])
        pe_rows = sb("pe_rows", [CMP_LEN // 2, 2, P])
        peT = sb("peT", [P, 2, CMP_LEN // 2])
        sk8 = sb("sk8", [P, HEADS])
        tm = sb("tm", [P, NH, ROPE + 24])
        krot = sb("krot", [P, NH, ROPE])
        kcmp = sb("kcmp", [P, 16])
        vcmp = sb("vcmp", [16, 2, HD])
        hid = sb("hid", [P, 2, 2 * NCMP])
        table8 = sb("table8", [NB + 1, 2 * HEADS])
        ssq = sb("ssq", [P, 8])
        ms = sb("ms", [P, 8])
        rstd = sb("rstd", [P, 8])
        mhalf = sb("mhalf", [P, 2])
        mx = sb("mx", [P, NU, G])
        nb = sb("nb", [P, NU, G])
        den = sb("den", [P, NU, G])
        fac = sb("fac", [P, NU, G])
        dsk = sb("dsk", [P, 4, G])
        esk = sb("esk", [P, 4, G])

        silu = qsT[:, 0:2, :]
        act = qsT[:, 2:4, :]

        def act_split(j):
            t = 2 if j == FJ - 1 else 0
            return oT_hi[:, t:t + 2, :], oT_lo[:, t:t + 2, :]

        workf = work[:].rearrange("p a b -> p (a b)")
        latn = workf[:, 0:2 * LAT].rearrange("p (h c) -> p h c", h=NH)
        kv2 = qsT[:, 4:8, :].rearrange("p (v g) t -> p v g t", v=2)
        blk = [b.rearrange("p (l g c) -> p l g c", g=2, c=NCMP) for b in (workf[:, 1280:1760], Z[:, 7680:8160])]
        ktok = workf[:, 0:NH * HEADS * QK].rearrange("p (h n c) -> p h n c", h=NH, c=QK)
        w1 = Z[:, 0:4096].rearrange("p (v l n) -> p v l n", v=2, l=CMP_LEN // 2)
        mqT = Z[0:QK, 0:2048].rearrange("p (n t) -> p n t", n=HEADS)
        mkT = Z[0:QK, 2048:4096].rearrange("p (n t) -> p n t", n=HEADS)
        rtmp = Z[:, 4096:5120].rearrange("p (i h n c) -> p i h n c", i=4, h=NH, n=HEADS)
        vmla = Z[:, 5120:6144].rearrange("p (h n c) -> p h n c", h=NH, c=HD)
        qtok = Z[:, 6144:7680].rearrange("p (h n c) -> p h n c", h=NH, c=QK)
        gates = Z[:, 0:6144].rearrange("p (i t) -> p i t", t=S)
        rev = Z[0:HEADS, 0:2 * TW].rearrange("p (a u) -> p a u", a=2)
        onehot = qsT[:].rearrange("p a b -> p (a b)")[0:NB + 1, 0:2 * TW].rearrange("p (a u) -> p a u", a=2)
        lat_hi, lat_lo = oT_hi[:, 0:5, :], oT_lo[:, 0:5, :]
        mg_hi, mg_lo = hT_hi, hT_lo

        def pt_sb(u):
            return Z[:, 6144 + 1024 * (u % 2):7168 + 1024 * (u % 2)].rearrange("p (k i t) -> p k i t", k=2, i=G)

        def prob(u):
            n, _, _, _ = keys_of(u)
            return work[:, u % 2, :].rearrange("p (i j) -> p i j", i=G)[:, :, 0:n]

        ps = ctx.enter_context(nc.psum_tensor("ps", [P, 8, 512], F32))

        def bank(i):
            return ps[:, i, :]

        def ybanks(h):
            return ps[:, 2 * h:2 * h + 2, :].rearrange("p a b -> p (a b)")

        def s_ps(u):
            n, _, step, _ = keys_of(u)
            return ps[:, 0:2, :].rearrange("p a b -> p (a b)")[:, 0:G * step].rearrange(
                "p (i j) -> p i j", i=G)[:, :, 0:n]

        def o_ps(u):
            return bank(4 + group_of(u) % 2)[:, 0:S].rearrange("p (a t) -> p a t", a=2)

        x_in = [sem(f"x_in{h}") for h in range(NH)]
        const_in = sem("const_in")
        table_in = sem("table_in")
        table_ok = sem("table_ok")
        rev_done = sem("rev_done")
        rev_sb = sem("rev_sb")
        rev_small = sem("rev_small")
        rev_out = sem("rev_out")
        bias_in = sem("bias_in")
        w_landed = [sem(f"w_landed{i}") for i in range(RING)]
        w_split_hi = sem("w_split_hi")
        w_split = sem("w_split")
        w_used = sem("w_used")
        gpre_in = sem("gpre_in")
        gpost_in = sem("gpost_in")
        mix_in = sem("mix_in")
        x_sq = sem("x_sq")
        x_r = sem("x_r")
        xn_ok = sem("xn_ok")
        tr_done = sem("tr_done")
        hT_hi_ok = sem("hT_hi_ok")
        hT_ok = sem("hT_ok")
        y_done = sem("y_done")
        y_sq = sem("y_sq")
        y_r = sem("y_r")
        x_up = sem("x_up")
        silu_ok = sem("silu_ok")
        mul_ok = sem("mul_ok")
        act_hi_ok = sem("act_hi_ok")
        act_ok = sem("act_ok")
        d_evac = sem("d_evac")
        pe_tr = sem("pe_tr")
        pe_ev = sem("pe_ev")
        blk_ok = sem("blk_ok")
        hid_done = sem("hid_done")
        gelu_ok = sem("gelu_ok")
        cmp_done = sem("cmp_done")
        cmp_ev = sem("cmp_ev")
        lat_sq = sem("lat_sq")
        lat_r = sem("lat_r")
        lat_n = sem("lat_n")
        lat_tr = sem("lat_tr")
        lat_hi_ok = sem("lat_hi_ok")
        lat_ok = sem("lat_ok")
        ng_tanh = sem("ng_tanh")
        q_cp = sem("q_cp")
        q_ok = sem("q_ok")
        q_tr = sem("q_tr")
        q_ev = sem("q_ev")
        kv_cp = sem("kv_cp")
        k_ok = sem("k_ok")
        k_tr = sem("k_tr")
        k_ev = sem("k_ev")
        sc_done = sem("sc_done")
        sm_bias = sem("sm_bias")
        sm_exp = sem("sm_exp")
        sm_norm = sem("sm_norm")
        pt_done = sem("pt_done")
        pt_ev = sem("pt_ev")
        pv_done = sem("pv_done")
        o_hi_ok = sem("o_hi_ok")
        o_ok = sem("o_ok")
        b_half = sem("b_half")
        b_ev = sem("b_ev")
        mg_sum = sem("mg_sum")
        mg_hi_ok = sem("mg_hi_ok")
        mg_ok = sem("mg_ok")
        out_sem = sem("out_sem")
        passed = sem("passed")

        rev_rows = nc.dram_tensor("rev_rows", (2 * HEADS, TW), F32, kind="Internal").ap()
        rev_dram = nc.dram_tensor("rev_copies", (2 * HEADS, P, TW), F32, kind="Internal").ap()

        block = ctx.enter_context(nc.Block())

        def used(l, n, dj=None):
            v = l * NC + (n + 1 + RING)
            return v if dj is None else v + dj * RING

        split = used

        def free(l, n, dj=None):
            v = l * NC + (n + 1)
            return v if dj is None else v + dj * RING

        def landed(l, n, dj=None):
            v = l * ARRIVED_LAYER[n % RING] + ARRIVED[n]
            return v if dj is None else v + dj * 16

        def nth(l, per_layer, k, dj=None):
            v = l * per_layer + (k + 1)
            return v if dj is None else v + dj

        def chunk_g(c0, j):
            return c0 + (3 * j - 1 if j else 0)

        def chunk_u(c0, j):
            return c0 + (3 * j if j else 1)

        def chunk_d(c0, j):
            return c0 + (3 * j + 4 if j < FJ - 1 else FC - 1)

        def wait_apart(eng, semaphore, value):
            eng.wait_ge(semaphore, value)
            eng.sem_inc(passed, 1)

        FFN_LOOP = (2, FJ - 1)

        @block.sync
        def _(sp):
            sp.dma_start(onehot, A["c_onehot"]).then_inc(table_in, 16)
            sp.dma_start(table8[0:NB, :], A["rel_bias_table"]).then_inc(table_in, 16)
            for h in range(NH):
                sp.dma_start(x[:, h, :], A["x"][0, h * P:h * P + P, :]).then_inc(x_in[h], 16)
            sp.dma_start(ident[:], A["c_ident"]).then_inc(const_in, 16)
            sp.dma_start(causal[:], A["c_causal"]).then_inc(const_in, 16)
            sp.dma_start(cs[:], A["c_rope"]).then_inc(const_in, 16)

            def chunk(l, n, pieces, dj=None):
                target = sp.snap(free(l, n, dj))
                slot = stage[n % RING]
                for i, (dst, src) in enumerate(pieces(slot)):
                    if i == 0:
                        wait_apart(sp, w_split, target)
                    sp.dma_start(dst, src).then_inc(w_landed[n % RING], 16)

            def columns(w, l, at, width=FW, k0=0, kn=KD, off=0, pitch=None):
                pitch = pitch or width

                def of(slot):
                    dst = slot[:, 0:kn * pitch].rearrange("p (k c) -> p k c", k=kn)[:, :, off:off + width]
                    src = A[w][l, k0 * P:(k0 + kn) * P, bass.ds(at, width)].rearrange("(k p) c -> p k c", p=P)
                    return dst, src
                return of

            def one(*args, **kw):
                return lambda slot: [columns(*args, **kw)(slot)]

            def ffn(l, c0, gu, down):
                def gate(j, jr, dj):
                    chunk(l, chunk_g(c0, j), lambda s: [columns(gu, l, jr * FW)(s)], dj)

                def up(j, jr, dj):
                    chunk(l, chunk_u(c0, j), lambda s: [columns(gu, l, jr * FW + FF)(s)], dj)

                def rows(j, jr, dj):
                    def of(slot):
                        dst = slot[:].rearrange("p (k c) -> p k c", k=2)
                        src = A[down][l, bass.ds(jr * FW, FW), :].rearrange("(k p) c -> p k c", p=P)
                        return [(dst, src)]
                    chunk(l, chunk_d(c0, j), of, dj)

                gate(0, 0, None)
                up(0, 0, None)
                gate(1, 1, None)
                up(1, 1, None)
                rows(0, 0, None)
                lo, hi = FFN_LOOP
                with sp.Fori(0, hi - lo) as dj:
                    gate(lo, dj + lo, dj)
                    up(lo, dj + lo, dj)
                    rows(lo - 1, dj + (lo - 1), dj)
                gate(FJ - 1, FJ - 1, None)
                up(FJ - 1, FJ - 1, None)
                rows(FJ - 2, FJ - 2, None)
                rows(FJ - 1, FJ - 1, None)

            with sp.Fori(0, L) as l:
                ffn(l, 0, "ffn1_w_gu", "ffn1_w_down")

                def m(k, *sources):
                    chunk(l, MIX0 + k, lambda s: [f(s) for f in sources])

                def pairs(at, t):
                    return [columns("w_in", l, at + (2 * t + i // 2 + G * (i % 2)) * HD, HD, off=i * HD, pitch=FW)
                            for i in range(4)]

                for i in range(4):
                    m(M_TM + i, columns("w_in", l, C_SV, TM - 24, 2 * i, 2, 0, TM),
                      columns("w_in", l, C_GATE, 24, 2 * i, 2, TM - 24, TM))
                m(M_KC, columns("w_in", l, C_KC))
                m(M_NQ, *pairs(C_NQ, 0))
                m(M_NQ + 1, *pairs(C_NQ, 1))
                for i in range(QR // P):
                    m(M_QB + i, columns("mla_w_qb", l, 0, HEADS * QK, i, 1))
                m(M_KK, columns("w_in", l, C_KS, P, pitch=FW), columns("w_in", l, C_KW, P, off=P, pitch=FW))
                for i in range(KVR // P):
                    m(M_KVB + i, columns("mla_w_kvb", l, 0, HEADS * 2 * HD, i, 1))
                m(M_VV, columns("w_in", l, C_KS + P, P, pitch=FW), columns("w_in", l, C_KW + P, P, off=P, pitch=FW))
                m(M_SQ, *pairs(C_SQ, 0))
                m(M_SQ + 1, *pairs(C_SQ, 1))
                m(M_SK, columns("w_in", l, C_SK, P))
                for i, c in enumerate(GATE_ORDER):
                    m(M_GATES + i, columns("w_in", l, C_MG + c * FW))
                for i, (n, half) in enumerate(BRANCHES):
                    def branch(slot, n=n, half=half):
                        src = A["w_branch"][l, n, :, half * 512:half * 512 + 512]
                        return (slot[:].rearrange("p (k c) -> p k c", k=4), src.rearrange("(k p) c -> p k c", p=P))
                    m(M_BR + i, branch)
                for i in range(4):
                    m(M_OUT + i, columns("w_out", l, 0, D, 2 * i, 2))
                ffn(l, FFN2_0, "ffn2_w_gu", "ffn2_w_down")

            sp.wait_ge(x_up, NH + L * 3 * NH)
            sp.dma_start(out.rearrange("b (h p) d -> p (b h) d", p=P), x[:]).then_inc(out_sem, 16)
            sp.wait_ge(out_sem, 16)

        @block.gpsimd
        def _(pool):
            pool.memset(mhalf[:], -0.5)

            def inv_rms(at, n, over, four):
                k = 4.0 if four else 1.0
                nc.gpsimd.tensor_scalar(ms[:, at:at + n], ssq[:, at:at + n], k / over, k * EPS, ALU.mult, ALU.add)
                pool.drain()
                return nc.gpsimd.tensor_tensor(rstd[:, at:at + n], ms[:, at:at + n], mhalf[:, 0:n], ALU.pow)

            def gains(l, sub):
                return [("ffn1_norm_pre", "ffn1_norm_post"), ("mix_norm_pre", "mix_norm_post"),
                        ("ffn2_norm_pre", "ffn2_norm_post")][sub]

            def rms_x(l, sub, h):
                wait_apart(pool, x_sq, nth(l, 6, 2 * sub + h))
                inv_rms(h, 1, D, False).then_inc(x_r, 1)

            def rms_y(l, sub, h):
                wait_apart(pool, y_sq, nth(l, 6, 2 * sub + h))
                inv_rms(2 + h, 1, D, sub != 1).then_inc(y_r, 1)

            def boundary(l, sub):
                for h in range(NH):
                    rms_y(l, sub, h)
                    rms_x(l, sub + 1, h)
                wait_apart(pool, x_up, nth(l, 6, 2 * sub + 1 + NH))
                pool.dma_start(gpost[:], A[gains(l, sub + 1)[1]][l, :].partition_broadcast(P)).then_inc(gpost_in, 16)
                next_gain(l, sub + 1)

            def next_gain(l, sub):
                if sub < 2:
                    wait_apart(pool, xn_ok, nth(l, 6, 2 * sub + 1))
                    pool.dma_start(gpre[:], A[gains(l, sub + 1)[0]][l, :].partition_broadcast(P)).then_inc(gpre_in, 16)

            pool.wait_ge(rev_small, 16)
            pool.dma_start(rev_dram, rev_rows.unsqueeze(1).to_broadcast([2 * HEADS, P, TW])).then_inc(rev_out, 16)
            pool.drain()
            with pool.Fori(0, L) as l:
                pool.dma_start(gpre[:], A["ffn1_norm_pre"][l, :].partition_broadcast(P)).then_inc(gpre_in, 16)
                wait_apart(pool, x_up, l * 6 + NH)
                pool.dma_start(gpost[:], A["ffn1_norm_post"][l, :].partition_broadcast(P)).then_inc(gpost_in, 16)
                for h in range(NH):
                    rms_x(l, 0, h)
                next_gain(l, 0)
                pool.wait_ge(rev_out, 16)
                toeplitz = bass.AP(rev_dram.tensor, P - 1, [[TW - 1, P], [TW * P, 2 * HEADS], [1, S]])
                pool.dma_start(bias[:], toeplitz).then_inc(mix_in, 16)
                for v, name in enumerate(("nsa_w1_k", "nsa_w1_v")):
                    pool.dma_start(w1[:, v], A[name][l].rearrange("(l p) n -> p l n", p=P)).then_inc(mix_in, 16)
                for v, name in enumerate(("nsa_w2_k", "nsa_w2_v")):
                    pool.dma_start(w2[:, v, :], A[name][l]).then_inc(mix_in, 16)
                for v, name in enumerate(("nsa_pe_k", "nsa_pe_v")):
                    pool.dma_start(pe_rows[:, v, :], A[name][l].rearrange("(l two) d -> l (two d)", two=2)
                                   ).then_inc(mix_in, 16)
                pool.dma_start(sk8[:], A["swa_sinks"][l, :].partition_broadcast(P)).then_inc(mix_in, 16)
                pool.dma_start(gl[:, 0:QR], A["mla_q_norm"][l, :].partition_broadcast(P)).then_inc(mix_in, 16)
                pool.dma_start(gl[:, QR:LAT], A["mla_kv_norm"][l, :].partition_broadcast(P)).then_inc(mix_in, 16)
                boundary(l, 0)
                wait_apart(pool, lat_sq, l + 1)
                inv_rms(4, 2, QR, False)
                inv_rms(6, 2, KVR, False).then_inc(lat_r, 1)
                boundary(l, 1)
                for h in range(NH):
                    rms_y(l, 2, h)

        MIX_LOADS = 10 * 16
        MIX_LAST = MIX_LOADS - 1

        @block.scalar
        def _(act_):
            copy = ACT.Copy

            def hi(l, n, dj=None):
                if n >= NC:
                    return
                act_.wait_ge(w_landed[n % RING], landed(l, n, dj))
                act_.wait_ge(w_used, free(l, n, dj))
                nc.scalar.activation(w_hi[n % RING][:, 0:width(n)], stage[n % RING][:, 0:width(n)], copy
                                     ).then_inc(w_split_hi, 1)

            def square_x(l, sub, h):
                act_.wait_ge(x_up, l * 6 + (2 * sub + h + 1))
                nc.scalar.activation(work[:, h, :], x[:, h, :], ACT.Square, accum_out=ssq[:, h:h + 1]).then_inc(x_sq, 1)

            def square_y(l, sub, h, last):
                if h == 0:
                    act_.wait_ge(y_done, nth(l, 3, sub))
                else:
                    act_.wait_ge(w_used, used(l, last))
                nc.scalar.activation(work[:, h, :], ybanks(h), ACT.Square, accum_out=ssq[:, 2 + h:3 + h]
                                     ).then_inc(y_sq, 1)

            def turned_hi(l, sub, h):
                act_.wait_ge(tr_done, nth(l, 6, 2 * sub + h))
                for b in range(2):
                    nc.scalar.activation(hT_hi[:, 4 * b:4 * b + 4, h * P:h * P + P],
                                         bank(4 + 2 * h + b).rearrange("p (k t) -> p k t", k=4), copy
                                         ).then_inc(hT_hi_ok, 1)

            def boundary(l, sub, c0):
                square_y(l, sub, 0, c0 - 1)
                hi(l, c0 + 1)
                square_x(l, sub + 1, 0)
                square_y(l, sub, 1, c0 - 1)
                hi(l, c0 + 2)
                turned_hi(l, sub + 1, 0)
                square_x(l, sub + 1, 1)
                turned_hi(l, sub + 1, 1)

            def ffn(l, f, c0):
                def step(j, dj=None):
                    n = chunk_g(c0, j)
                    hi(l, n + RING, dj)
                    act_.wait_ge(w_used, used(l, n, dj))
                    if j:
                        act_.wait_ge(mul_ok, nth(l, 2 * FJ, f * FJ + j - 1, dj))
                    nc.scalar.activation(silu, bank(4).rearrange("p (a t) -> p a t", a=2), ACT.Silu).then_inc(silu_ok, 1)
                    hi(l, chunk_u(c0, j) + RING, dj)
                    act_.wait_ge(mul_ok, nth(l, 2 * FJ, f * FJ + j, dj))
                    if 0 < j < FJ - 1:
                        act_.wait_ge(w_used, used(l, chunk_d(c0, j - 1), dj))
                    nc.scalar.activation(act_split(j)[0], act, copy).then_inc(act_hi_ok, 1)
                    if 0 < j < FJ - 1:
                        hi(l, chunk_d(c0, j - 1) + RING, dj)

                step(0)
                step(1)
                with act_.Fori(0, FFN_LOOP[1] - FFN_LOOP[0]) as dj:
                    step(FFN_LOOP[0], dj)
                step(FJ - 1)

            def project_out(l, m_):
                i = DIDX[m_]
                n = MIX0 + m_
                src = bank(6 + i % 2)
                pair = src.rearrange("p (a t) -> p a t", a=2)
                act_.wait_ge(w_used, used(l, n))
                if m_ == M_KC:
                    for g in range(2):
                        rows = src[HD * g:HD * g + HD, :].rearrange("p (a t) -> p a t", a=2)
                        nc.scalar.activation(kv2[0:HD, :, g, :], rows, copy)
                        ins = nc.scalar.activation(kv2[HD:P, :, g, 0:S - 1], rows[:, :, 1:S], copy)
                elif m_ in (M_NQ, M_NQ + 1):
                    t = 2 * (m_ - M_NQ)
                    ins = nc.scalar.activation(qsT[:, t:t + 2, :], pair, copy)
                elif m_ in (M_SQ, M_SQ + 1):
                    t = 4 + 2 * (m_ - M_SQ)
                    ins = nc.scalar.activation(qsT[:, t:t + 2, :], pair, copy)
                elif m_ == M_KK:
                    ins = nc.scalar.activation(kT[:, 0:2, :], pair, copy)
                elif m_ == M_VV:
                    ins = nc.scalar.activation(vtok[:, 0:2].rearrange("p k h c -> p h k c"),
                                               src.rearrange("p (h k c) -> p h k c", h=NH, k=2), copy)
                elif m_ == M_SK:
                    ins = nc.scalar.activation(kT[:, 2, :], src[:, 0:S], copy)
                else:
                    c = GATE_ORDER[m_ - M_GATES]
                    ins = nc.scalar.activation(gates[:, 2 * c:2 * c + 2, :], pair, ACT.Tanh, scale=0.5)
                ins.then_inc(d_evac, 1)
                hi(l, n + RING)

            act_.wait_ge(rev_done, 1)
            nc.scalar.activation(rev, ps[0:HEADS, 0:2, 0:TW], copy).then_inc(rev_sb, 1)
            act_.wait_ge(rev_sb, 1)
            act_.dma_start(rev_rows.rearrange("(a h) u -> h a u", a=2), rev).then_inc(rev_small, 16)

            with act_.Fori(0, L) as l:
                for h in range(NH):
                    square_x(l, 0, h)
                hi(l, 0)
                for h in range(NH):
                    turned_hi(l, 0, h)
                    hi(l, 1 + h)
                ffn(l, 0, 0)
                boundary(l, 0, MIX0)

                for i in range(3):
                    hi(l, MIX0 + M_TM + i + RING)
                act_.wait_ge(w_used, used(l, MIX0 + M_TM + 3))
                nc.scalar.activation(vtok[:, 2], ps[:, 0:2 * NH:2, 0:P], copy)
                for part, (col, w) in enumerate(((P, QR), (0, KVR))):
                    for h in range(NH):
                        k = 4 + 2 * part + h
                        ins = nc.scalar.activation(latn[:, h, QR * part:QR * part + w],
                                                   bank(2 * h + part)[:, col:col + w], ACT.Square,
                                                   accum_out=ssq[:, k:k + 1])
                ins.then_inc(lat_sq, 1)
                hi(l, MIX0 + M_TM + 3 + RING)
                project_out(l, M_KC)
                act_.wait_ge(pe_tr, l + 1)
                nc.scalar.activation(peT[:], bank(4)[:, 0:CMP_LEN].rearrange("p (v l) -> p v l", v=2), copy
                                     ).then_inc(pe_ev, 1)
                project_out(l, M_NQ)
                act_.wait_ge(lat_tr, l + 1)
                for b in range(3):
                    n = 2 if b < 2 else 1
                    ins = nc.scalar.activation(lat_hi[:, 2 * b:2 * b + n, :],
                                               bank(b)[:, 0:n * S].rearrange("p (a t) -> p a t", a=n), copy)
                    ins.then_inc(lat_hi_ok, 1)
                act_.wait_ge(lat_n, l + 1)
                nc.scalar.activation(tm[:, :, ROPE:], tm[:, :, ROPE:], ACT.Tanh, scale=0.5).then_inc(ng_tanh, 1)
                project_out(l, M_NQ + 1)
                for i in range(2):
                    hi(l, MIX0 + M_QB + i + RING)
                act_.wait_ge(w_used, used(l, MIX0 + M_QB + 2))
                for h in range(NH):
                    for p in range(2):
                        ins = nc.scalar.activation(qtok[:, h, 4 * p:4 * p + 4, :],
                                                   bank(2 * h + p)[:, 0:4 * QK].rearrange("p (n c) -> p n c", n=4), copy)
                ins.then_inc(q_cp, 1)
                hi(l, MIX0 + M_QB + 2 + RING)
                act_.wait_ge(hid_done, l + 1)
                nc.scalar.activation(hid[:], bank(4)[:, 0:4 * NCMP].rearrange("p (v c) -> p v c", v=2),
                                     ACT.Gelu_apprx_tanh).then_inc(gelu_ok, 1)
                project_out(l, M_KK)
                hi(l, MIX0 + M_KVB + RING)
                act_.wait_ge(w_used, used(l, MIX0 + M_KVB + 1))
                for h in range(NH):
                    for p in range(2):
                        src = bank(2 * h + p).rearrange("p (n c) -> p n c", n=4)
                        nc.scalar.activation(ktok[:, h, 4 * p:4 * p + 4, 0:HD], src[:, :, 0:HD], copy)
                        ins = nc.scalar.activation(vmla[:, h, 4 * p:4 * p + 4, :], src[:, :, HD:], copy)
                ins.then_inc(kv_cp, 1)
                hi(l, MIX0 + M_KVB + 1 + RING)
                act_.wait_ge(cmp_done, l + 1)
                nc.scalar.activation(kcmp[:, 0:NCMP], bank(4)[:, 0:NCMP], copy)
                nc.scalar.activation(vcmp[0:NCMP], bank(5)[0:NCMP, 0:P].rearrange("p (g d) -> p g d", g=2), copy
                                     ).then_inc(cmp_ev, 1)
                project_out(l, M_VV)
                act_.wait_ge(q_tr, l + 1)
                for b in range(4):
                    ins = nc.scalar.activation(mqT[:, 2 * b:2 * b + 2, :],
                                               bank(b)[0:QK, :].rearrange("p (n t) -> p n t", n=2), copy)
                ins.then_inc(q_ev, 1)
                project_out(l, M_SQ)
                act_.wait_ge(k_tr, l + 1)
                for b in range(4):
                    ins = nc.scalar.activation(mkT[:, 2 * b:2 * b + 2, :],
                                               bank(b)[0:QK, :].rearrange("p (n t) -> p n t", n=2), copy)
                ins.then_inc(k_ev, 1)
                project_out(l, M_SQ + 1)

                for s in range(NSTEP):
                    if s < NU:
                        kind, g, q = UNITS[s]
                        scale = keys_of(s)[3]
                        act_.wait_ge(sm_bias, nth(l, NU, s))
                        for i in range(G):
                            ins = nc.scalar.activation(prob(s)[:, i, :], prob(s)[:, i, :], ACT.Exp,
                                                       bias=nb[:, s, i:i + 1], scale=scale,
                                                       accum_out=den[:, s, i:i + 1])
                        if kind == "swa":
                            k = s - (NU - 4)
                            ins = nc.scalar.activation(esk[:, k, :], dsk[:, k, :], ACT.Exp, scale=SC)
                        ins.then_inc(sm_exp, 1)
                    if 0 <= s - 1 < NU:
                        u = s - 1
                        n, tiles, _, _ = keys_of(u)
                        rows = min(n, P)
                        act_.wait_ge(pt_done, nth(l, NU, u))
                        if u >= 2:
                            act_.wait_ge(pv_done, nth(l, NU, u - 2))
                        nc.scalar.activation(pt_sb(u)[0:rows, 0:tiles],
                                             ps[0:rows, 2:2 + tiles, :].rearrange("p k (i t) -> p k i t", i=G), copy
                                             ).then_inc(pt_ev, 1)
                    if s in STEPS:
                        if STEPS[s] in DIDX:
                            project_out(l, STEPS[s])
                        else:
                            hi(l, MIX0 + STEPS[s] + RING)
                    u = s - 2
                    if u in OGROUP:
                        kind, g, q = UNITS[u]
                        t = {"win": 0, "swa": 4, "mla": 8}[kind] + 2 * g
                        act_.wait_ge(pv_done, nth(l, NU, u))
                        nc.scalar.activation(oT_hi[:, t:t + 2, q * P:q * P + P], o_ps(u), copy).then_inc(o_hi_ok, 1)

                for i in (4, 5):
                    hi(l, MIX0 + M_BR + i + RING)
                for half in range(2):
                    act_.wait_ge(mg_sum, nth(l, 4, 2 * half + 1))
                    nc.scalar.activation(mg_hi[:, 4 * half:4 * half + 4, :], gates[:, 16 + 4 * half:20 + 4 * half, :],
                                         copy, scale=0.5).then_inc(mg_hi_ok, 1)
                for i in range(2):
                    hi(l, MIX0 + M_OUT + i + RING)
                boundary(l, 1, FFN2_0)
                ffn(l, 1, FFN2_0)
                for h in range(NH):
                    square_y(l, 2, h, NC - 1)

        @block.vector
        def _(dve):
            def lo(l, n, dj=None):
                if n >= NC:
                    return
                dve.wait_ge(w_split_hi, nth(l, NC, n) if dj is None else nth(l, NC, n, dj * RING))
                w = slice(0, width(n))
                nc.vector.tensor_tensor(w_lo[n % RING][:, w], stage[n % RING][:, w],
                                        w_hi[n % RING][:, w].bitcast(F32), ALU.subtract).then_inc(w_split, 1)

            def scaled(l, sub, h):
                if h == 0:
                    dve.wait_ge(gpre_in, l * 48 + 16 * (sub + 1))
                dve.wait_ge(x_r, nth(l, 6, 2 * sub + h))
                nc.vector.scalar_tensor_tensor(work[:, h, :], x[:, h, :], rstd[:, h:h + 1], gpre[:],
                                               ALU.mult, ALU.mult).then_inc(xn_ok, 1)

            def turned_lo(l, sub, h):
                for b in range(2):
                    dve.wait_ge(hT_hi_ok, nth(l, 12, 4 * sub + 2 * h + b))
                    t = (slice(None), slice(4 * b, 4 * b + 4), slice(h * P, h * P + P))
                    nc.vector.tensor_tensor(hT_lo[t], bank(4 + 2 * h + b).rearrange("p (k t) -> p k t", k=4),
                                            hT_hi[t].bitcast(F32), ALU.subtract).then_inc(hT_ok, 1)

            def residual(l, sub, h):
                if h == 0:
                    dve.wait_ge(gpost_in, l * 48 + 16 * (sub + 1))
                dve.wait_ge(y_r, nth(l, 6, 2 * sub + h))
                nc.vector.scalar_tensor_tensor(work[:, h, :], ybanks(h), rstd[:, 2 + h:3 + h], gpost[:],
                                               ALU.mult, ALU.mult)
                dve.drain()
                nc.vector.tensor_tensor(x[:, h, :], x[:, h, :], work[:, h, :], ALU.add).then_inc(x_up, 1)

            def boundary(l, sub, c0):
                residual(l, sub, 0)
                lo(l, c0 + 1)
                scaled(l, sub + 1, 0)
                residual(l, sub, 1)
                turned_lo(l, sub + 1, 0)
                lo(l, c0 + 2)
                scaled(l, sub + 1, 1)
                turned_lo(l, sub + 1, 1)

            def ffn(l, f, c0):
                def step(j, dj=None):
                    lo(l, chunk_g(c0, j) + RING, dj)
                    dve.wait_ge(silu_ok, nth(l, 2 * FJ, f * FJ + j, dj))
                    dve.wait_ge(w_used, used(l, chunk_u(c0, j), dj))
                    if j:
                        dve.wait_ge(act_ok, nth(l, 2 * FJ, f * FJ + j - 1, dj))
                    nc.vector.tensor_tensor(act, bank(5).rearrange("p (a t) -> p a t", a=2), silu, ALU.mult
                                            ).then_inc(mul_ok, 1)
                    lo(l, chunk_u(c0, j) + RING, dj)
                    dve.wait_ge(act_hi_ok, nth(l, 2 * FJ, f * FJ + j, dj))
                    a_hi, a_lo = act_split(j)
                    nc.vector.tensor_tensor(a_lo, act, a_hi.bitcast(F32), ALU.subtract).then_inc(act_ok, 1)
                    if 0 < j < FJ - 1:
                        lo(l, chunk_d(c0, j - 1) + RING, dj)

                step(0)
                step(1)
                with dve.Fori(0, FFN_LOOP[1] - FFN_LOOP[0]) as dj:
                    step(FFN_LOOP[0], dj)
                step(FJ - 1)

            def rope(src, dst, heads):
                x1, x2 = src[:, :, :, 0:16], src[:, :, :, 16:32]
                cos, sin = (cs[:, i].unsqueeze(2).to_broadcast([P, NH, heads, 16]) for i in range(2))
                t = [rtmp[:, i, :, 0:heads, :] for i in range(4)]
                nc.vector.tensor_tensor(t[0], x1, cos, ALU.mult)
                nc.vector.tensor_tensor(t[1], x2, sin, ALU.mult)
                nc.vector.tensor_tensor(t[2], x1, sin, ALU.mult)
                nc.vector.tensor_tensor(t[3], x2, cos, ALU.mult)
                dve.drain()
                nc.vector.tensor_tensor(dst[:, :, :, 0:16], t[0], t[1], ALU.subtract)
                return nc.vector.tensor_tensor(dst[:, :, :, 16:32], t[2], t[3], ALU.add)

            def biased(l, u):
                kind, g, q = UNITS[u]
                n, _, _, scale = keys_of(u)
                off = 0 if q else P
                if u >= 2:
                    dve.wait_ge(pt_done, nth(l, NU, u - 2))
                wait_apart(dve, sc_done, nth(l, NU, u))
                for i in range(G):
                    if kind == "mla":
                        b = causal[:, off:off + n]
                    elif kind == "cmp":
                        first = CMP_LEN - 1 + off
                        b = bias[:, G * g + i, first:first + CMP_STRIDE * (n - 1) + 1:CMP_STRIDE]
                    else:
                        b = bias[:, (HEADS if kind == "swa" else 0) + G * g + i, off:off + n]
                    nc.vector.tensor_tensor_reduce(prob(u)[:, i, :], s_ps(u)[:, i, :], b, 1.0, -3.0e38,
                                                   ALU.add, ALU.max, mx[:, u, i:i + 1])
                dve.drain()
                if kind == "cmp":
                    ins = nc.vector.tensor_scalar(nb[:, u, :], mx[:, u, :], BAR, -scale, ALU.max, ALU.mult)
                elif kind == "swa":
                    k = u - (NU - 4)
                    sink = sk8[:, G * g:G * g + G]
                    nc.vector.tensor_tensor(mx[:, u, :], mx[:, u, :], sink, ALU.max)
                    dve.drain()
                    nc.vector.tensor_tensor(dsk[:, k, :], sink, mx[:, u, :], ALU.subtract)
                    ins = nc.vector.tensor_scalar(nb[:, u, :], mx[:, u, :], -scale, None, ALU.mult)
                else:
                    ins = nc.vector.tensor_scalar(nb[:, u, :], mx[:, u, :], -scale, None, ALU.mult)
                ins.then_inc(sm_bias, 1)

            def normalised(l, u):
                kind, g, q = UNITS[u]
                n = keys_of(u)[0]
                dve.wait_ge(sm_exp, nth(l, NU, u))
                if kind == "cmp":
                    nc.vector.tensor_scalar(den[:, u, :], den[:, u, :], 1e-30, None, ALU.max)
                    dve.drain()
                elif kind == "swa":
                    nc.vector.tensor_tensor(den[:, u, :], den[:, u, :], esk[:, u - (NU - 4), :], ALU.add)
                    dve.drain()
                nc.vector.reciprocal(fac[:, u, :], den[:, u, :])
                dve.drain()
                if kind in ("cmp", "sel", "win"):
                    first = ROPE + 3 * G * g + ("cmp", "sel", "win").index(kind)
                    nc.vector.tensor_tensor(fac[:, u, :], fac[:, u, :], tm[:, q, first:first + 3 * (G - 1) + 1:3],
                                            ALU.mult)
                    dve.drain()
                nc.vector.tensor_tensor(prob(u), prob(u), fac[:, u, :].unsqueeze(2).to_broadcast([P, G, n]),
                                        ALU.mult).then_inc(sm_norm, 1)

            def merged(l, b):
                n, half = BRANCHES[b]
                for p in range(2):
                    t = 4 * half + 2 * p
                    src = bank(6 + p).rearrange("p (a t) -> p a t", a=2)
                    gate, total = gates[:, 8 * n + t:8 * n + t + 2, :], gates[:, 16 + t:18 + t, :]
                    if b == 0:
                        dve.wait_ge(d_evac, nth(l, ND, ND - 1))
                    if p == 0:
                        dve.wait_ge(b_half, nth(l, 6, b))
                    else:
                        dve.wait_ge(w_used, used(l, MIX0 + M_BR + b))
                    nc.vector.scalar_tensor_tensor(gate, gate, 1.0, src, ALU.add, ALU.mult).then_inc(b_ev, 1)
                    if b >= 2:
                        dve.drain()
                        ins = nc.vector.tensor_tensor(total, total, gate, ALU.add)
                        if b >= 4:
                            ins.then_inc(mg_sum, 1)
                lo(l, MIX0 + M_BR + b + RING)

            nc.vector.memset(table8[NB:NB + 1, :], 8 * NEG)
            dve.wait_ge(table_in, 32)
            nc.vector.tensor_scalar(table8[0:NB, :], table8[0:NB, :], 8.0, None, ALU.mult).then_inc(table_ok, 1)
            dve.sem_inc(w_split, RING)
            for h in range(NH):
                dve.wait_ge(x_in[h], 16)
                dve.sem_inc(x_up, 1)

            with dve.Fori(0, L) as l:
                for h in range(NH):
                    scaled(l, 0, h)
                lo(l, 0)
                for h in range(NH):
                    turned_lo(l, 0, h)
                    lo(l, 1 + h)
                ffn(l, 0, 0)
                boundary(l, 0, MIX0)

                for i in range(3):
                    lo(l, MIX0 + M_TM + i + RING)
                dve.wait_ge(mix_in, l * MIX_LOADS + MIX_LOADS)
                dve.wait_ge(lat_r, l + 1)
                for part, (col, w) in enumerate(((P, QR), (0, KVR))):
                    for h in range(NH):
                        c = slice(QR * part, QR * part + w)
                        k = 4 + 2 * part + h
                        nc.vector.scalar_tensor_tensor(latn[:, h, c], bank(2 * h + part)[:, col:col + w],
                                                       rstd[:, k:k + 1], gl[:, c], ALU.mult, ALU.mult)
                nc.vector.tensor_copy(tm[:], ps[:, 1:2 * NH:2, KVR:TM2]).then_inc(lat_n, 1)
                lo(l, MIX0 + M_TM + 3 + RING)
                nc.vector.tensor_scalar(sk8[:], sk8[:], 1.0 / SC, None, ALU.mult)
                dve.wait_ge(pe_ev, l + 1)
                dve.wait_ge(d_evac, nth(l, ND, DIDX[M_KC]))
                half = CMP_STRIDE // 2
                for v in range(2):
                    for part in range(2):
                        at = CMP_STRIDE * part
                        tok = kv2[:, v, :, at:at + CMP_STRIDE * NCMP].rearrange(
                            "p g (c l two) -> p l g c two", l=half, two=2)[:, :, :, :, 0]
                        pos = peT[:, v, half * part:half * part + half].unsqueeze(2).unsqueeze(3).to_broadcast(
                            [P, half, 2, NCMP])
                        ins = nc.vector.tensor_tensor(blk[v][:, half * part:half * part + half], tok, pos, ALU.add)
                ins.then_inc(blk_ok, 1)
                lo(l, MIX0 + M_KC + RING)
                for b in range(3):
                    n = 2 if b < 2 else 1
                    dve.wait_ge(lat_hi_ok, nth(l, 3, b))
                    ins = nc.vector.tensor_tensor(lat_lo[:, 2 * b:2 * b + n, :],
                                                  bank(b)[:, 0:n * S].rearrange("p (a t) -> p a t", a=n),
                                                  lat_hi[:, 2 * b:2 * b + n, :].bitcast(F32), ALU.subtract)
                ins.then_inc(lat_ok, 1)
                lo(l, MIX0 + M_NQ + RING)
                dve.wait_ge(ng_tanh, l + 1)
                nc.vector.tensor_scalar(tm[:, :, ROPE:], tm[:, :, ROPE:], 0.5, 0.5, ALU.mult, ALU.add)
                lo(l, MIX0 + M_NQ + 1 + RING)
                rope(tm[:, :, 0:ROPE].unsqueeze(2), krot[:].unsqueeze(2), 1)
                dve.drain()
                for i in range(2):
                    lo(l, MIX0 + M_QB + i + RING)
                dve.wait_ge(q_cp, l + 1)
                rope(qtok[:, :, :, HD:], qtok[:, :, :, HD:], HEADS).then_inc(q_ok, 1)
                lo(l, MIX0 + M_QB + 2 + RING)
                dve.wait_ge(hid_done, l + 1)
                for h in range(NH):
                    ins = nc.vector.tensor_copy(ktok[:, h, :, HD:], krot[:, h:h + 1, :].to_broadcast([P, HEADS, ROPE]))
                ins.then_inc(k_ok, 1)
                for m_ in (M_KK, M_KVB, M_KVB + 1, M_VV, M_SQ, M_SQ + 1):
                    lo(l, MIX0 + m_ + RING)

                for s in range(NSTEP):
                    if s < NU:
                        biased(l, s)
                        normalised(l, s)
                    u = s - 2
                    if s in STEPS:
                        m_ = STEPS[s]
                        if m_ in DIDX:
                            lo(l, MIX0 + m_ + RING)
                        else:
                            merged(l, m_ - M_BR)
                    if u in OGROUP:
                        kind, g, q = UNITS[u]
                        t = {"win": 0, "swa": 4, "mla": 8}[kind] + 2 * g
                        dst = (slice(None), slice(t, t + 2), slice(q * P, q * P + P))
                        dve.wait_ge(o_hi_ok, nth(l, NOG, OGROUP.index(u)))
                        nc.vector.tensor_tensor(oT_lo[dst], o_ps(u), oT_hi[dst].bitcast(F32), ALU.subtract
                                                ).then_inc(o_ok, 1)
                for b in (4, 5):
                    merged(l, b)
                for half in range(2):
                    dve.wait_ge(mg_hi_ok, nth(l, 2, half))
                    t = slice(4 * half, 4 * half + 4)
                    nc.vector.scalar_tensor_tensor(mg_lo[:, t, :], gates[:, 16 + 4 * half:20 + 4 * half, :], 0.5,
                                                   mg_hi[:, t, :].bitcast(F32), ALU.mult, ALU.subtract
                                                   ).then_inc(mg_ok, 1)
                for i in range(2):
                    lo(l, MIX0 + M_OUT + i + RING)
                boundary(l, 1, FFN2_0)
                ffn(l, 1, FFN2_0)
                for h in range(NH):
                    residual(l, 2, h)

        @block.tensor
        def _(pe):
            def mm3(dst, a, b, start, stop):
                (a_hi, a_lo), (b_hi, b_lo) = a, b
                nc.tensor.matmul(dst, a_hi, b_hi, start=start, stop=False)
                nc.tensor.matmul(dst, a_hi, b_lo, start=False, stop=False)
                return nc.tensor.matmul(dst, a_lo, b_hi, start=False, stop=stop)

            def both(hi_, lo_, *at):
                return hi_[at], lo_[at]

            def ring(n, lo_, hi_):
                at = (slice(None), slice(lo_, hi_))
                return both(w_hi[n % RING], w_lo[n % RING], *at)

            def tokens(h):
                return slice(h * P, h * P + P)

            ALL = slice(None)

            def turn(dst, src):
                rows = src.shape[0]
                return nc.tensor.transpose(dst, src, ident[0:rows, 0:rows])

            def turned(l, sub, h):
                pe.wait_ge(xn_ok, nth(l, 6, 2 * sub + h))
                for k in range(KD):
                    ins = turn(bank(4 + 2 * h + k // 4)[:, (k % 4) * P:(k % 4) * P + P],
                               work[:, h, k * P:k * P + P])
                ins.then_inc(tr_done, 1)

            def norm_in(l, sub):
                for h in range(NH):
                    turned(l, sub, h)
                pe.wait_ge(hT_ok, nth(l, 12, 4 * sub + 3))

            def two_tiles(n, dst):
                for c in range(2):
                    for k in range(KD):
                        a = ring(n, k * FW + c * P, k * FW + c * P + P)
                        ins = mm3(dst[:, c * S:c * S + S], a, both(hT_hi, hT_lo, ALL, k, ALL), k == 0, k == KD - 1)
                return ins

            def rows_half(n, lhs, h, first, last):
                for kt in range(2):
                    for c in range(2):
                        ins = mm3(bank(2 * h + c), lhs(kt, h), ring(n, kt * D + c * 512, kt * D + c * 512 + 512),
                                  first and kt == 0, last and kt == 1)
                return ins

            def rows_out(n, lhs, first):
                for h in range(NH):
                    ins = rows_half(n, lhs, h, first, False)
                ins.then_inc(w_used, 1)

            def rows_last(ready, chunks):
                for h in range(NH):
                    for i, (n, lhs) in enumerate(chunks):
                        if h == 0:
                            ready(i)
                        ins = rows_half(n, lhs, h, False, i == 1)
                        if h == 1:
                            ins.then_inc(w_used, 1)
                        elif i == 1:
                            ins.then_inc(y_done, 1)

            def ffn(l, f, c0):
                def lhs(j):
                    return lambda kt, h: both(*act_split(j), ALL, kt, tokens(h))

                def down_ready(j, dj=None):
                    pe.wait_ge(w_split, split(l, chunk_d(c0, j), dj))
                    pe.wait_ge(act_ok, nth(l, 2 * FJ, f * FJ + j, dj))

                def step(j, dj=None):
                    n = chunk_g(c0, j)
                    pe.wait_ge(w_split, split(l, n, dj))
                    if j:
                        pe.wait_ge(silu_ok, nth(l, 2 * FJ, f * FJ + j - 1, dj))
                    two_tiles(n, bank(4)).then_inc(w_used, 1)
                    n = chunk_u(c0, j)
                    pe.wait_ge(w_split, split(l, n, dj))
                    if j:
                        pe.wait_ge(mul_ok, nth(l, 2 * FJ, f * FJ + j - 1, dj))
                    two_tiles(n, bank(5)).then_inc(w_used, 1)
                    if 0 < j < FJ - 1:
                        down_ready(j - 1, dj)
                        rows_out(chunk_d(c0, j - 1), lhs(j - 1), j == 1)

                step(0)
                step(1)
                with pe.Fori(0, FFN_LOOP[1] - FFN_LOOP[0]) as dj:
                    step(FFN_LOOP[0], dj)
                step(FJ - 1)
                rows_last(lambda i: down_ready(FJ - 2 + i), [(chunk_d(c0, j), lhs(j)) for j in (FJ - 2, FJ - 1)])

            def project(l, m_):
                n, i = MIX0 + m_, DIDX[m_]
                dst = bank(6 + i % 2)
                pe.wait_ge(w_split, split(l, n))
                if i >= 2:
                    pe.wait_ge(d_evac, nth(l, ND, i - 2))
                if m_ == M_SK:
                    for k in range(KD):
                        ins = mm3(dst[:, 0:S], ring(n, k * P, k * P + P), both(hT_hi, hT_lo, ALL, k, ALL),
                                  k == 0, k == KD - 1)
                elif m_ == M_VV:
                    for h in range(NH):
                        for k in range(KD):
                            ins = mm3(dst[:, h * FW:h * FW + FW], both(hT_hi, hT_lo, ALL, k, tokens(h)),
                                      ring(n, k * FW, k * FW + FW), k == 0, k == KD - 1)
                else:
                    ins = two_tiles(n, dst)
                ins.then_inc(w_used, 1)

            def scores(l, u):
                kind, g, q = UNITS[u]
                n, _, _, _ = keys_of(u)
                if u == 0:
                    pe.wait_ge(k_ev, l + 1)
                else:
                    pe.wait_ge(sm_bias, nth(l, NU, u - 1))
                if kind == "cmp":
                    pe.wait_ge(cmp_ev, l + 1)
                if kind in ("sel", "win"):
                    pe.wait_ge(d_evac, nth(l, ND, DIDX[M_VV]))
                if kind == "swa":
                    pe.wait_ge(d_evac, nth(l, ND, DIDX[M_SK]))
                rows = slice(HD * g, HD * g + HD)
                for i in range(G):
                    if kind == "mla":
                        a, b = mqT[:, G * g + i, tokens(q)], mkT[:, G * g + i, 0:n]
                    else:
                        a = qsT[rows, (4 if kind == "swa" else 0) + i, tokens(q)]
                        b = (kcmp[rows, 0:n] if kind == "cmp"
                             else kT[rows, ("sel", "win", "swa").index(kind), 0:n])
                    ins = nc.tensor.matmul(s_ps(u)[:, i, :], a, b, start=True, stop=True)
                ins.then_inc(sc_done, 1)

            def turn_p(l, u):
                n, tiles, _, _ = keys_of(u)
                rows = min(n, P)
                pe.wait_ge(sm_norm, nth(l, NU, u))
                if u >= 1:
                    pe.wait_ge(pt_ev, nth(l, NU, u - 1))
                for kt in range(tiles):
                    for i in range(G):
                        ins = turn(bank(2 + kt)[0:rows, i * P:i * P + P], prob(u)[:, i, kt * P:kt * P + rows])
                ins.then_inc(pt_done, 1)

            def values(l, u):
                kind, g, q = UNITS[u]
                n, tiles, _, _ = keys_of(u)
                rows = min(n, P)
                og = group_of(u)
                first = kind in ("cmp", "mla", "swa")
                last = kind in ("win", "mla", "swa")
                pe.wait_ge(pt_ev, nth(l, NU, u))
                if first and og >= 2:
                    pe.wait_ge(o_ok, nth(l, NOG, og - 2))
                for odd in range(2):
                    part = slice(HD * odd, HD * odd + HD)
                    if kind == "mla":
                        for pair in range(2):
                            i = 2 * pair + odd
                            for kt in range(tiles):
                                ins = nc.tensor.matmul(o_ps(u)[part, pair, :], vmla[:, kt, G * g + i, :],
                                                       pt_sb(u)[:, kt, i, :], start=kt == 0, stop=kt == tiles - 1)
                        continue
                    for kt in range(tiles):
                        v = (vcmp[0:rows, g, :] if kind == "cmp" else
                             vtok[:, ("sel", "win", "swa").index(kind), kt, HD * g:HD * g + HD])
                        ins = nc.tensor.matmul(o_ps(u)[part], v, pt_sb(u)[0:rows, kt, odd:G:2, :],
                                               start=first and kt == 0, stop=last and kt == tiles - 1)
                ins.then_inc(pv_done, 1)

            def branch(l, b):
                n, (br, half) = MIX0 + M_BR + b, BRANCHES[b]
                base = 4 * br
                pe.wait_ge(w_split, split(l, n))
                if b in (0, 2, 4):
                    done = max(i for i, u in enumerate(OGROUP) if UNITS[u][0] == ("win", "swa", "mla")[br])
                    pe.wait_ge(o_ok, nth(l, NOG, done))
                for p in range(2):
                    if b == 0:
                        pe.wait_ge(d_evac, nth(l, ND, ND - 2 + p))
                    else:
                        pe.wait_ge(b_ev, nth(l, 12, 2 * (b - 1) + p))
                    for c in range(2):
                        for k in range(4):
                            at = k * 512 + (2 * p + c) * P
                            ins = mm3(bank(6 + p)[:, c * S:c * S + S], ring(n, at, at + P),
                                      both(oT_hi, oT_lo, ALL, base + k, ALL), k == 0, k == 3)
                    ins.then_inc(b_half if p == 0 else w_used, 1)

            pe.sem_inc(w_used, RING)
            pe.wait_ge(table_ok, 1)
            for a in range(2):
                ins = nc.tensor.matmul(bank(a)[0:HEADS, 0:TW], table8[:, HEADS * a:HEADS * a + HEADS], onehot[:, a, :],
                                       start=True, stop=True)
            ins.then_inc(rev_done, 1)
            pe.wait_ge(const_in, 48)
            pe.wait_ge(rev_sb, 1)

            with pe.Fori(0, L) as l:
                norm_in(l, 0)
                ffn(l, 0, 0)

                def token_major(i, h):
                    n = MIX0 + M_TM + i
                    for kt in range(2):
                        k = 2 * i + kt
                        a = both(hT_hi, hT_lo, ALL, k, tokens(h))
                        for dst, lo_, hi_ in ((bank(2 * h), 0, TM1), (bank(2 * h + 1), TM1, TM)):
                            ins = mm3(dst[:, 0:hi_ - lo_], a, ring(n, kt * TM + lo_, kt * TM + hi_),
                                      k == 0, k == KD - 1)
                    return ins

                turned(l, 1, 0)
                pe.wait_ge(hT_ok, nth(l, 12, 4 + 1))
                for i in range(3):
                    pe.wait_ge(w_split, split(l, MIX0 + M_TM + i))
                    token_major(i, 0)
                    if i == 0:
                        turned(l, 1, 1)
                pe.wait_ge(hT_ok, nth(l, 12, 4 + 3))
                for i in range(3):
                    token_major(i, 1).then_inc(w_used, 1)
                pe.wait_ge(w_split, split(l, MIX0 + M_TM + 3))
                token_major(3, 0)
                token_major(3, 1).then_inc(w_used, 1)
                project(l, M_KC)
                wait_apart(pe, mix_in, l * MIX_LOADS + MIX_LOADS)
                for v in range(2):
                    ins = turn(bank(4)[:, v * CMP_LEN // 2:(v + 1) * CMP_LEN // 2], pe_rows[:, v, :])
                ins.then_inc(pe_tr, 1)
                project(l, M_NQ)
                pe.wait_ge(lat_n, l + 1)
                for t in range(LAT // P):
                    for h in range(NH):
                        ins = turn(bank(t // 2)[:, (t % 2) * S + h * P:(t % 2) * S + h * P + P],
                                   latn[:, h, t * P:t * P + P])
                ins.then_inc(lat_tr, 1)
                project(l, M_NQ + 1)
                pe.wait_ge(lat_ok, l + 1)
                for i in range(QR // P):
                    n = MIX0 + M_QB + i
                    pe.wait_ge(w_split, split(l, n))
                    for h in range(NH):
                        for p in range(2):
                            ins = mm3(bank(2 * h + p)[:, 0:4 * QK], both(lat_hi, lat_lo, ALL, i, tokens(h)),
                                      ring(n, p * 4 * QK, (p + 1) * 4 * QK), i == 0, i == QR // P - 1)
                    ins.then_inc(w_used, 1)
                pe.wait_ge(blk_ok, l + 1)
                for v in range(2):
                    for i in range(CMP_LEN // 2):
                        ins = nc.tensor.matmul(bank(4)[:, 2 * NCMP * v:2 * NCMP * (v + 1)], w1[:, v, i, :],
                                               blk[v][:, i].rearrange("p g c -> p (g c)"),
                                               start=i == 0, stop=i == CMP_LEN // 2 - 1)
                ins.then_inc(hid_done, 1)
                project(l, M_KK)
                pe.wait_ge(q_cp, l + 1)
                for i in range(KVR // P):
                    n = MIX0 + M_KVB + i
                    pe.wait_ge(w_split, split(l, n))
                    for h in range(NH):
                        for p in range(2):
                            ins = mm3(bank(2 * h + p), both(lat_hi, lat_lo, ALL, QR // P + i, tokens(h)),
                                      ring(n, p * 512, (p + 1) * 512), i == 0, i == KVR // P - 1)
                    ins.then_inc(w_used, 1)
                pe.wait_ge(gelu_ok, l + 1)
                for g in range(2):
                    nc.tensor.matmul(bank(4)[HD * g:HD * g + HD, 0:NCMP], w2[:, 0, :],
                                     hid[:, 0, NCMP * g:NCMP * g + NCMP], start=True, stop=True)
                for g in range(2):
                    ins = nc.tensor.matmul(bank(5)[0:NCMP, HD * g:HD * g + HD], hid[:, 1, NCMP * g:NCMP * g + NCMP],
                                           w2[:, 1, :], start=True, stop=True)
                ins.then_inc(cmp_done, 1)
                project(l, M_VV)
                pe.wait_ge(q_ok, l + 1)
                pe.wait_ge(kv_cp, l + 1)
                for n in range(HEADS):
                    for h in range(NH):
                        ins = turn(bank(n // 2)[0:QK, (n % 2) * S + h * P:(n % 2) * S + h * P + P], qtok[:, h, n, :])
                ins.then_inc(q_tr, 1)
                project(l, M_SQ)
                pe.wait_ge(k_ok, l + 1)
                pe.wait_ge(q_ev, l + 1)
                for n in range(HEADS):
                    for h in range(NH):
                        ins = turn(bank(n // 2)[0:QK, (n % 2) * S + h * P:(n % 2) * S + h * P + P], ktok[:, h, n, :])
                ins.then_inc(k_tr, 1)
                project(l, M_SQ + 1)
                pe.wait_ge(cmp_ev, l + 1)

                for s in range(NSTEP):
                    if s < NU:
                        scores(l, s)
                    if s in STEPS:
                        if STEPS[s] in DIDX:
                            project(l, STEPS[s])
                        else:
                            branch(l, STEPS[s] - M_BR)
                    if 0 <= s - 1 < NU:
                        turn_p(l, s - 1)
                    if 0 <= s - 2 < NU:
                        values(l, s - 2)
                branch(l, 4)
                branch(l, 5)

                def out_ready(i):
                    pe.wait_ge(w_split, split(l, MIX0 + M_OUT + i))
                    pe.wait_ge(mg_ok, nth(l, 2, i // 2))

                def merged(i):
                    return lambda kt, h: both(mg_hi, mg_lo, ALL, 2 * i + kt, tokens(h))

                for i in range(2):
                    out_ready(i)
                    rows_out(MIX0 + M_OUT + i, merged(i), i == 0)
                rows_last(lambda i: out_ready(2 + i), [(MIX0 + M_OUT + i, merged(i)) for i in (2, 3)])
                norm_in(l, 2)
                ffn(l, 1, FFN2_0)


_INS = ["x", "rel_bias_table", "ffn1_norm_pre", "ffn1_w_gu", "ffn1_w_down", "ffn1_norm_post",
        "mix_norm_pre", "w_in", "nsa_pe_k", "nsa_w1_k", "nsa_w2_k", "nsa_pe_v", "nsa_w1_v", "nsa_w2_v",
        "swa_sinks", "mla_q_norm", "mla_w_qb", "mla_kv_norm", "mla_w_kvb", "w_branch", "w_out",
        "mix_norm_post", "ffn2_norm_pre", "ffn2_w_gu", "ffn2_w_down", "ffn2_norm_post"]


def shape_constants():
    dist = np.arange(S, dtype=np.int32)
    ratio = np.log(np.maximum(dist, 1).astype(np.float32) / np.float32(16)) / np.float32(np.log(64.0))
    far = np.minimum(16 + (ratio * np.float32(16)).astype(np.int32), NB - 1)
    bucket = np.where(dist < 16, dist, far)
    onehot = np.zeros((NB + 1, 2, TW), np.float32)
    for u in range(TW):
        d = S - 1 - u
        for kind, window in enumerate((S, P)):
            onehot[bucket[d] if 0 <= d < window else NB, kind, u] = 1.0
    p, j = np.arange(P)[:, None], np.arange(S)[None, :]
    causal = np.where(P + p - j >= 0, 0.0, NEG).astype(np.float32)
    inv = (10000.0 ** (-np.arange(16, dtype=np.float32) / 16)).astype(np.float32)
    ang = np.arange(S, dtype=np.float32)[:, None] * inv[None, :]
    rope = np.stack([np.cos(ang), np.sin(ang)]).astype(np.float32).reshape(2, NH, P, 16).transpose(2, 0, 1, 3)
    return {"c_onehot": onehot, "c_causal": causal, "c_rope": rope, "c_ident": np.eye(P, dtype=np.float32)}


def kernel(**inputs):
    import concourse.bacc as _bacc
    from concourse import mybir as _mybir
    from concourse.bass_utils import run_bass_kernel_spmd as _run

    nc = _bacc.Bacc("TRN2", target_bir_lowering=False, num_devices=1)
    arrays, aps = {}, {}
    for name, a in list((n, inputs[n]) for n in _INS) + list(shape_constants().items()):
        a = np.ascontiguousarray(a)
        arrays[f"in_{name}_dram"] = a
        aps[name] = nc.dram_tensor(f"in_{name}_dram", a.shape, _mybir.dt.from_np(a.dtype), kind="ExternalInput").ap()
    out = nc.dram_tensor("out_0_dram", (1, S, D), _mybir.dt.float32, kind="ExternalOutput").ap()
    decoder_kernel(nc, aps, out)
    r = _run(nc, [arrays], core_ids=[0])
    return r.results[0]["out_0_dram"]
```

```python
from contextlib import ExitStack

import numpy as np

import concourse.bass as bass
from concourse import mybir

ALU = mybir.AluOpType
ACT = mybir.ActivationFunctionType
F32 = mybir.dt.float32
F32R = mybir.dt.float32r

P = 128
S = 256
D = 1024
L = 2
NH = S // P
KD = D // P
FF = 2816
FW = 256
FJ = FF // FW
EPS = 1e-6
HD = 64
G = 4
HEADS = 8
NCMP = 15
CMP_LEN, CMP_STRIDE, CMP_HID = 32, 16, 128
QR, KVR, ROPE = 384, 256, 32
QK = HD + ROPE
NB = 32
TW = 384
NEG = -1e30
BAR = -1e29
SC = HD ** -0.5
SC_MLA = QK ** -0.5

C_NQ, C_KC, C_KS, C_KW, C_GATE, C_SQ, C_SK, C_SV = 0, 512, 768, 1024, 1280, 1304, 1816, 1944
C_MG = 2744
LAT = QR + KVR
TM1 = P + QR
TM2 = KVR + ROPE + 24
TM = TM1 + TM2

RING = 3
CH = 2048
FC = 3 * FJ
MIX0 = FC
M_TM, M_KC, M_NQ, M_QB, M_KK, M_KVB, M_VV, M_SQ, M_SK, M_OUT = (
    0, 4, 5, 7, 10, 11, 13, 14, 16, 35)
MC = 39
FFN2_0 = FC + MC
NC = FC + MC + FC
assert NC % RING == 0
BRANCHES = [(2, 0), (2, 1), (0, 0), (0, 1), (1, 0), (1, 1)]

FILL = {0: "sk", 1: ("gate", 8), 2: ("gate", 9), 4: ("gate", 0), 6: ("gate", 10), 7: ("gate", 11),
        8: ("branch", 0), 10: ("branch", 1), 11: ("gate", 1), 12: ("gate", 2), 14: ("gate", 3), 16: ("gate", 4),
        18: ("gate", 5), 19: ("branch", 2), 20: ("branch", 3), 21: ("gate", 6), 22: ("gate", 7)}
STEPS = {s: M_SK + i for i, s in enumerate(sorted(FILL))}
GATE_OF = {STEPS[s]: f[1] for s, f in FILL.items() if f[0] == "gate"}
BRANCH_OF = {STEPS[s]: f[1] for s, f in FILL.items() if f[0] == "branch"}
BRANCH_OF.update({M_OUT - 2: 4, M_OUT - 1: 5})
BRANCH_AT = {b: m for m, b in BRANCH_OF.items()}

DMAS = {**{MIX0 + m: 2 for m in (*range(M_TM, M_TM + 4), M_KK, M_VV)}, **{MIX0 + m: 4 for m in (M_NQ, M_NQ + 1, M_SQ, M_SQ + 1)}}
ARRIVED = [16 * sum(DMAS.get(k, 1) for k in range(n % RING, n + 1, RING)) for n in range(NC)]
ARRIVED_LAYER = [ARRIVED[NC - RING + i] for i in range(RING)]

DENSE = [M_KC, M_NQ, M_NQ + 1, M_KK, M_VV, M_SQ, M_SQ + 1, M_SK] + sorted(GATE_OF)
DIDX = {m: i for i, m in enumerate(DENSE)}
ND = len(DENSE)

UNITS = [("mla", g, q) for g in range(2) for q in range(2)]
UNITS += [(k, g, q) for g in range(2) for q in range(2) for k in ("cmp", "sel", "win")]
UNITS += [("swa", g, q) for g in range(2) for q in range(2)]
NU = len(UNITS)
OGROUP = [u for u, (k, _, _) in enumerate(UNITS) if k in ("mla", "win", "swa")]
NOG = len(OGROUP)
NSTEP = NU + 3


def width(n):
    m = n - MIX0
    if M_TM <= m < M_TM + 4:
        return 2 * TM
    if M_QB <= m < M_QB + QR // P:
        return HEADS * QK
    if M_KVB <= m < M_KVB + KVR // P:
        return HEADS * 2 * HD
    if m == M_SK:
        return KD * P
    return CH


def group_of(u):
    return next(i for i, last in enumerate(OGROUP) if last >= u)


def keys_of(u):
    kind, _, q = UNITS[u]
    if kind == "cmp":
        return (NCMP if q else 7), 1, 16, SC
    return (S if q else P), (2 if q else 1), (S if q else P), (SC_MLA if kind == "mla" else SC)


def decoder_kernel(nc, A, out):
    ctx = ExitStack()
    with ctx:
        def sb(name, shape, dt=F32):
            return ctx.enter_context(nc.sbuf_tensor(name, shape, dt))

        def sem(name):
            return ctx.enter_context(nc.semaphore(name))

        x = sb("x", [P, NH, D])
        work = sb("work", [P, NH, D])
        hT_hi = sb("hT_hi", [P, KD, S], F32R)
        hT_lo = sb("hT_lo", [P, KD, S], F32R)
        stage = [sb(f"stage{i}", [P, CH]) for i in range(RING)]
        w_hi = [sb(f"w_hi{i}", [P, CH], F32R) for i in range(RING)]
        w_lo = [sb(f"w_lo{i}", [P, CH], F32R) for i in range(RING)]
        bias = sb("bias", [P, 2 * HEADS, S])
        Z = sb("Z", [P, 8192])
        oT_hi = sb("oT_hi", [P, 12, S], F32R)
        oT_lo = sb("oT_lo", [P, 12, S], F32R)
        gpre = sb("gpre", [P, D])
        gpost = sb("gpost", [P, D])
        qsT = sb("qsT", [P, 8, S])
        kT = sb("kT", [P, 3, S])
        vtok = sb("vtok", [P, 3, NH, P])
        ident = sb("ident", [P, P])
        causal = sb("causal", [P, S])
        cs = sb("cs", [P, 2, NH, 16])
        gl = sb("gl", [P, LAT])
        w2 = sb("w2", [P, 2, HD])
        pe_rows = sb("pe_rows", [CMP_LEN // 2, 2, P])
        peT = sb("peT", [P, 2, CMP_LEN // 2])
        sk8 = sb("sk8", [P, HEADS])
        tm = sb("tm", [P, NH, ROPE + 24])
        krot = sb("krot", [P, NH, ROPE])
        kcmp = sb("kcmp", [P, 16])
        vcmp = sb("vcmp", [16, 2, HD])
        hid = sb("hid", [P, 2, 2 * NCMP])
        table8 = sb("table8", [NB + 1, 2 * HEADS])
        ms = sb("ms", [P, 8])
        rstd = sb("rstd", [P, 8])
        mhalf = sb("mhalf", [P, 4])
        mx = sb("mx", [P, NU, G])
        nb = sb("nb", [P, NU, G])
        den = sb("den", [P, NU, G])
        fac = sb("fac", [P, NU, G])
        dsk = sb("dsk", [P, 4, G])
        esk = sb("esk", [P, 4, G])

        silu = qsT[:, 0:2, :]
        act = qsT[:, 2:4, :]

        def act_split(j):
            t = 2 if j == FJ - 1 else 0
            return oT_hi[:, t:t + 2, :], oT_lo[:, t:t + 2, :]

        workf = work[:].rearrange("p a b -> p (a b)")
        latn = workf[:, 0:2 * LAT].rearrange("p (h c) -> p h c", h=NH)
        kv2 = qsT[:, 4:8, :].rearrange("p (v g) t -> p v g t", v=2)
        unused = Z[:, 4096:6144].rearrange("p (h c) -> p h c", h=NH)
        blk = [b.rearrange("p (l g c) -> p l g c", g=2, c=NCMP) for b in (workf[:, 1280:1760], Z[:, 7680:8160])]
        ktok = workf[:, 0:NH * HEADS * QK].rearrange("p (h n c) -> p h n c", h=NH, c=QK)
        w1 = Z[:, 0:4096].rearrange("p (v l n) -> p v l n", v=2, l=CMP_LEN // 2)
        mqT = Z[0:QK, 0:2048].rearrange("p (n t) -> p n t", n=HEADS)
        mkT = Z[0:QK, 2048:4096].rearrange("p (n t) -> p n t", n=HEADS)
        rtmp = Z[:, 4096:5120].rearrange("p (i h n c) -> p i h n c", i=4, h=NH, n=HEADS)
        vmla = Z[:, 5120:6144].rearrange("p (h n c) -> p h n c", h=NH, c=HD)
        qtok = Z[:, 6144:7680].rearrange("p (h n c) -> p h n c", h=NH, c=QK)
        gates = Z[:, 0:6144].rearrange("p (i t) -> p i t", t=S)
        rev = Z[0:HEADS, 0:2 * TW].rearrange("p (a u) -> p a u", a=2)
        onehot = qsT[:].rearrange("p a b -> p (a b)")[0:NB + 1, 0:2 * TW].rearrange("p (a u) -> p a u", a=2)
        lat_hi, lat_lo = oT_hi[:, 0:5, :], oT_lo[:, 0:5, :]
        mg_hi, mg_lo = hT_hi, hT_lo

        def pt_sb(u):
            return Z[:, 6144 + 1024 * (u % 2):7168 + 1024 * (u % 2)].rearrange("p (k i t) -> p k i t", k=2, i=G)

        def prob(u):
            n, _, _, _ = keys_of(u)
            return work[:, u % 2, :].rearrange("p (i j) -> p i j", i=G)[:, :, 0:n]

        ps = ctx.enter_context(nc.psum_tensor("ps", [P, 8, 512], F32))

        def bank(i):
            return ps[:, i, :]

        def ybanks(h):
            return ps[:, 2 * h:2 * h + 2, :].rearrange("p a b -> p (a b)")

        def s_ps(u):
            n, _, step, _ = keys_of(u)
            return ps[:, 0:2, :].rearrange("p a b -> p (a b)")[:, 0:G * step].rearrange(
                "p (i j) -> p i j", i=G)[:, :, 0:n]

        actT = bank(6).rearrange("p (a t) -> p a t", a=2)

        def o_ps(u):
            return bank(4 + group_of(u) % 2)[:, 0:S].rearrange("p (a t) -> p a t", a=2)

        x_in = [sem(f"x_in{h}") for h in range(NH)]
        const_in = sem("const_in")
        tables_in = sem("tables_in")
        table_in = sem("table_in")
        table_ok = sem("table_ok")
        rev_done = sem("rev_done")
        rev_sb = sem("rev_sb")
        rev_out = sem("rev_out")
        w_landed = [sem(f"w_landed{i}") for i in range(RING)]
        w_split_hi = sem("w_split_hi")
        w_split = sem("w_split")
        w_used = sem("w_used")
        gpre_top = sem("gpre_top")
        gpre_in = sem("gpre_in")
        gpost_in = sem("gpost_in")
        mix_in = sem("mix_in")
        x_sq = sem("x_sq")
        x_r = sem("x_r")
        xn_ok = sem("xn_ok")
        tr_done = sem("tr_done")
        hT_hi_ok = sem("hT_hi_ok")
        hT_ok = sem("hT_ok")
        y_done = sem("y_done")
        y_sq = sem("y_sq")
        y_r = sem("y_r")
        x_up = sem("x_up")
        silu_ok = sem("silu_ok")
        mul_ok = sem("mul_ok")
        act_hi_ok = sem("act_hi_ok")
        act_ok = sem("act_ok")
        act_tr = sem("act_tr")
        d_evac = sem("d_evac")
        pe_tr = sem("pe_tr")
        pe_ev = sem("pe_ev")
        blk_ok = sem("blk_ok")
        hid_done = sem("hid_done")
        gelu_ok = sem("gelu_ok")
        cmp_done = sem("cmp_done")
        cmp_ev = sem("cmp_ev")
        lat_sq = sem("lat_sq")
        lat_r = sem("lat_r")
        lat_n = sem("lat_n")
        lat_tr = sem("lat_tr")
        lat_hi_ok = sem("lat_hi_ok")
        lat_ok = sem("lat_ok")
        ng_tanh = sem("ng_tanh")
        q_cp = sem("q_cp")
        q_ok = sem("q_ok")
        q_tr = sem("q_tr")
        q_ev = sem("q_ev")
        kv_cp = sem("kv_cp")
        k_ok = sem("k_ok")
        k_tr = sem("k_tr")
        k_ev = sem("k_ev")
        sc_done = sem("sc_done")
        sm_bias = sem("sm_bias")
        sm_exp = sem("sm_exp")
        sm_norm = sem("sm_norm")
        pt_done = sem("pt_done")
        pt_ev = sem("pt_ev")
        pv_done = sem("pv_done")
        o_hi_ok = sem("o_hi_ok")
        o_ok = sem("o_ok")
        b_half = sem("b_half")
        b_ev = sem("b_ev")
        mg_sum = sem("mg_sum")
        mg_hi_ok = sem("mg_hi_ok")
        mg_ok = sem("mg_ok")
        out_sem = sem("out_sem")
        passed = sem("passed")

        rev_dram = nc.dram_tensor("rev_copies", (2 * HEADS, P, TW), F32, kind="Internal").ap()

        block = ctx.enter_context(nc.Block())

        def used(l, n, dj=None):
            v = l * NC + (n + 1 + RING)
            return v if dj is None else v + dj * RING

        split = used

        def free(l, n, dj=None):
            v = l * NC + (n + 1)
            return v if dj is None else v + dj * RING

        def landed(l, n, dj=None):
            v = l * ARRIVED_LAYER[n % RING] + ARRIVED[n]
            return v if dj is None else v + dj * 16

        def nth(l, per_layer, k, dj=None):
            v = l * per_layer + (k + 1)
            return v if dj is None else v + dj

        def chunk_g(c0, j):
            return c0 + (3 * j - 1 if j else 0)

        def chunk_u(c0, j):
            return c0 + (3 * j if j else 1)

        def chunk_d(c0, j):
            return c0 + (3 * j + 4 if j < FJ - 1 else FC - 1)

        def wait_apart(eng, semaphore, value):
            eng.wait_ge(semaphore, value)
            eng.sem_inc(passed, 1)

        FFN_LOOP = (2, FJ - 1)

        @block.sync
        def _(sp):
            sp.dma_start(x[:, 0, :], A["x"][0, 0:P, :]).then_inc(x_in[0], 16)
            sp.dma_start(onehot, A["c_onehot"]).then_inc(table_in, 16)
            sp.dma_start(table8[0:NB, :], A["rel_bias_table"]).then_inc(table_in, 16)
            sp.dma_start(ident[:], A["c_ident"]).then_inc(const_in, 16)
            sp.dma_start(x[:, 1, :], A["x"][0, P:S, :]).then_inc(x_in[1], 16)
            sp.dma_start(causal[:], A["c_causal"]).then_inc(tables_in, 16)
            sp.dma_start(cs[:], A["c_rope"]).then_inc(tables_in, 16)

            def chunk(l, n, pieces, dj=None):
                target = sp.snap(free(l, n, dj))
                slot = stage[n % RING]
                for i, (dst, src) in enumerate(pieces(slot)):
                    if i == 0:
                        wait_apart(sp, w_split, target)
                    sp.dma_start(dst, src).then_inc(w_landed[n % RING], 16)

            def columns(w, l, at, width=FW, k0=0, kn=KD, off=0, pitch=None):
                pitch = pitch or width

                def of(slot):
                    dst = slot[:, 0:kn * pitch].rearrange("p (k c) -> p k c", k=kn)[:, :, off:off + width]
                    src = A[w][l, k0 * P:(k0 + kn) * P, bass.ds(at, width)].rearrange("(k p) c -> p k c", p=P)
                    return dst, src
                return of

            def one(*args, **kw):
                return lambda slot: [columns(*args, **kw)(slot)]

            def ffn(l, c0, gu, down, gain=None):
                def gate(j, jr, dj):
                    chunk(l, chunk_g(c0, j), lambda s: [columns(gu, l, jr * FW)(s)], dj)

                def up(j, jr, dj):
                    chunk(l, chunk_u(c0, j), lambda s: [columns(gu, l, jr * FW + FF)(s)], dj)

                def rows(j, jr, dj):
                    def of(slot):
                        dst = slot[:].rearrange("p (k c) -> p k c", k=2)
                        src = A[down][l, bass.ds(jr * FW, FW), :].rearrange("(k p) c -> p k c", p=P)
                        return [(dst, src)]
                    chunk(l, chunk_d(c0, j), of, dj)

                gate(0, 0, None)
                if gain:
                    sp.dma_start(gpre[:], A[gain][l, :].partition_broadcast(P)).then_inc(gpre_top, 16)
                up(0, 0, None)
                gate(1, 1, None)
                up(1, 1, None)
                rows(0, 0, None)
                lo, hi = FFN_LOOP
                with sp.Fori(0, hi - lo) as dj:
                    gate(lo, dj + lo, dj)
                    up(lo, dj + lo, dj)
                    rows(lo - 1, dj + (lo - 1), dj)
                gate(FJ - 1, FJ - 1, None)
                up(FJ - 1, FJ - 1, None)
                rows(FJ - 2, FJ - 2, None)
                rows(FJ - 1, FJ - 1, None)

            with sp.Fori(0, L) as l:
                ffn(l, 0, "ffn1_w_gu", "ffn1_w_down", "ffn1_norm_pre")

                def m(k, *sources):
                    chunk(l, MIX0 + k, lambda s: [f(s) for f in sources])

                def pairs(at, t):
                    return [columns("w_in", l, at + (2 * t + i // 2 + G * (i % 2)) * HD, HD, off=i * HD, pitch=FW)
                            for i in range(4)]

                for i in range(4):
                    m(M_TM + i, columns("w_in", l, C_SV, TM - 24, 2 * i, 2, 0, TM),
                      columns("w_in", l, C_GATE, 24, 2 * i, 2, TM - 24, TM))
                m(M_KC, columns("w_in", l, C_KC))
                m(M_NQ, *pairs(C_NQ, 0))
                m(M_NQ + 1, *pairs(C_NQ, 1))
                for i in range(QR // P):
                    m(M_QB + i, columns("mla_w_qb", l, 0, HEADS * QK, i, 1))
                m(M_KK, columns("w_in", l, C_KS, P, pitch=FW), columns("w_in", l, C_KW, P, off=P, pitch=FW))
                for i in range(KVR // P):
                    m(M_KVB + i, columns("mla_w_kvb", l, 0, HEADS * 2 * HD, i, 1))
                m(M_VV, columns("w_in", l, C_KS + P, P, pitch=FW), columns("w_in", l, C_KW + P, P, off=P, pitch=FW))
                m(M_SQ, *pairs(C_SQ, 0))
                m(M_SQ + 1, *pairs(C_SQ, 1))
                m(M_SK, columns("w_in", l, C_SK, P))
                for k in range(M_SK + 1, M_OUT):
                    if k in GATE_OF:
                        m(k, columns("w_in", l, C_MG + GATE_OF[k] * FW))
                        continue
                    n, half = BRANCHES[BRANCH_OF[k]]

                    def branch(slot, n=n, half=half):
                        src = A["w_branch"][l, n, :, half * 512:half * 512 + 512]
                        return (slot[:].rearrange("p (k c) -> p k c", k=4), src.rearrange("(k p) c -> p k c", p=P))
                    m(k, branch)
                for i in range(4):
                    m(M_OUT + i, columns("w_out", l, 0, D, 2 * i, 2))
                ffn(l, FFN2_0, "ffn2_w_gu", "ffn2_w_down")

            for h in range(NH):
                sp.wait_ge(x_up, L * 3 * NH + h + 1)
                sp.dma_start(out[0, h * P:h * P + P, :], x[:, h, :]).then_inc(out_sem, 16)
            sp.wait_ge(out_sem, 32)

        @block.gpsimd
        def _(pool):
            pool.memset(mhalf[:], -0.5)
            pool.drain()

            def inv_rms(at, n, four=False):
                at_ = slice(at, at + n)
                nc.gpsimd.tensor_scalar(ms[:, at_], ms[:, at_], 4 * EPS if four else EPS, None, ALU.add)
                pool.drain()
                return nc.gpsimd.tensor_tensor(rstd[:, at_], ms[:, at_], mhalf[:, 0:n], ALU.pow)

            def gains(l, sub):
                return [("ffn1_norm_pre", "ffn1_norm_post"), ("mix_norm_pre", "mix_norm_post"),
                        ("ffn2_norm_pre", "ffn2_norm_post")][sub]

            def rms_x(l, sub, h):
                wait_apart(pool, x_sq, nth(l, 6, 2 * sub + h))
                inv_rms(h, 1).then_inc(x_r, 1)

            def rms_y(l, sub, h):
                wait_apart(pool, y_sq, nth(l, 6, 2 * sub + h))
                inv_rms(2 + h, 1, sub != 1).then_inc(y_r, 1)

            def boundary(l, sub):
                for h in range(NH):
                    rms_y(l, sub, h)
                    rms_x(l, sub + 1, h)
                wait_apart(pool, x_up, nth(l, 6, 2 * sub + 1 + NH))
                pool.dma_start(gpost[:], A[gains(l, sub + 1)[1]][l, :].partition_broadcast(P)).then_inc(gpost_in, 16)
                next_gain(l, sub + 1)

            def next_gain(l, sub):
                if sub < 2:
                    wait_apart(pool, xn_ok, nth(l, 12, 4 * sub + 3))
                    pool.dma_start(gpre[:], A[gains(l, sub + 1)[0]][l, :].partition_broadcast(P)).then_inc(gpre_in, 16)

            rms_x(0, 0, 0)
            with pool.Fori(0, L) as l:
                rms_x(l, 0, 1)
                wait_apart(pool, x_up, l * 6 + NH)
                pool.dma_start(gpost[:], A["ffn1_norm_post"][l, :].partition_broadcast(P)).then_inc(gpost_in, 16)
                next_gain(l, 0)

                def spread(j):
                    wait_apart(pool, mul_ok, nth(l, 2 * FJ, j))

                spread(2)
                pool.wait_ge(rev_out, 32)
                toeplitz = bass.AP(rev_dram.tensor, P - 1, [[TW - 1, P], [TW * P, 2 * HEADS], [1, S]])
                pool.dma_start(bias[:], toeplitz).then_inc(mix_in, 16)
                for v, name in enumerate(("nsa_w1_k", "nsa_w1_v")):
                    spread(3 + v)
                    pool.dma_start(w1[:, v], A[name][l].rearrange("(l p) n -> p l n", p=P)).then_inc(mix_in, 16)
                spread(5)
                for v, name in enumerate(("nsa_w2_k", "nsa_w2_v")):
                    pool.dma_start(w2[:, v, :], A[name][l]).then_inc(mix_in, 16)
                for v, name in enumerate(("nsa_pe_k", "nsa_pe_v")):
                    pool.dma_start(pe_rows[:, v, :], A[name][l].rearrange("(l two) d -> l (two d)", two=2)
                                   ).then_inc(mix_in, 16)
                pool.dma_start(sk8[:], A["swa_sinks"][l, :].partition_broadcast(P)).then_inc(mix_in, 16)
                pool.dma_start(gl[:, 0:QR], A["mla_q_norm"][l, :].partition_broadcast(P)).then_inc(mix_in, 16)
                pool.dma_start(gl[:, QR:LAT], A["mla_kv_norm"][l, :].partition_broadcast(P)).then_inc(mix_in, 16)
                boundary(l, 0)
                wait_apart(pool, lat_sq, l + 1)
                inv_rms(4, 4).then_inc(lat_r, 1)
                boundary(l, 1)
                rms_y(l, 2, 0)
                rms_x(l, 3, 0)
                rms_y(l, 2, 1)

        MIX_LOADS = 10 * 16
        MIX_LAST = MIX_LOADS - 1

        @block.scalar
        def _(act_):
            copy = ACT.Copy

            def hi(l, n, dj=None):
                if n >= NC:
                    return
                act_.wait_ge(w_landed[n % RING], landed(l, n, dj))
                act_.wait_ge(w_used, free(l, n, dj))
                nc.scalar.activation(w_hi[n % RING][:, 0:width(n)], stage[n % RING][:, 0:width(n)], copy
                                     ).then_inc(w_split_hi, 1)

            def square_x(l, sub, h):
                act_.wait_ge(x_up, l * 6 + (2 * sub + h + 1))
                nc.scalar.activation(unused[:, h, :], x[:, h, :], ACT.Square, scale=D ** -0.5,
                                     accum_out=ms[:, h:h + 1]).then_inc(x_sq, 1)

            def square_y(l, sub, h, last):
                if h == 0:
                    act_.wait_ge(y_done, nth(l, 3, sub))
                else:
                    act_.wait_ge(w_used, used(l, last))
                scale = D ** -0.5 * (1 if sub == 1 else 2)
                nc.scalar.activation(unused[:, h, :], ybanks(h), ACT.Square, scale=scale,
                                     accum_out=ms[:, 2 + h:3 + h]).then_inc(y_sq, 1)

            def turned_hi(l, sub, h):
                for b in range(2):
                    act_.wait_ge(tr_done, nth(l, 12, 4 * sub + 2 * h + b))
                    nc.scalar.activation(hT_hi[:, 4 * b:4 * b + 4, h * P:h * P + P],
                                         bank(4 + 2 * h + b).rearrange("p (k t) -> p k t", k=4), copy
                                         ).then_inc(hT_hi_ok, 1)

            def boundary(l, sub, c0):
                square_y(l, sub, 0, c0 - 1)
                hi(l, c0 + 1)
                square_x(l, sub + 1, 0)
                square_y(l, sub, 1, c0 - 1)
                hi(l, c0 + 2)
                turned_hi(l, sub + 1, 0)
                square_x(l, sub + 1, 1)
                turned_hi(l, sub + 1, 1)

            def ffn(l, f, c0):
                def step(j, dj=None):
                    n = chunk_g(c0, j)
                    act_.wait_ge(w_used, used(l, n, dj))
                    if j:
                        act_.wait_ge(mul_ok, nth(l, 2 * FJ, f * FJ + j - 1, dj))
                    nc.scalar.activation(silu, bank(4).rearrange("p (a t) -> p a t", a=2), ACT.Silu).then_inc(silu_ok, 1)
                    hi(l, n + RING, dj)
                    if j < FJ - 1:
                        hi(l, chunk_u(c0, j) + RING, dj)
                    if j == 0:
                        act_.wait_ge(act_tr, nth(l, 2, f))
                    else:
                        act_.wait_ge(mul_ok, nth(l, 2 * FJ, f * FJ + j, dj))
                    if 0 < j < FJ - 1:
                        act_.wait_ge(w_used, used(l, chunk_d(c0, j - 1), dj))
                    nc.scalar.activation(act_split(j)[0], act if j else actT, copy).then_inc(act_hi_ok, 1)
                    if j == FJ - 1:
                        hi(l, chunk_u(c0, j) + RING, dj)
                    elif j:
                        hi(l, chunk_d(c0, j - 1) + RING, dj)

                step(0)
                step(1)
                with act_.Fori(0, FFN_LOOP[1] - FFN_LOOP[0]) as dj:
                    step(FFN_LOOP[0], dj)
                step(FJ - 1)

            def project_out(l, m_):
                i = DIDX[m_]
                n = MIX0 + m_
                src = bank(6 + i % 2)
                pair = src.rearrange("p (a t) -> p a t", a=2)
                act_.wait_ge(w_used, used(l, n))
                if m_ == M_KC:
                    for g in range(2):
                        rows = src[HD * g:HD * g + HD, :].rearrange("p (a t) -> p a t", a=2)
                        nc.scalar.activation(kv2[0:HD, :, g, :], rows, copy)
                        ins = nc.scalar.activation(kv2[HD:P, :, g, 0:S - 1], rows[:, :, 1:S], copy)
                elif m_ in (M_NQ, M_NQ + 1):
                    t = 2 * (m_ - M_NQ)
                    ins = nc.scalar.activation(qsT[:, t:t + 2, :], pair, copy)
                elif m_ in (M_SQ, M_SQ + 1):
                    t = 4 + 2 * (m_ - M_SQ)
                    ins = nc.scalar.activation(qsT[:, t:t + 2, :], pair, copy)
                elif m_ == M_KK:
                    ins = nc.scalar.activation(kT[:, 0:2, :], pair, copy)
                elif m_ == M_VV:
                    ins = nc.scalar.activation(vtok[:, 0:2].rearrange("p k h c -> p h k c"),
                                               src.rearrange("p (h k c) -> p h k c", h=NH, k=2), copy)
                elif m_ == M_SK:
                    ins = nc.scalar.activation(kT[:, 2, :], src[:, 0:S], copy)
                else:
                    c = GATE_OF[m_]
                    ins = nc.scalar.activation(gates[:, 2 * c:2 * c + 2, :], pair, ACT.Tanh, scale=0.5)
                ins.then_inc(d_evac, 1)
                if m_ < M_SK:
                    hi(l, n + RING)

            square_x(0, 0, 0)
            act_.wait_ge(rev_done, 1)
            nc.scalar.activation(rev, ps[0:HEADS, 0:2, 0:TW], copy).then_inc(rev_sb, 1)
            act_.wait_ge(rev_sb, 1)
            for a in range(2):
                act_.dma_start(rev_dram[HEADS * a:HEADS * a + HEADS],
                               rev[:, a, :].unsqueeze(1).to_broadcast([HEADS, P, TW])).then_inc(rev_out, 16)


            with act_.Fori(0, L) as l:
                hi(l, 0)
                square_x(l, 0, 1)
                for h in range(NH):
                    turned_hi(l, 0, h)
                    hi(l, 1 + h)
                ffn(l, 0, 0)
                boundary(l, 0, MIX0)

                for i in range(3):
                    hi(l, MIX0 + M_TM + i + RING)
                act_.wait_ge(w_used, used(l, MIX0 + M_TM + 3))
                nc.scalar.activation(vtok[:, 2], ps[:, 0:2 * NH:2, 0:P], copy)
                for part, (col, w) in enumerate(((P, QR), (0, KVR))):
                    for h in range(NH):
                        k = 4 + 2 * part + h
                        ins = nc.scalar.activation(latn[:, h, QR * part:QR * part + w],
                                                   bank(2 * h + part)[:, col:col + w], ACT.Square,
                                                   scale=w ** -0.5, accum_out=ms[:, k:k + 1])
                ins.then_inc(lat_sq, 1)
                hi(l, MIX0 + M_TM + 3 + RING)
                project_out(l, M_KC)
                act_.wait_ge(pe_tr, l + 1)
                nc.scalar.activation(peT[:], bank(4)[:, 0:CMP_LEN].rearrange("p (v l) -> p v l", v=2), copy
                                     ).then_inc(pe_ev, 1)
                project_out(l, M_NQ)
                act_.wait_ge(lat_tr, l + 1)
                for b in range(3):
                    n = 2 if b < 2 else 1
                    ins = nc.scalar.activation(lat_hi[:, 2 * b:2 * b + n, :],
                                               bank(b)[:, 0:n * S].rearrange("p (a t) -> p a t", a=n), copy)
                    ins.then_inc(lat_hi_ok, 1)
                act_.wait_ge(lat_n, l + 1)
                nc.scalar.activation(tm[:, :, ROPE:], tm[:, :, ROPE:], ACT.Tanh, scale=0.5).then_inc(ng_tanh, 1)
                project_out(l, M_NQ + 1)
                for i in range(2):
                    hi(l, MIX0 + M_QB + i + RING)
                act_.wait_ge(w_used, used(l, MIX0 + M_QB + 2))
                for h in range(NH):
                    for p in range(2):
                        ins = nc.scalar.activation(qtok[:, h, 4 * p:4 * p + 4, :],
                                                   bank(2 * h + p)[:, 0:4 * QK].rearrange("p (n c) -> p n c", n=4), copy)
                ins.then_inc(q_cp, 1)
                hi(l, MIX0 + M_QB + 2 + RING)
                act_.wait_ge(hid_done, l + 1)
                nc.scalar.activation(hid[:], bank(4)[:, 0:4 * NCMP].rearrange("p (v c) -> p v c", v=2),
                                     ACT.Gelu_apprx_tanh).then_inc(gelu_ok, 1)
                project_out(l, M_KK)
                hi(l, MIX0 + M_KVB + RING)
                act_.wait_ge(w_used, used(l, MIX0 + M_KVB + 1))
                for h in range(NH):
                    for p in range(2):
                        src = bank(2 * h + p).rearrange("p (n c) -> p n c", n=4)
                        nc.scalar.activation(ktok[:, h, 4 * p:4 * p + 4, 0:HD], src[:, :, 0:HD], copy)
                        ins = nc.scalar.activation(vmla[:, h, 4 * p:4 * p + 4, :], src[:, :, HD:], copy)
                ins.then_inc(kv_cp, 1)
                hi(l, MIX0 + M_KVB + 1 + RING)
                act_.wait_ge(cmp_done, l + 1)
                nc.scalar.activation(kcmp[:, 0:NCMP], bank(4)[:, 0:NCMP], copy)
                nc.scalar.activation(vcmp[0:NCMP], bank(5)[0:NCMP, 0:P].rearrange("p (g d) -> p g d", g=2), copy
                                     ).then_inc(cmp_ev, 1)
                project_out(l, M_VV)
                act_.wait_ge(q_tr, l + 1)
                for b in range(4):
                    ins = nc.scalar.activation(mqT[:, 2 * b:2 * b + 2, :],
                                               bank(b)[0:QK, :].rearrange("p (n t) -> p n t", n=2), copy)
                ins.then_inc(q_ev, 1)
                project_out(l, M_SQ)
                act_.wait_ge(k_tr, l + 1)
                for b in range(4):
                    ins = nc.scalar.activation(mkT[:, 2 * b:2 * b + 2, :],
                                               bank(b)[0:QK, :].rearrange("p (n t) -> p n t", n=2), copy)
                ins.then_inc(k_ev, 1)
                project_out(l, M_SQ + 1)

                for s in range(NSTEP):
                    if s < NU:
                        kind, g, q = UNITS[s]
                        scale = keys_of(s)[3]
                        act_.wait_ge(sm_bias, nth(l, NU, s))
                        for i in range(G):
                            ins = nc.scalar.activation(prob(s)[:, i, :], prob(s)[:, i, :], ACT.Exp,
                                                       bias=nb[:, s, i:i + 1], scale=scale,
                                                       accum_out=den[:, s, i:i + 1])
                        if kind == "swa":
                            k = s - (NU - 4)
                            ins = nc.scalar.activation(esk[:, k, :], dsk[:, k, :], ACT.Exp, scale=SC)
                        ins.then_inc(sm_exp, 1)
                    m_ = STEPS.get(s)
                    if m_ in DIDX:
                        project_out(l, m_)
                    u = s - 2
                    if u in OGROUP:
                        kind, g, q = UNITS[u]
                        t = {"win": 0, "swa": 4, "mla": 8}[kind] + 2 * g
                        act_.wait_ge(pv_done, nth(l, NU, u))
                        nc.scalar.activation(oT_hi[:, t:t + 2, q * P:q * P + P], o_ps(u), copy).then_inc(o_hi_ok, 1)
                    if 0 <= s - 1 < NU:
                        u = s - 1
                        n, tiles, _, _ = keys_of(u)
                        rows = min(n, P)
                        act_.wait_ge(pt_done, nth(l, NU, u))
                        if u >= 2:
                            act_.wait_ge(pv_done, nth(l, NU, u - 2))
                        nc.scalar.activation(pt_sb(u)[0:rows, 0:tiles],
                                             ps[0:rows, 2:2 + tiles, :].rearrange("p k (i t) -> p k i t", i=G), copy
                                             ).then_inc(pt_ev, 1)
                    if m_ is not None:
                        hi(l, MIX0 + m_ + RING)

                for half in range(2):
                    act_.wait_ge(mg_sum, nth(l, 4, 2 * half + 1))
                    nc.scalar.activation(mg_hi[:, 4 * half:4 * half + 4, :], gates[:, 16 + 4 * half:20 + 4 * half, :],
                                         copy, scale=0.5).then_inc(mg_hi_ok, 1)
                    hi(l, MIX0 + BRANCH_AT[4 + half] + RING)
                for i in range(2):
                    hi(l, MIX0 + M_OUT + i + RING)
                boundary(l, 1, FFN2_0)
                ffn(l, 1, FFN2_0)
                square_y(l, 2, 0, NC - 1)
                square_x(l, 3, 0)
                square_y(l, 2, 1, NC - 1)

        @block.vector
        def _(dve):
            def lo(l, n, dj=None):
                if n >= NC:
                    return
                dve.wait_ge(w_split_hi, nth(l, NC, n) if dj is None else nth(l, NC, n, dj * RING))
                w = slice(0, width(n))
                nc.vector.tensor_tensor(w_lo[n % RING][:, w], stage[n % RING][:, w],
                                        w_hi[n % RING][:, w].bitcast(F32), ALU.subtract).then_inc(w_split, 1)

            def gain_in(l, sub):
                if sub == 0:
                    dve.wait_ge(gpre_top, l * 16 + 16)
                else:
                    dve.wait_ge(gpre_in, l * 32 + 16 * sub)

            def gained_x(l, sub, h):
                dve.drain()
                if h == 0:
                    gain_in(l, sub)
                nc.vector.tensor_tensor(work[:, h, :], x[:, h, :], gpre[:], ALU.mult)

            def normalised_x(l, sub, h):
                gain_in(l, sub)
                dve.wait_ge(x_r, nth(l, 6, 2 * sub + h))
                for b in range(2):
                    c = slice(512 * b, 512 * b + 512)
                    nc.vector.scalar_tensor_tensor(work[:, h, c], x[:, h, c], rstd[:, h:h + 1], gpre[:, c],
                                                   ALU.mult, ALU.mult).then_inc(xn_ok, 1)

            def scaled(l, sub, h):
                dve.drain()
                dve.wait_ge(x_r, nth(l, 6, 2 * sub + h))
                for b in range(2):
                    c = slice(512 * b, 512 * b + 512)
                    nc.vector.tensor_scalar(work[:, h, c], work[:, h, c], rstd[:, h:h + 1], None, ALU.mult
                                            ).then_inc(xn_ok, 1)

            def turned_lo(l, sub, h, banks=(0, 1)):
                for b in banks:
                    dve.wait_ge(hT_hi_ok, nth(l, 12, 4 * sub + 2 * h + b))
                    t = (slice(None), slice(4 * b, 4 * b + 4), slice(h * P, h * P + P))
                    nc.vector.tensor_tensor(hT_lo[t], bank(4 + 2 * h + b).rearrange("p (k t) -> p k t", k=4),
                                            hT_hi[t].bitcast(F32), ALU.subtract).then_inc(hT_ok, 1)

            def gained_y(l, sub, h):
                if h == 0:
                    dve.wait_ge(gpost_in, l * 48 + 16 * (sub + 1))
                dve.wait_ge(y_sq, nth(l, 6, 2 * sub + h))
                nc.vector.tensor_tensor(work[:, h, :], ybanks(h), gpost[:], ALU.mult)

            def residual(l, sub, h):
                dve.drain()
                dve.wait_ge(y_r, nth(l, 6, 2 * sub + h))
                nc.vector.scalar_tensor_tensor(x[:, h, :], work[:, h, :], rstd[:, 2 + h:3 + h], x[:, h, :],
                                               ALU.mult, ALU.add).then_inc(x_up, 1)

            def boundary(l, sub, c0):
                gained_y(l, sub, 0)
                residual(l, sub, 0)
                lo(l, c0 + 1)
                normalised_x(l, sub + 1, 0)
                gained_y(l, sub, 1)
                turned_lo(l, sub + 1, 0, (0,))
                residual(l, sub, 1)
                turned_lo(l, sub + 1, 0, (1,))
                gained_x(l, sub + 1, 1)
                if sub == 0:
                    lo(l, c0 + 2)
                scaled(l, sub + 1, 1)
                turned_lo(l, sub + 1, 1)
                if sub:
                    lo(l, c0 + 2)

            def ffn(l, f, c0):
                def step(j, dj=None):
                    lo(l, chunk_g(c0, j) + RING, dj)
                    dve.wait_ge(silu_ok, nth(l, 2 * FJ, f * FJ + j, dj))
                    dve.wait_ge(w_used, used(l, chunk_u(c0, j), dj))
                    if j:
                        dve.wait_ge(act_ok, nth(l, 2 * FJ, f * FJ + j - 1, dj))
                    nc.vector.tensor_tensor(act, bank(5).rearrange("p (a t) -> p a t", a=2), silu, ALU.mult
                                            ).then_inc(mul_ok, 1)
                    if j < FJ - 1:
                        lo(l, chunk_u(c0, j) + RING, dj)
                    dve.wait_ge(act_hi_ok, nth(l, 2 * FJ, f * FJ + j, dj))
                    a_hi, a_lo = act_split(j)
                    nc.vector.tensor_tensor(a_lo, act if j else actT, a_hi.bitcast(F32), ALU.subtract).then_inc(act_ok, 1)
                    if j == FJ - 1:
                        lo(l, chunk_u(c0, j) + RING, dj)
                    elif j:
                        lo(l, chunk_d(c0, j - 1) + RING, dj)

                step(0)
                step(1)
                with dve.Fori(0, FFN_LOOP[1] - FFN_LOOP[0]) as dj:
                    step(FFN_LOOP[0], dj)
                step(FJ - 1)

            def rope(src, dst, heads):
                x1, x2 = src[:, :, :, 0:16], src[:, :, :, 16:32]
                cos, sin = (cs[:, i].unsqueeze(2).to_broadcast([P, NH, heads, 16]) for i in range(2))
                t = [rtmp[:, i, :, 0:heads, :] for i in range(4)]
                nc.vector.tensor_tensor(t[0], x1, cos, ALU.mult)
                nc.vector.tensor_tensor(t[1], x2, sin, ALU.mult)
                nc.vector.tensor_tensor(t[2], x1, sin, ALU.mult)
                nc.vector.tensor_tensor(t[3], x2, cos, ALU.mult)
                dve.drain()
                nc.vector.tensor_tensor(dst[:, :, :, 0:16], t[0], t[1], ALU.subtract)
                return nc.vector.tensor_tensor(dst[:, :, :, 16:32], t[2], t[3], ALU.add)

            def biased(l, u):
                kind, g, q = UNITS[u]
                n, _, _, scale = keys_of(u)
                off = 0 if q else P
                if u >= 2:
                    dve.wait_ge(pt_done, nth(l, NU, u - 2))
                wait_apart(dve, sc_done, nth(l, NU, u))
                for i in range(G):
                    if kind == "mla":
                        b = causal[:, off:off + n]
                    elif kind == "cmp":
                        first = CMP_LEN - 1 + off
                        b = bias[:, G * g + i, first:first + CMP_STRIDE * (n - 1) + 1:CMP_STRIDE]
                    else:
                        b = bias[:, (HEADS if kind == "swa" else 0) + G * g + i, off:off + n]
                    nc.vector.tensor_tensor_reduce(prob(u)[:, i, :], s_ps(u)[:, i, :], b, 1.0, -3.0e38,
                                                   ALU.add, ALU.max, mx[:, u, i:i + 1])
                dve.drain()
                if kind == "cmp":
                    ins = nc.vector.tensor_scalar(nb[:, u, :], mx[:, u, :], BAR, -scale, ALU.max, ALU.mult)
                elif kind == "swa":
                    k = u - (NU - 4)
                    sink = sk8[:, G * g:G * g + G]
                    nc.vector.tensor_tensor(mx[:, u, :], mx[:, u, :], sink, ALU.max)
                    dve.drain()
                    nc.vector.tensor_tensor(dsk[:, k, :], sink, mx[:, u, :], ALU.subtract)
                    ins = nc.vector.tensor_scalar(nb[:, u, :], mx[:, u, :], -scale, None, ALU.mult)
                else:
                    ins = nc.vector.tensor_scalar(nb[:, u, :], mx[:, u, :], -scale, None, ALU.mult)
                ins.then_inc(sm_bias, 1)

            def normalised(l, u):
                kind, g, q = UNITS[u]
                n = keys_of(u)[0]
                dve.wait_ge(sm_exp, nth(l, NU, u))
                if kind == "cmp":
                    nc.vector.tensor_scalar(den[:, u, :], den[:, u, :], 1e-30, None, ALU.max)
                    dve.drain()
                elif kind == "swa":
                    nc.vector.tensor_tensor(den[:, u, :], den[:, u, :], esk[:, u - (NU - 4), :], ALU.add)
                    dve.drain()
                nc.vector.reciprocal(fac[:, u, :], den[:, u, :])
                dve.drain()
                if kind in ("cmp", "sel", "win"):
                    first = ROPE + 3 * G * g + ("cmp", "sel", "win").index(kind)
                    nc.vector.tensor_tensor(fac[:, u, :], fac[:, u, :], tm[:, q, first:first + 3 * (G - 1) + 1:3],
                                            ALU.mult)
                    dve.drain()
                nc.vector.tensor_tensor(prob(u), prob(u), fac[:, u, :].unsqueeze(2).to_broadcast([P, G, n]),
                                        ALU.mult).then_inc(sm_norm, 1)

            def merged(l, b):
                n, half = BRANCHES[b]
                for p in range(2):
                    t = 4 * half + 2 * p
                    src = bank(6 + p).rearrange("p (a t) -> p a t", a=2)
                    gate, total = gates[:, 8 * n + t:8 * n + t + 2, :], gates[:, 16 + t:18 + t, :]
                    if p == 0:
                        dve.wait_ge(d_evac, nth(l, ND, DIDX[max(m_ for m_ in DIDX if m_ < BRANCH_AT[b])]))
                        dve.wait_ge(b_half, nth(l, 6, b))
                    else:
                        dve.wait_ge(w_used, used(l, MIX0 + BRANCH_AT[b]))
                    nc.vector.scalar_tensor_tensor(gate, gate, 1.0, src, ALU.add, ALU.mult).then_inc(b_ev, 1)
                    if b >= 2:
                        dve.drain()
                        ins = nc.vector.tensor_tensor(total, total, gate, ALU.add)
                        if b >= 4:
                            ins.then_inc(mg_sum, 1)

            nc.vector.memset(table8[NB:NB + 1, :], 8 * NEG)
            dve.sem_inc(w_split, RING)
            dve.wait_ge(x_in[0], 16)
            dve.sem_inc(x_up, 1)
            dve.wait_ge(table_in, 32)
            nc.vector.tensor_scalar(table8[0:NB, :], table8[0:NB, :], 8.0, None, ALU.mult).then_inc(table_ok, 1)
            dve.wait_ge(x_in[1], 16)
            dve.sem_inc(x_up, 1)

            with dve.Fori(0, L) as l:
                gained_x(l, 0, 0)
                scaled(l, 0, 0)
                lo(l, 0)
                turned_lo(l, 0, 0)
                gained_x(l, 0, 1)
                scaled(l, 0, 1)
                lo(l, 1)
                turned_lo(l, 0, 1)
                lo(l, 2)
                ffn(l, 0, 0)
                boundary(l, 0, MIX0)

                for i in range(3):
                    lo(l, MIX0 + M_TM + i + RING)
                dve.wait_ge(mix_in, l * MIX_LOADS + MIX_LOADS)
                dve.wait_ge(tables_in, 32)
                dve.wait_ge(lat_r, l + 1)
                for part, (col, w) in enumerate(((P, QR), (0, KVR))):
                    for h in range(NH):
                        c = slice(QR * part, QR * part + w)
                        k = 4 + 2 * part + h
                        nc.vector.scalar_tensor_tensor(latn[:, h, c], bank(2 * h + part)[:, col:col + w],
                                                       rstd[:, k:k + 1], gl[:, c], ALU.mult, ALU.mult)
                nc.vector.tensor_copy(tm[:], ps[:, 1:2 * NH:2, KVR:TM2]).then_inc(lat_n, 1)
                lo(l, MIX0 + M_TM + 3 + RING)
                nc.vector.tensor_scalar(sk8[:], sk8[:], 1.0 / SC, None, ALU.mult)
                dve.wait_ge(pe_ev, l + 1)
                dve.wait_ge(d_evac, nth(l, ND, DIDX[M_KC]))
                half = CMP_STRIDE // 2
                for v in range(2):
                    for part in range(2):
                        at = CMP_STRIDE * part
                        tok = kv2[:, v, :, at:at + CMP_STRIDE * NCMP].rearrange(
                            "p g (c l two) -> p l g c two", l=half, two=2)[:, :, :, :, 0]
                        pos = peT[:, v, half * part:half * part + half].unsqueeze(2).unsqueeze(3).to_broadcast(
                            [P, half, 2, NCMP])
                        ins = nc.vector.tensor_tensor(blk[v][:, half * part:half * part + half], tok, pos, ALU.add)
                ins.then_inc(blk_ok, 1)
                lo(l, MIX0 + M_KC + RING)
                for b in range(3):
                    n = 2 if b < 2 else 1
                    dve.wait_ge(lat_hi_ok, nth(l, 3, b))
                    ins = nc.vector.tensor_tensor(lat_lo[:, 2 * b:2 * b + n, :],
                                                  bank(b)[:, 0:n * S].rearrange("p (a t) -> p a t", a=n),
                                                  lat_hi[:, 2 * b:2 * b + n, :].bitcast(F32), ALU.subtract)
                ins.then_inc(lat_ok, 1)
                lo(l, MIX0 + M_NQ + RING)
                dve.wait_ge(ng_tanh, l + 1)
                nc.vector.tensor_scalar(tm[:, :, ROPE:], tm[:, :, ROPE:], 0.5, 0.5, ALU.mult, ALU.add)
                lo(l, MIX0 + M_NQ + 1 + RING)
                rope(tm[:, :, 0:ROPE].unsqueeze(2), krot[:].unsqueeze(2), 1)
                dve.drain()
                for i in range(2):
                    lo(l, MIX0 + M_QB + i + RING)
                dve.wait_ge(q_cp, l + 1)
                rope(qtok[:, :, :, HD:], qtok[:, :, :, HD:], HEADS).then_inc(q_ok, 1)
                lo(l, MIX0 + M_QB + 2 + RING)
                dve.wait_ge(hid_done, l + 1)
                for h in range(NH):
                    ins = nc.vector.tensor_copy(ktok[:, h, :, HD:], krot[:, h:h + 1, :].to_broadcast([P, HEADS, ROPE]))
                ins.then_inc(k_ok, 1)
                for m_ in (M_KK, M_KVB, M_KVB + 1, M_VV, M_SQ):
                    lo(l, MIX0 + m_ + RING)

                for s in range(NSTEP):
                    if s < NU:
                        biased(l, s)
                    u = s - 3
                    if u in OGROUP:
                        kind, g, q = UNITS[u]
                        t = {"win": 0, "swa": 4, "mla": 8}[kind] + 2 * g
                        dst = (slice(None), slice(t, t + 2), slice(q * P, q * P + P))
                        dve.wait_ge(o_hi_ok, nth(l, NOG, OGROUP.index(u)))
                        nc.vector.tensor_tensor(oT_lo[dst], o_ps(u), oT_hi[dst].bitcast(F32), ALU.subtract
                                                ).then_inc(o_ok, 1)
                    if s == 0:
                        lo(l, MIX0 + M_SQ + 1 + RING)
                    elif s - 1 in STEPS:
                        lo(l, MIX0 + STEPS[s - 1] + RING)
                    if s < NU:
                        normalised(l, s)
                    if STEPS.get(s) in BRANCH_OF:
                        merged(l, BRANCH_OF[STEPS[s]])
                lo(l, MIX0 + STEPS[NSTEP - 1] + RING)
                for half in range(2):
                    merged(l, 4 + half)
                    if half:
                        lo(l, MIX0 + BRANCH_AT[5] + RING)
                    dve.wait_ge(mg_hi_ok, nth(l, 2, half))
                    t = slice(4 * half, 4 * half + 4)
                    nc.vector.scalar_tensor_tensor(mg_lo[:, t, :], gates[:, 16 + 4 * half:20 + 4 * half, :], 0.5,
                                                   mg_hi[:, t, :].bitcast(F32), ALU.mult, ALU.subtract
                                                   ).then_inc(mg_ok, 1)
                    if not half:
                        lo(l, MIX0 + BRANCH_AT[4] + RING)
                for i in range(2):
                    lo(l, MIX0 + M_OUT + i + RING)
                boundary(l, 1, FFN2_0)
                ffn(l, 1, FFN2_0)
                for h in range(NH):
                    gained_y(l, 2, h)
                    residual(l, 2, h)

        @block.tensor
        def _(pe):
            def mm3(dst, a, b, start, stop):
                (a_hi, a_lo), (b_hi, b_lo) = a, b
                nc.tensor.matmul(dst, a_hi, b_hi, start=start, stop=False)
                nc.tensor.matmul(dst, a_hi, b_lo, start=False, stop=False)
                return nc.tensor.matmul(dst, a_lo, b_hi, start=False, stop=stop)

            def both(hi_, lo_, *at):
                return hi_[at], lo_[at]

            def ring(n, lo_, hi_):
                at = (slice(None), slice(lo_, hi_))
                return both(w_hi[n % RING], w_lo[n % RING], *at)

            def tokens(h):
                return slice(h * P, h * P + P)

            ALL = slice(None)

            def turn(dst, src):
                rows = src.shape[0]
                return nc.tensor.transpose(dst, src, ident[0:rows, 0:rows])

            def turned(l, sub, h):
                for b in range(2):
                    pe.wait_ge(xn_ok, nth(l, 12, 4 * sub + 2 * h + b))
                    for k in range(4 * b, 4 * b + 4):
                        ins = turn(bank(4 + 2 * h + b)[:, (k % 4) * P:(k % 4) * P + P], work[:, h, k * P:k * P + P])
                    ins.then_inc(tr_done, 1)

            def two_tiles(n, dst):
                for c in range(2):
                    for k in range(KD):
                        a = ring(n, k * FW + c * P, k * FW + c * P + P)
                        ins = mm3(dst[:, c * S:c * S + S], a, both(hT_hi, hT_lo, ALL, k, ALL), k == 0, k == KD - 1)
                return ins

            def rows_half(n, lhs, h, first, last):
                for kt in range(2):
                    for c in range(2):
                        ins = mm3(bank(2 * h + c), lhs(kt, h), ring(n, kt * D + c * 512, kt * D + c * 512 + 512),
                                  first and kt == 0, last and kt == 1)
                return ins

            def rows_out(n, lhs, first):
                for h in range(NH):
                    ins = rows_half(n, lhs, h, first, False)
                ins.then_inc(w_used, 1)

            def rows_last(ready, chunks):
                for h in range(NH):
                    for i, (n, lhs) in enumerate(chunks):
                        if h == 0:
                            ready(i)
                        ins = rows_half(n, lhs, h, False, i == 1)
                        if h == 1:
                            ins.then_inc(w_used, 1)
                        elif i == 1:
                            ins.then_inc(y_done, 1)

            def ffn(l, f, c0):
                def lhs(j):
                    return lambda kt, h: both(*act_split(j), ALL, kt, tokens(h))

                def down_ready(j, dj=None):
                    pe.wait_ge(w_split, split(l, chunk_d(c0, j), dj))
                    pe.wait_ge(act_ok, nth(l, 2 * FJ, f * FJ + j, dj))

                def first():
                    turned(l, 2 * f, 0)
                    for h in range(NH):
                        for b, n in ((4, c0), (5, c0 + 1)):
                            if h == 0:
                                pe.wait_ge(w_split, split(l, n))
                            for k in range(KD):
                                if b == 4 and k % 4 == 0:
                                    pe.wait_ge(hT_ok, nth(l, 12, 8 * f + 2 * h + k // 4))
                                ins = mm3(bank(b)[:, h * FW:h * FW + FW], both(hT_hi, hT_lo, ALL, k, tokens(h)),
                                          ring(n, k * FW, k * FW + FW), k == 0, k == KD - 1)
                            if h == 1:
                                ins.then_inc(w_used, 1)
                            elif b == 4:
                                turned(l, 2 * f, 1)

                def step(j, dj=None):
                    n = chunk_g(c0, j)
                    pe.wait_ge(w_split, split(l, n, dj))
                    pe.wait_ge(silu_ok, nth(l, 2 * FJ, f * FJ + j - 1, dj))
                    two_tiles(n, bank(4)).then_inc(w_used, 1)
                    if j == 1:
                        pe.wait_ge(mul_ok, nth(l, 2 * FJ, f * FJ))
                        for a in range(2):
                            for h in range(NH):
                                ins = turn(bank(6)[:, a * S + h * P:a * S + h * P + P], act[:, h, a * P:a * P + P])
                        ins.then_inc(act_tr, 1)
                    n = chunk_u(c0, j)
                    pe.wait_ge(w_split, split(l, n, dj))
                    pe.wait_ge(mul_ok, nth(l, 2 * FJ, f * FJ + j - 1, dj))
                    two_tiles(n, bank(5)).then_inc(w_used, 1)
                    if j < FJ - 1:
                        down_ready(j - 1, dj)
                        rows_out(chunk_d(c0, j - 1), lhs(j - 1), j == 1)

                first()
                step(1)
                with pe.Fori(0, FFN_LOOP[1] - FFN_LOOP[0]) as dj:
                    step(FFN_LOOP[0], dj)
                step(FJ - 1)
                rows_last(lambda i: down_ready(FJ - 2 + i), [(chunk_d(c0, j), lhs(j)) for j in (FJ - 2, FJ - 1)])

            def bank_read(l, m_, b):
                before = [k for k in sorted([*DIDX, *BRANCH_OF]) if k < m_ and (k in BRANCH_OF or 6 + DIDX[k] % 2 == b)]
                if before and before[-1] in BRANCH_OF:
                    pe.wait_ge(b_ev, nth(l, 12, 2 * BRANCH_OF[before[-1]] + b - 6))
                elif before:
                    pe.wait_ge(d_evac, nth(l, ND, DIDX[before[-1]]))

            def project(l, m_):
                n, i = MIX0 + m_, DIDX[m_]
                dst = bank(6 + i % 2)
                pe.wait_ge(w_split, split(l, n))
                bank_read(l, m_, 6 + i % 2)
                if m_ == M_SK:
                    for k in range(KD):
                        ins = mm3(dst[:, 0:S], ring(n, k * P, k * P + P), both(hT_hi, hT_lo, ALL, k, ALL),
                                  k == 0, k == KD - 1)
                elif m_ == M_VV:
                    for h in range(NH):
                        for k in range(KD):
                            ins = mm3(dst[:, h * FW:h * FW + FW], both(hT_hi, hT_lo, ALL, k, tokens(h)),
                                      ring(n, k * FW, k * FW + FW), k == 0, k == KD - 1)
                else:
                    ins = two_tiles(n, dst)
                ins.then_inc(w_used, 1)

            def scores(l, u):
                kind, g, q = UNITS[u]
                n, _, _, _ = keys_of(u)
                if u == 0:
                    pe.wait_ge(k_ev, l + 1)
                else:
                    pe.wait_ge(sm_bias, nth(l, NU, u - 1))
                if kind == "cmp":
                    pe.wait_ge(cmp_ev, l + 1)
                if kind in ("sel", "win"):
                    pe.wait_ge(d_evac, nth(l, ND, DIDX[M_VV]))
                if kind == "swa":
                    pe.wait_ge(d_evac, nth(l, ND, DIDX[M_SK]))
                rows = slice(HD * g, HD * g + HD)
                for i in range(G):
                    if kind == "mla":
                        a, b = mqT[:, G * g + i, tokens(q)], mkT[:, G * g + i, 0:n]
                    else:
                        a = qsT[rows, (4 if kind == "swa" else 0) + i, tokens(q)]
                        b = (kcmp[rows, 0:n] if kind == "cmp"
                             else kT[rows, ("sel", "win", "swa").index(kind), 0:n])
                    ins = nc.tensor.matmul(s_ps(u)[:, i, :], a, b, start=True, stop=True)
                ins.then_inc(sc_done, 1)

            def turn_p(l, u):
                n, tiles, _, _ = keys_of(u)
                rows = min(n, P)
                pe.wait_ge(sm_norm, nth(l, NU, u))
                if u >= 1:
                    pe.wait_ge(pt_ev, nth(l, NU, u - 1))
                for kt in range(tiles):
                    for i in range(G):
                        ins = turn(bank(2 + kt)[0:rows, i * P:i * P + P], prob(u)[:, i, kt * P:kt * P + rows])
                ins.then_inc(pt_done, 1)

            def values(l, u):
                kind, g, q = UNITS[u]
                n, tiles, _, _ = keys_of(u)
                rows = min(n, P)
                og = group_of(u)
                first = kind in ("cmp", "mla", "swa")
                last = kind in ("win", "mla", "swa")
                pe.wait_ge(pt_ev, nth(l, NU, u))
                if first and og >= 2:
                    pe.wait_ge(o_ok, nth(l, NOG, og - 2))
                for odd in range(2):
                    part = slice(HD * odd, HD * odd + HD)
                    if kind == "mla":
                        for pair in range(2):
                            i = 2 * pair + odd
                            for kt in range(tiles):
                                ins = nc.tensor.matmul(o_ps(u)[part, pair, :], vmla[:, kt, G * g + i, :],
                                                       pt_sb(u)[:, kt, i, :], start=kt == 0, stop=kt == tiles - 1)
                        continue
                    for kt in range(tiles):
                        v = (vcmp[0:rows, g, :] if kind == "cmp" else
                             vtok[:, ("sel", "win", "swa").index(kind), kt, HD * g:HD * g + HD])
                        ins = nc.tensor.matmul(o_ps(u)[part], v, pt_sb(u)[0:rows, kt, odd:G:2, :],
                                               start=first and kt == 0, stop=last and kt == tiles - 1)
                ins.then_inc(pv_done, 1)

            def branch(l, b):
                n, (br, half) = MIX0 + BRANCH_AT[b], BRANCHES[b]
                base = 4 * br
                pe.wait_ge(w_split, split(l, n))
                if b in (0, 2, 4):
                    done = max(i for i, u in enumerate(OGROUP) if UNITS[u][0] == ("win", "swa", "mla")[br])
                    pe.wait_ge(o_ok, nth(l, NOG, done))
                for p in range(2):
                    bank_read(l, BRANCH_AT[b], 6 + p)
                    for c in range(2):
                        for k in range(4):
                            at = k * 512 + (2 * p + c) * P
                            ins = mm3(bank(6 + p)[:, c * S:c * S + S], ring(n, at, at + P),
                                      both(oT_hi, oT_lo, ALL, base + k, ALL), k == 0, k == 3)
                    ins.then_inc(b_half if p == 0 else w_used, 1)

            pe.sem_inc(w_used, RING)
            pe.wait_ge(table_ok, 1)
            for a in range(2):
                ins = nc.tensor.matmul(bank(a)[0:HEADS, 0:TW], table8[:, HEADS * a:HEADS * a + HEADS], onehot[:, a, :],
                                       start=True, stop=True)
            ins.then_inc(rev_done, 1)
            pe.wait_ge(const_in, 16)
            pe.wait_ge(rev_sb, 1)

            with pe.Fori(0, L) as l:
                ffn(l, 0, 0)

                def token_major(i, h):
                    n = MIX0 + M_TM + i
                    for kt in range(2):
                        k = 2 * i + kt
                        a = both(hT_hi, hT_lo, ALL, k, tokens(h))
                        for dst, lo_, hi_ in ((bank(2 * h), 0, TM1), (bank(2 * h + 1), TM1, TM)):
                            ins = mm3(dst[:, 0:hi_ - lo_], a, ring(n, kt * TM + lo_, kt * TM + hi_),
                                      k == 0, k == KD - 1)
                    return ins

                turned(l, 1, 0)
                for i in range(3):
                    if i != 1:
                        pe.wait_ge(hT_ok, nth(l, 12, 4 + i // 2))
                    pe.wait_ge(w_split, split(l, MIX0 + M_TM + i))
                    token_major(i, 0)
                    if i == 1:
                        turned(l, 1, 1)
                for i in range(3):
                    if i != 1:
                        pe.wait_ge(hT_ok, nth(l, 12, 4 + 2 + i // 2))
                    token_major(i, 1).then_inc(w_used, 1)
                pe.wait_ge(w_split, split(l, MIX0 + M_TM + 3))
                token_major(3, 0)
                token_major(3, 1).then_inc(w_used, 1)
                project(l, M_KC)
                wait_apart(pe, mix_in, l * MIX_LOADS + MIX_LOADS)
                for v in range(2):
                    ins = turn(bank(4)[:, v * CMP_LEN // 2:(v + 1) * CMP_LEN // 2], pe_rows[:, v, :])
                ins.then_inc(pe_tr, 1)
                project(l, M_NQ)
                pe.wait_ge(lat_n, l + 1)
                for t in range(LAT // P):
                    for h in range(NH):
                        ins = turn(bank(t // 2)[:, (t % 2) * S + h * P:(t % 2) * S + h * P + P],
                                   latn[:, h, t * P:t * P + P])
                ins.then_inc(lat_tr, 1)
                project(l, M_NQ + 1)
                pe.wait_ge(lat_ok, l + 1)
                for i in range(QR // P):
                    n = MIX0 + M_QB + i
                    pe.wait_ge(w_split, split(l, n))
                    for h in range(NH):
                        for p in range(2):
                            ins = mm3(bank(2 * h + p)[:, 0:4 * QK], both(lat_hi, lat_lo, ALL, i, tokens(h)),
                                      ring(n, p * 4 * QK, (p + 1) * 4 * QK), i == 0, i == QR // P - 1)
                    ins.then_inc(w_used, 1)
                pe.wait_ge(blk_ok, l + 1)
                for v in range(2):
                    for i in range(CMP_LEN // 2):
                        ins = nc.tensor.matmul(bank(4)[:, 2 * NCMP * v:2 * NCMP * (v + 1)], w1[:, v, i, :],
                                               blk[v][:, i].rearrange("p g c -> p (g c)"),
                                               start=i == 0, stop=i == CMP_LEN // 2 - 1)
                ins.then_inc(hid_done, 1)
                project(l, M_KK)
                pe.wait_ge(q_cp, l + 1)
                for i in range(KVR // P):
                    n = MIX0 + M_KVB + i
                    pe.wait_ge(w_split, split(l, n))
                    for h in range(NH):
                        for p in range(2):
                            ins = mm3(bank(2 * h + p), both(lat_hi, lat_lo, ALL, QR // P + i, tokens(h)),
                                      ring(n, p * 512, (p + 1) * 512), i == 0, i == KVR // P - 1)
                    ins.then_inc(w_used, 1)
                pe.wait_ge(gelu_ok, l + 1)
                for g in range(2):
                    nc.tensor.matmul(bank(4)[HD * g:HD * g + HD, 0:NCMP], w2[:, 0, :],
                                     hid[:, 0, NCMP * g:NCMP * g + NCMP], start=True, stop=True)
                for g in range(2):
                    ins = nc.tensor.matmul(bank(5)[0:NCMP, HD * g:HD * g + HD], hid[:, 1, NCMP * g:NCMP * g + NCMP],
                                           w2[:, 1, :], start=True, stop=True)
                ins.then_inc(cmp_done, 1)
                project(l, M_VV)
                pe.wait_ge(q_ok, l + 1)
                pe.wait_ge(kv_cp, l + 1)
                for n in range(HEADS):
                    for h in range(NH):
                        ins = turn(bank(n // 2)[0:QK, (n % 2) * S + h * P:(n % 2) * S + h * P + P], qtok[:, h, n, :])
                ins.then_inc(q_tr, 1)
                project(l, M_SQ)
                pe.wait_ge(k_ok, l + 1)
                pe.wait_ge(q_ev, l + 1)
                for n in range(HEADS):
                    for h in range(NH):
                        ins = turn(bank(n // 2)[0:QK, (n % 2) * S + h * P:(n % 2) * S + h * P + P], ktok[:, h, n, :])
                ins.then_inc(k_tr, 1)
                project(l, M_SQ + 1)
                pe.wait_ge(cmp_ev, l + 1)

                for s in range(NSTEP):
                    if s < NU:
                        scores(l, s)
                    if s in STEPS:
                        if STEPS[s] in DIDX:
                            project(l, STEPS[s])
                        else:
                            branch(l, BRANCH_OF[STEPS[s]])
                    if 0 <= s - 2 < NU:
                        values(l, s - 2)
                    if 0 <= s - 1 < NU:
                        turn_p(l, s - 1)
                branch(l, 4)
                branch(l, 5)

                def out_ready(i):
                    pe.wait_ge(w_split, split(l, MIX0 + M_OUT + i))
                    pe.wait_ge(mg_ok, nth(l, 2, i // 2))

                def merged(i):
                    return lambda kt, h: both(mg_hi, mg_lo, ALL, 2 * i + kt, tokens(h))

                for i in range(2):
                    out_ready(i)
                    rows_out(MIX0 + M_OUT + i, merged(i), i == 0)
                rows_last(lambda i: out_ready(2 + i), [(MIX0 + M_OUT + i, merged(i)) for i in (2, 3)])
                ffn(l, 1, FFN2_0)


_INS = ["x", "rel_bias_table", "ffn1_norm_pre", "ffn1_w_gu", "ffn1_w_down", "ffn1_norm_post",
        "mix_norm_pre", "w_in", "nsa_pe_k", "nsa_w1_k", "nsa_w2_k", "nsa_pe_v", "nsa_w1_v", "nsa_w2_v",
        "swa_sinks", "mla_q_norm", "mla_w_qb", "mla_kv_norm", "mla_w_kvb", "w_branch", "w_out",
        "mix_norm_post", "ffn2_norm_pre", "ffn2_w_gu", "ffn2_w_down", "ffn2_norm_post"]


def shape_constants():
    dist = np.arange(S, dtype=np.int32)
    ratio = np.log(np.maximum(dist, 1).astype(np.float32) / np.float32(16)) / np.float32(np.log(64.0))
    far = np.minimum(16 + (ratio * np.float32(16)).astype(np.int32), NB - 1)
    bucket = np.where(dist < 16, dist, far)
    onehot = np.zeros((NB + 1, 2, TW), np.float32)
    for u in range(TW):
        d = S - 1 - u
        for kind, window in enumerate((S, P)):
            onehot[bucket[d] if 0 <= d < window else NB, kind, u] = 1.0
    p, j = np.arange(P)[:, None], np.arange(S)[None, :]
    causal = np.where(P + p - j >= 0, 0.0, NEG).astype(np.float32)
    inv = (10000.0 ** (-np.arange(16, dtype=np.float32) / 16)).astype(np.float32)
    ang = np.arange(S, dtype=np.float32)[:, None] * inv[None, :]
    rope = np.stack([np.cos(ang), np.sin(ang)]).astype(np.float32).reshape(2, NH, P, 16).transpose(2, 0, 1, 3)
    return {"c_onehot": onehot, "c_causal": causal, "c_rope": rope, "c_ident": np.eye(P, dtype=np.float32)}


def kernel(**inputs):
    import concourse.bacc as _bacc
    from concourse import mybir as _mybir
    from concourse.bass_utils import run_bass_kernel_spmd as _run

    nc = _bacc.Bacc("TRN2", target_bir_lowering=False, num_devices=1)
    arrays, aps = {}, {}
    for name, a in list((n, inputs[n]) for n in _INS) + list(shape_constants().items()):
        a = np.ascontiguousarray(a)
        arrays[f"in_{name}_dram"] = a
        aps[name] = nc.dram_tensor(f"in_{name}_dram", a.shape, _mybir.dt.from_np(a.dtype), kind="ExternalInput").ap()
    out = nc.dram_tensor("out_0_dram", (1, S, D), _mybir.dt.float32, kind="ExternalOutput").ap()
    decoder_kernel(nc, aps, out)
    r = _run(nc, [arrays], core_ids=[0])
    return r.results[0]["out_0_dram"]
```
